# Optimizing a Trainium2 kernel written in Bass

```python
import math
import jax
import jax.numpy as jnp
from jax import lax

D_MODEL = 1024
BATCH = 1
SEQ = 512
DEPTH = 1
DEC_BATCH = 8
DEC_SEQ = 1
PAST_LEN = 512
PAGE_SIZE = 128

SSD_HEADS = 16
SSD_HEAD_DIM = 64
SSD_WIDTH = SSD_HEADS * SSD_HEAD_DIM
SSD_GROUPS = 2
SSD_STATE = 128
SSD_CONV = 4
SSD_CONV_DIM = SSD_WIDTH + 2 * SSD_GROUPS * SSD_STATE
SSD_CHUNK = 128
SC_WIDTH = 512
SC_CONV = 3
SB_HEADS = 8
SB_HEAD_DIM = 64
SB_WIDTH = SB_HEADS * SB_HEAD_DIM
SB_BLOCK = 128
SB_BIAS_INIT = -6.0
N_BRANCHES = 3
D_FF = 2816
EPS = 1e-6
IN_SPLITS = (N_BRANCHES * D_MODEL, SSD_WIDTH, SSD_CONV_DIM, SSD_HEADS,
             SC_WIDTH, SC_WIDTH, SC_WIDTH, SB_WIDTH, SB_WIDTH, SB_WIDTH)
IN_COLS = sum(IN_SPLITS)

kernel_name = "hybrid_ssd_shortconv_stickbreaking_macaron_step"

def rmsnorm(x, g):
    xf = x.astype(jnp.float32)
    y = xf * lax.rsqrt(jnp.mean(xf * xf, axis=-1, keepdims=True) + EPS)
    return (y * g.astype(jnp.float32)).astype(x.dtype)

def swiglu(x, w_gate, w_up, w_down):
    return (jax.nn.silu(x @ w_gate) * (x @ w_up)) @ w_down

def split_cols(u, sizes):
    parts, start = [], 0
    for size in sizes:
        parts.append(u[..., start:start + size])
        start += size
    return parts

def causal_dwconv(u, w, prev):
    k_width, t = w.shape[0], u.shape[1]
    full = jnp.concatenate([prev.astype(u.dtype), u], axis=1)
    out = sum(full[:, k:k + t] * w[k] for k in range(k_width))
    return out, full[:, full.shape[1] - (k_width - 1):]

def ssd_chunked(xh, dt, a, bm, cm):
    b, t = xh.shape[0], xh.shape[1]
    nc, e = t // SSD_CHUNK, SSD_HEADS // SSD_GROUPS
    xd = (xh * dt[..., None]).reshape(b, nc, SSD_CHUNK, SSD_GROUPS, e, SSD_HEAD_DIM)
    la = (dt * a).reshape(b, nc, SSD_CHUNK, SSD_GROUPS, e)
    bc = bm.reshape(b, nc, SSD_CHUNK, SSD_GROUPS, SSD_STATE)
    cc = cm.reshape(b, nc, SSD_CHUNK, SSD_GROUPS, SSD_STATE)
    cs = jnp.cumsum(la, axis=2)
    causal = jnp.tril(jnp.ones((SSD_CHUNK, SSD_CHUNK), dtype=bool))
    seg = cs[:, :, :, None] - cs[:, :, None, :]
    decay = jnp.exp(jnp.where(causal[:, :, None, None], seg, -jnp.inf))
    cb = jnp.einsum("bclgn,bcsgn->bclsg", cc, bc)
    y_diag = jnp.einsum("bclsg,bclsge,bcsgep->bclgep", cb, decay, xd)
    to_end = jnp.exp(cs[:, :, -1:] - cs)
    chunk_states = jnp.einsum("bclgn,bclge,bclgep->bcgepn", bc, to_end, xd)
    chunk_decay = jnp.exp(cs[:, :, -1])

    def step(h, inp):
        st, dcy = inp
        return h * dcy[..., None, None] + st, h

    h0 = jnp.zeros((b, SSD_GROUPS, e, SSD_HEAD_DIM, SSD_STATE), jnp.float32)
    h_final, h_in = lax.scan(step, h0, (jnp.moveaxis(chunk_states, 1, 0), jnp.moveaxis(chunk_decay, 1, 0)))
    h_in = jnp.moveaxis(h_in, 0, 1)
    y_off = jnp.einsum("bclgn,bcgepn,bclge->bclgep", cc, h_in, jnp.exp(cs))
    y = (y_diag + y_off).reshape(b, t, SSD_HEADS, SSD_HEAD_DIM)
    return y, h_final.reshape(b, SSD_HEADS, SSD_HEAD_DIM, SSD_STATE)

def ssd_recurrent(xh, dt, a, bm, cm, h0):
    b, e = xh.shape[0], SSD_HEADS // SSD_GROUPS

    def step(h, inp):
        x_t, dt_t, b_t, c_t = inp
        da = jnp.exp(dt_t * a).reshape(b, SSD_GROUPS, e)
        xd = (x_t * dt_t[..., None]).reshape(b, SSD_GROUPS, e, SSD_HEAD_DIM)
        h = h * da[..., None, None] + jnp.einsum("bgep,bgn->bgepn", xd, b_t)
        y = jnp.einsum("bgepn,bgn->bgep", h, c_t).reshape(b, SSD_HEADS, SSD_HEAD_DIM)
        return h, y

    xs = tuple(jnp.moveaxis(arr, 1, 0) for arr in (xh, dt, bm, cm))
    h_init = h0.astype(jnp.float32).reshape(b, SSD_GROUPS, e, SSD_HEAD_DIM, SSD_STATE)
    h_final, ys = lax.scan(step, h_init, xs)
    return jnp.moveaxis(ys, 0, 1), h_final.reshape(b, SSD_HEADS, SSD_HEAD_DIM, SSD_STATE)

def ssd_branch(z, xbc, dt_raw, lp, conv_prev, h0):
    bsz, t = xbc.shape[0], xbc.shape[1]
    conv_out, conv_state = causal_dwconv(xbc, lp["ssd_conv_w"], conv_prev)
    act = jax.nn.silu((conv_out + lp["ssd_conv_b"]).astype(jnp.float32))
    xs, bm, cm = split_cols(act, (SSD_WIDTH, SSD_GROUPS * SSD_STATE, SSD_GROUPS * SSD_STATE))
    xh = xs.reshape(bsz, t, SSD_HEADS, SSD_HEAD_DIM)
    bm = bm.reshape(bsz, t, SSD_GROUPS, SSD_STATE)
    cm = cm.reshape(bsz, t, SSD_GROUPS, SSD_STATE)
    dt = jax.nn.softplus(dt_raw.astype(jnp.float32) + lp["ssd_dt_bias"].astype(jnp.float32))
    a = -jnp.exp(lp["ssd_a_log"].astype(jnp.float32))
    if h0 is None:
        y, h_new = ssd_chunked(xh, dt, a, bm, cm)
    else:
        y, h_new = ssd_recurrent(xh, dt, a, bm, cm, h0)
    y = y + xh * lp["ssd_d"].astype(jnp.float32)[:, None]
    y = y.reshape(bsz, t, SSD_WIDTH) * jax.nn.silu(z.astype(jnp.float32))
    y = rmsnorm(y.reshape(bsz, t, SSD_GROUPS, SSD_WIDTH // SSD_GROUPS),
                lp["ssd_norm"].reshape(SSD_GROUPS, SSD_WIDTH // SSD_GROUPS)).reshape(bsz, t, SSD_WIDTH)
    return y.astype(z.dtype), h_new.astype(z.dtype), conv_state

def shortconv_branch(gate_b, gate_c, x_in, w, prev):
    conv_out, conv_state = causal_dwconv(gate_c * x_in, w, prev)
    return gate_b * conv_out, conv_state

def stick_breaking_block(q, k, v, bias, q_start):
    tq, tk = q.shape[1], k.shape[1]
    z = jnp.einsum("bihd,bjhd->bhij", q.astype(jnp.float32), k.astype(jnp.float32)) * (SB_HEAD_DIM ** -0.5)
    z = z + bias.astype(jnp.float32)[None, :, None, None]
    mask = jnp.arange(tk)[None, :] < (q_start + jnp.arange(tq))[:, None]
    log_beta = jax.nn.log_sigmoid(z)
    log_keep = jnp.where(mask, jax.nn.log_sigmoid(-z), 0.0)
    log_tail = lax.cumsum(log_keep, axis=3, reverse=True) - log_keep
    weights = jnp.exp(jnp.where(mask, log_beta + log_tail, -jnp.inf))
    out = jnp.einsum("bhij,bjhd->bihd", weights, v.astype(jnp.float32))
    return out.astype(v.dtype)

def sb_branch(q, k, v, lp, past_k, past_v):
    bsz, t = q.shape[0], q.shape[1]
    q = rmsnorm(q.reshape(bsz, t, SB_HEADS, SB_HEAD_DIM), lp["sb_q_norm"])
    k = rmsnorm(k.reshape(bsz, t, SB_HEADS, SB_HEAD_DIM), lp["sb_k_norm"])
    v = v.reshape(bsz, t, SB_HEADS, SB_HEAD_DIM)
    if past_k is None:
        k_all, v_all, offset = k, v, 0
    else:
        k_all = jnp.concatenate([past_k.astype(k.dtype), k], axis=1)
        v_all = jnp.concatenate([past_v.astype(v.dtype), v], axis=1)
        offset = past_k.shape[1]
    outs = []
    for start in range(0, t, SB_BLOCK):
        stop = min(start + SB_BLOCK, t)
        kv_len = offset + stop
        outs.append(stick_breaking_block(q[:, start:stop], k_all[:, :kv_len], v_all[:, :kv_len],
                                         lp["sb_logit_bias"], offset + start))
    out = jnp.concatenate(outs, axis=1).reshape(bsz, t, SB_WIDTH)
    return out, k, v

def mix_layer(h, lp, past):
    u = h @ lp["w_in"]
    gate_pre, z, xbc, dt_raw, sc_b, sc_c, sc_x, q, k, v = split_cols(u, IN_SPLITS)
    gates = jax.nn.sigmoid((gate_pre + lp["gate_bias"]).astype(jnp.float32)).astype(h.dtype)
    g_a, g_b, g_c = split_cols(gates, (D_MODEL, D_MODEL, D_MODEL))
    bsz = h.shape[0]
    if past is None:
        past_k = past_v = h0 = None
        ssd_prev = jnp.zeros((bsz, SSD_CONV - 1, SSD_CONV_DIM), h.dtype)
        sc_prev = jnp.zeros((bsz, SC_CONV - 1, SC_WIDTH), h.dtype)
    else:
        past_k, past_v, h0, ssd_prev, sc_prev = past
    y_a, ssd_h, ssd_conv = ssd_branch(z, xbc, dt_raw, lp, ssd_prev, h0)
    y_b, sc_conv = shortconv_branch(sc_b, sc_c, sc_x, lp["sc_conv_w"], sc_prev)
    y_c, k_new, v_new = sb_branch(q, k, v, lp, past_k, past_v)
    merged = (g_a * (y_a @ lp["w_proj_a"]) + g_b * (y_b @ lp["w_proj_b"])
              + g_c * (y_c @ lp["w_proj_c"]))
    return merged @ lp["w_out"], (k_new, v_new, ssd_h, ssd_conv, sc_conv)

def block(x, lp, past):
    x = x + 0.5 * swiglu(rmsnorm(x, lp["ffn1_norm"]), lp["ffn1_w_gate"], lp["ffn1_w_up"], lp["ffn1_w_down"])
    m, new_state = mix_layer(rmsnorm(x, lp["mix_norm"]), lp, past)
    x = x + m
    x = x + 0.5 * swiglu(rmsnorm(x, lp["ffn2_norm"]), lp["ffn2_w_gate"], lp["ffn2_w_up"], lp["ffn2_w_down"])
    return x, new_state

def setup_inputs(seed: int = 0) -> dict:
    key = jax.random.key(seed)
    ks = iter(jax.random.split(key, 48))
    f32 = jnp.float32

    def nrm(shape, scale):
        return jax.random.normal(next(ks), shape, f32) * scale

    def gain(shape):
        return 1.0 + nrm(shape, 0.1)

    n_pages = PAST_LEN // PAGE_SIZE
    n_used = DEC_BATCH * n_pages
    n_phys = n_used + (n_used + 3) // 4
    page_table = jax.random.permutation(next(ks), n_phys)[:n_used].reshape(DEC_BATCH, n_pages).astype(jnp.int32)
    dt_init = jnp.exp(jax.random.uniform(next(ks), (DEPTH, SSD_HEADS), f32, math.log(1e-3), math.log(1e-1)))
    return {
        "x_prompt": nrm((BATCH, SEQ, D_MODEL), 1.0),
        "x_sample": nrm((DEC_BATCH, DEC_SEQ, D_MODEL), 1.0),
        "cache_sb_k": nrm((DEPTH, n_phys, PAGE_SIZE, SB_HEADS, SB_HEAD_DIM), 1.0),
        "cache_sb_v": nrm((DEPTH, n_phys, PAGE_SIZE, SB_HEADS, SB_HEAD_DIM), 1.0),
        "page_table": page_table,
        "state_ssd": nrm((DEPTH, DEC_BATCH, SSD_HEADS, SSD_HEAD_DIM, SSD_STATE), 0.1),
        "state_ssd_conv": nrm((DEPTH, DEC_BATCH, SSD_CONV - 1, SSD_CONV_DIM), 1.0),
        "state_sc_conv": nrm((DEPTH, DEC_BATCH, SC_CONV - 1, SC_WIDTH), 1.0),
        "ffn1_norm": gain((DEPTH, D_MODEL)),
        "ffn1_w_gate": nrm((DEPTH, D_MODEL, D_FF), D_MODEL ** -0.5),
        "ffn1_w_up": nrm((DEPTH, D_MODEL, D_FF), D_MODEL ** -0.5),
        "ffn1_w_down": nrm((DEPTH, D_FF, D_MODEL), D_FF ** -0.5),
        "mix_norm": gain((DEPTH, D_MODEL)),
        "w_in": nrm((DEPTH, D_MODEL, IN_COLS), D_MODEL ** -0.5),
        "gate_bias": nrm((DEPTH, N_BRANCHES * D_MODEL), 0.1),
        "ssd_conv_w": nrm((DEPTH, SSD_CONV, SSD_CONV_DIM), SSD_CONV ** -0.5),
        "ssd_conv_b": nrm((DEPTH, SSD_CONV_DIM), 0.1),
        "ssd_dt_bias": dt_init + jnp.log(-jnp.expm1(-dt_init)),
        "ssd_a_log": jnp.log(jax.random.uniform(next(ks), (DEPTH, SSD_HEADS), f32, 1.0, 16.0)),
        "ssd_d": gain((DEPTH, SSD_HEADS)),
        "ssd_norm": gain((DEPTH, SSD_WIDTH)),
        "sc_conv_w": nrm((DEPTH, SC_CONV, SC_WIDTH), SC_CONV ** -0.5),
        "sb_q_norm": gain((DEPTH, SB_HEAD_DIM)),
        "sb_k_norm": gain((DEPTH, SB_HEAD_DIM)),
        "sb_logit_bias": SB_BIAS_INIT + nrm((DEPTH, SB_HEADS), 0.5),
        "w_proj_a": nrm((DEPTH, SSD_WIDTH, D_MODEL), SSD_WIDTH ** -0.5),
        "w_proj_b": nrm((DEPTH, SC_WIDTH, D_MODEL), SC_WIDTH ** -0.5),
        "w_proj_c": nrm((DEPTH, SB_WIDTH, D_MODEL), SB_WIDTH ** -0.5),
        "w_out": nrm((DEPTH, D_MODEL, D_MODEL), D_MODEL ** -0.5),
        "ffn2_norm": gain((DEPTH, D_MODEL)),
        "ffn2_w_gate": nrm((DEPTH, D_MODEL, D_FF), D_MODEL ** -0.5),
        "ffn2_w_up": nrm((DEPTH, D_MODEL, D_FF), D_MODEL ** -0.5),
        "ffn2_w_down": nrm((DEPTH, D_FF, D_MODEL), D_FF ** -0.5),
    }

def reference(x_prompt, x_sample, cache_sb_k, cache_sb_v, page_table, state_ssd, state_ssd_conv,
              state_sc_conv, ffn1_norm, ffn1_w_gate, ffn1_w_up, ffn1_w_down, mix_norm, w_in, gate_bias,
              ssd_conv_w, ssd_conv_b, ssd_dt_bias, ssd_a_log, ssd_d, ssd_norm, sc_conv_w, sb_q_norm,
              sb_k_norm, sb_logit_bias, w_proj_a, w_proj_b, w_proj_c, w_out, ffn2_norm, ffn2_w_gate,
              ffn2_w_up, ffn2_w_down):
    dec_b = x_sample.shape[0]
    past_len = page_table.shape[1] * cache_sb_k.shape[2]
    yp, ys = x_prompt, x_sample
    kp_l, vp_l, ks_l, vs_l = [], [], [], []
    hp_l, hs_l, cp_l, cs_l, sp_l, ss_l = [], [], [], [], [], []
    for l in range(DEPTH):
        lp = {
            "ffn1_norm": ffn1_norm[l], "ffn1_w_gate": ffn1_w_gate[l], "ffn1_w_up": ffn1_w_up[l],
            "ffn1_w_down": ffn1_w_down[l], "mix_norm": mix_norm[l], "w_in": w_in[l],
            "gate_bias": gate_bias[l], "ssd_conv_w": ssd_conv_w[l], "ssd_conv_b": ssd_conv_b[l],
            "ssd_dt_bias": ssd_dt_bias[l], "ssd_a_log": ssd_a_log[l], "ssd_d": ssd_d[l],
            "ssd_norm": ssd_norm[l], "sc_conv_w": sc_conv_w[l], "sb_q_norm": sb_q_norm[l],
            "sb_k_norm": sb_k_norm[l], "sb_logit_bias": sb_logit_bias[l], "w_proj_a": w_proj_a[l],
            "w_proj_b": w_proj_b[l], "w_proj_c": w_proj_c[l], "w_out": w_out[l],
            "ffn2_norm": ffn2_norm[l], "ffn2_w_gate": ffn2_w_gate[l], "ffn2_w_up": ffn2_w_up[l],
            "ffn2_w_down": ffn2_w_down[l],
        }
        yp, (kp, vp, hp, cp, sp) = block(yp, lp, None)
        past_k = cache_sb_k[l][page_table].reshape(dec_b, past_len, SB_HEADS, SB_HEAD_DIM)
        past_v = cache_sb_v[l][page_table].reshape(dec_b, past_len, SB_HEADS, SB_HEAD_DIM)
        past = (past_k, past_v, state_ssd[l], state_ssd_conv[l], state_sc_conv[l])
        ys, (ks, vs, hs, cs, ss) = block(ys, lp, past)
        kp_l.append(kp); vp_l.append(vp); ks_l.append(ks); vs_l.append(vs)
        hp_l.append(hp); hs_l.append(hs); cp_l.append(cp); cs_l.append(cs); sp_l.append(sp); ss_l.append(ss)
    return (yp, ys,
            jnp.stack(kp_l), jnp.stack(vp_l), jnp.stack(ks_l), jnp.stack(vs_l),
            jnp.stack(hp_l), jnp.stack(hs_l), jnp.stack(cp_l), jnp.stack(cs_l),
            jnp.stack(sp_l), jnp.stack(ss_l))


_drawn_inputs = setup_inputs


def setup_inputs(seed=0):
    import zlib

    import numpy as np

    out = dict(_drawn_inputs(seed))
    spreads = {}
    factors = {}
    for name, (base, spread) in spreads.items():
        noise = np.random.default_rng([zlib.crc32(name.encode()), seed]).standard_normal(out[name].shape)
        drawn = base * np.exp(spread * noise) if base else spread * noise
        out[name] = jnp.asarray(drawn.astype(out[name].dtype))
    for name, factor in factors.items():
        out[name] = (out[name] * factor).astype(out[name].dtype)
    return out
```

```python
from contextlib import ExitStack

import concourse.bass as bass
from concourse import mybir

F32 = mybir.dt.float32
F32R = mybir.dt.float32r
I32 = mybir.dt.int32
ALU = mybir.AluOpType
ACT = mybir.ActivationFunctionType
AX_X = mybir.AxisListType.X
ds = bass.ds

P = 128
D = 1024
NP = 512
NS = 8
T = NP + NS
HALF = T // 2
DT = D // P
D_FF = 2816
FT = D_FF // P
EPS = 1e-6
HD = 64
SB_HEADS = 8
SB_T = SB_HEADS * HD // P
PAGES = 4
SSD_HEADS = 16
SSD_T = SSD_HEADS * HD // P
GROUPS = 2
GT = SSD_T // GROUPS
CH = NP // P
XBC_T = SSD_T + 2 * GROUPS
SC_T = 4

COL_GATE = 0
COL_Z = 3 * D
COL_XBC = COL_Z + D
COL_DT = COL_XBC + XBC_T * P
COL_SCB = COL_DT + SSD_HEADS
COL_SCC = COL_SCB + SC_T * P
COL_SCX = COL_SCC + SC_T * P
COL_Q = COL_SCX + SC_T * P
COL_K = COL_Q + SB_T * P
COL_V = COL_K + SB_T * P

KMAX = 8
STAGES = 4
SPLITS = 2
DOWN_K = [(0, 8), (8, 7), (15, 7)]
MERGE_K = [8, 8, 8, 4, 8, 4]

U_FFN1A, O_FFN1A = 0, 0
U_FFN1B, O_FFN1B = 2 * FT, 2 * FT
U_DT, O_DT = U_FFN1B + 3 * DT, O_FFN1B + DT
U_ATT, O_ATT = U_DT + 1, O_DT + 1
U_SSD, O_SSD = U_ATT + 8 * SB_T, O_ATT + 8 * SB_T
U_MERGE, O_MERGE = U_SSD + 3 * SC_T, O_SSD + 3 * SC_T
U_OUT, O_OUT = U_MERGE + 6 * DT, O_MERGE + 6 * DT
U_FFN2A, O_FFN2A = U_OUT + DT, O_OUT + DT
U_FFN2B, O_FFN2B = U_FFN2A + 2 * FT, O_FFN2A + 2 * FT
U_END = U_FFN2B + 3 * DT

SCORE_AT = [0, 512, 1024, 896]
SCORE_W = [512, 384, 256, 128]
SCORES = 1280
CONSTS = 6


class Signal:

    def __init__(self, sem, n):
        self.sem, self.n = sem, n

    def now(self, i, k=0):
        return self.n * i + (self.n + k + 1)

    def before(self, i, k=0):
        return self.n * i + (k + 1)


class Chain:

    def __init__(self, eng, sem):
        self.eng, self.sem, self.n, self.step = eng, sem, 0, 0

    def __call__(self, ins):
        ins.then_inc(self.sem, 1)
        self.n += 1
        self.eng.wait_ge(self.sem, self.n + self.step)

    def loop(self, i, per):
        self.step, self.first, self.per = per * i, self.n, per

    def end(self, turns):
        assert self.n == self.first + self.per, (self.n - self.first, self.per)
        self.step, self.n = 0, self.first + self.per * turns


def build(nc, ins, outs):
    ctx = ExitStack()
    with ctx:
        def sb(name, shape, dt=F32):
            return ctx.enter_context(nc.sbuf_tensor(name, shape, dt))

        def sem(name):
            return ctx.enter_context(nc.semaphore(name))

        ARENA = 128 * 1024
        arena_at = (nc.sbuf_base + 31) // 32 * 32
        arena = sb("arena", [P, ARENA // 4])
        xg_hi = sb("xg_hi", [P, DT, T], F32R)
        xg_lo = sb("xg_lo", [P, DT, T], F32R)
        stage = sb("stage", [P, STAGES, KMAX, P])
        w_hi = sb("w_hi", [P, SPLITS, KMAX, P], F32R)
        w_lo = sb("w_lo", [P, SPLITS, KMAX, P], F32R)
        rstd = sb("rstd", [P, T])
        sumsq = sb("sumsq", [P, T])
        sq = sb("sq", [P, T])
        silu = sb("silu", [P, T])
        prod = sb("prod", [P, T])
        ones = sb("ones", [P, P])
        ident = sb("ident", [P, P])
        upto = sb("upto", [P, P])
        after = sb("after", [P, P])
        blocks = sb("blocks", [P, P])
        norms = sb("norms", [P, 3, DT])
        gate_b = sb("gate_b", [P, 3 * DT])
        conv_w = sb("conv_w", [P, 5, XBC_T])
        sc_w = sb("sc_w", [P, 3, SC_T])
        qk_g = sb("qk_g", [P, 2])
        sb_bias = sb("sb_bias", [P, SB_HEADS])
        ssd_cols = sb("ssd_cols", [P, 2, SSD_T])
        ssd_rows = sb("ssd_rows", [SSD_HEADS, 2])
        eps = sb("eps", [P, 1])
        one = sb("one", [P, 1])
        table = sb("table", [1, NS * PAGES], I32)
        ps = ctx.enter_context(nc.psum_tensor("ps", [P, 8, 512], F32))
        flat = ps[:, :, :].rearrange("p b c -> p (b c)")

        def plan(at, *tenants):
            made = []
            for name, shape, dt in tenants:
                size = 4
                for n in shape[1:]:
                    size *= n
                made.append(nc.alloc_sbuf_tensor_at(name, shape, dt, offset=arena_at + at))
                at += (size + 31) // 32 * 32
            assert at <= ARENA, (tenants[0][0], at, ARENA)
            return made + [at]
        x, after_x = plan(0, ("x", [P, DT, T], F32))
        hid_hi, hid_lo, _ = plan(after_x, ("hid_hi", [P, FT, T], F32R), ("hid_lo", [P, FT, T], F32R))
        m_hi, m_lo, y_hi, y_lo, _ = plan(ARENA - 4 * T * 48, ("m_hi", [P, DT, T], F32R), ("m_lo", [P, DT, T], F32R),
                                         ("y_hi", [P, 16, T], F32R), ("y_lo", [P, 16, T], F32R))
        zs, yc, yb, xb, qdec, dt_t, la_t, end_branch = plan(
            0, ("zs", [P, SSD_T, T], F32), ("yc", [P, SB_T, T], F32), ("yb", [P, SC_T, T], F32),
            ("xb", [P, XBC_T, 3 + T], F32), ("qdec", [P, SB_T, NS], F32), ("dt_t", [SSD_HEADS, T], F32),
            ("la_t", [SSD_HEADS, T], F32))
        qr, kr, vr, qh, kh, v_tok, zb, lg, spl, strict, _ = plan(
            end_branch, ("qr", [P, T], F32), ("kr", [P, T], F32), ("vr", [P, T], F32), ("qh", [P, T], F32),
            ("kh", [P, T], F32), ("v_tok", [P, CH, P], F32), ("zb", [P, 2, SCORES], F32),
            ("lg", [P, 2, SCORES], F32), ("spl", [P, 2, SCORES], F32), ("strict", [P, P], F32))
        pages, qdiag, qb, zd, lgd, spd, _ = plan(
            end_branch, ("pages", [P, 2, PAGES, 512], F32), ("qdiag", [P, 2, SB_T, P], F32),
            ("qb", [P, 2, 512], F32), ("zd", [P, PAGES, NS, SB_HEADS], F32),
            ("lgd", [P, PAGES, NS, SB_HEADS], F32), ("spd", [P, PAGES, NS, SB_HEADS], F32))
        (bt, ct, b_tok, cb, dt_tok, la_tok, cs_tok, to_end, ch_dec, cs_t, sprev, cdec, ctmp, dtda, dtda_t,
         xdd, expand, neg, cv, xs, xd, xde, hin, gbuf, csc, state, stmp, bb, cbb, ydec, scx, scprev, sctail,
         _) = plan(
            end_branch, ("bt", [P, GROUPS, NP], F32), ("ct", [P, GROUPS, NP], F32),
            ("b_tok", [P, GROUPS, CH, P], F32), ("cb", [P, NP], F32),
            ("dt_tok", [P, CH, SSD_HEADS], F32), ("la_tok", [P, CH, SSD_HEADS], F32),
            ("cs_tok", [P, CH, SSD_HEADS], F32), ("to_end", [P, CH, SSD_HEADS], F32),
            ("ch_dec", [P, CH, SSD_HEADS], F32), ("cs_t", [SSD_HEADS, NP], F32),
            ("sprev", [P, XBC_T, 3, NS], F32), ("cdec", [P, XBC_T, NS], F32), ("ctmp", [P, XBC_T, NS], F32),
            ("dtda", [P, SSD_T, 2, NS], F32), ("dtda_t", [SSD_HEADS, 2, NS], F32), ("xdd", [P, SSD_T, NS], F32),
            ("expand", [SSD_HEADS, SSD_T, P], F32), ("neg", [P, P], F32),
            ("cv", [P, NP], F32), ("xs", [P, NP], F32), ("xd", [P, CH, P], F32), ("xde", [P, CH, P], F32),
            ("hin", [P, CH + 1, P], F32), ("gbuf", [P, 2, NP], F32), ("csc", [P, 2, NP], F32),
            ("state", [P, 2, NS, P], F32), ("stmp", [P, NS, P], F32), ("bb", [P, NS, P], F32),
            ("cbb", [P, NS, P], F32), ("ydec", [P, NS], F32), ("scx", [P, 2 + T], F32),
            ("scprev", [P, SC_T, 2, NS], F32), ("sctail", [P, SC_T, 2 + NS], F32))
        head_cs = la_t[:, 0:NP]
        x_kept = nc.dram_tensor("x_kept", (P, DT, T), F32, kind="Internal").ap()

        def acc(o):
            return ps[:, 2 * (o % 2):2 * (o % 2) + 2, 0:HALF]

        def halves(ap):
            return ap.rearrange("p (a b) -> p a b", a=2)

        landed = sem("landed")
        consts_set = sem("consts_set")
        w_landed = [sem(f"w_landed{s}") for s in range(STAGES)]
        unit_split = sem("unit_split")
        hi_ready = sem("hi_ready")
        unit_done = sem("unit_done")
        acc_read = sem("acc_read")
        silu_ready = sem("silu_ready")
        silu_scaled = sem("silu_scaled")
        hid_hi_ready = sem("hid_hi_ready")
        hid_ready = sem("hid_ready")
        xg_hi_ready = sem("xg_hi_ready")
        xg_ready = sem("xg_ready")
        sq_ready = sem("sq_ready")
        sumsq_ready = sem("sumsq_ready")
        stats_ready = sem("stats_ready")
        rms_ready = sem("rms_ready")
        rstd_ready = sem("rstd_ready")
        x_saved = sem("x_saved")
        x_back = sem("x_back")
        out_written = sem("out_written")
        dve_step = sem("dve_step")
        act_step = sem("act_step")
        pool_step = sem("pool_step")
        signals = []

        def signal(name, n):
            signals.append(Signal(sem(name), n))
            return signals[-1]
        qk_squared = signal("qk_squared", 2)
        qk_summed = signal("qk_summed", 2)
        qk_root = signal("qk_root", 2)
        qk_normed = signal("qk_normed", 2)
        kv_written = sem("kv_written")
        v_turned = signal("v_turned", 1)
        v_tok_ready = signal("v_tok_ready", 1)
        scored = signal("scored", 2)
        z_biased = signal("z_biased", 2)
        log_ready = signal("log_ready", 2)
        sp_ready = signal("sp_ready", 2)
        tail_summed = signal("tail_summed", 2)
        tail_taken = signal("tail_taken", 2)
        w_exped = signal("w_exped", 2)
        w_ready = signal("w_ready", 2)
        pv_done = signal("pv_done", 2)
        yc_ready = signal("yc_ready", 1)
        page_landed = [sem("page_landed0"), sem("page_landed1")]
        pages_used = signal("pages_used", 2)
        qdiag_ready = signal("qdiag_ready", 2)
        qb_spread = signal("qb_spread", 2)
        qb_ready = signal("qb_ready", 2)
        kq_ready = signal("kq_ready", 2)
        spd_ready = sem("spd_ready")
        zd_ready = sem("zd_ready")
        lgd_ready = sem("lgd_ready")
        taild_ready = sem("taild_ready")
        wd_raw = sem("wd_raw")
        wd_ready = sem("wd_ready")
        pvd_done = signal("pvd_done", 2)
        expand_set = sem("expand_set")
        cb_made = sem("cb_made")
        cb_ready = sem("cb_ready")
        bc_diag = sem("bc_diag")
        bc_spread = sem("bc_spread")
        bc_ready = sem("bc_ready")
        prep_d = sem("prep_d")
        prep_a = sem("prep_a")
        prep_p = sem("prep_p")
        conv_in = sem("conv_in")
        ssd_written = sem("ssd_written")
        conv_ready = signal("conv_ready", 2)
        xs_ready = signal("xs_ready", 2)
        xs_turned = signal("xs_turned", 2)
        xd_ready = signal("xd_ready", 2)
        xde_ready = signal("xde_ready", 2)
        states_ready = signal("states_ready", 2)
        hin_ready = signal("hin_ready", 2)
        hfin_written = [sem("hfin_written0"), sem("hfin_written1")]
        head_cs_ready = signal("head_cs_ready", 4)
        cs_spread = signal("cs_spread", 4)
        seg_ready = signal("seg_ready", 4)
        decay_ready = signal("decay_ready", 4)
        ecs_ready = signal("ecs_ready", 4)
        csc_ready = signal("csc_ready", 4)
        g_ready = signal("g_ready", 4)
        y_summed = signal("y_summed", 2)
        y_ready = signal("y_ready", 2)
        state_landed = [sem("state_landed0"), sem("state_landed1")]
        state_written = [sem("state_written0"), sem("state_written1")]
        outer_ready = signal("outer_ready", 2)
        state_ready = signal("state_ready", 2)
        sample_done = signal("sample_done", 2)
        ysq_ready = sem("ysq_ready")
        ysum_ready = sem("ysum_ready")
        yroot_ready = sem("yroot_ready")
        yhi_ready = sem("yhi_ready")
        yprod_ready = sem("yprod_ready")
        y_split = sem("y_split")
        gate_open = sem("gate_open")
        merged = sem("merged")
        m_hi_ready = sem("m_hi_ready")
        m_ready = sem("m_ready")

        def kpm(w):
            return w.rearrange("l (k p) m -> (l p) k m", p=P)
        w = {n: kpm(ins[n]) for n in ("ffn1_w_gate", "ffn1_w_up", "ffn1_w_down", "w_in", "w_proj_a", "w_proj_b",
                                      "w_proj_c", "w_out", "ffn2_w_gate", "ffn2_w_up", "ffn2_w_down")}

        def load_unit(u0, step, src, kt):
            s = u0 % STAGES
            nc.sync.wait_ge(unit_split, u0 + 1 + step)
            nc.sync.dma_start(stage[:, s, 0:kt, :], src).then_inc(w_landed[s], 16)

        def round_unit(u0, step, kt):
            s, r = u0 % STAGES, u0 % SPLITS
            nc.scalar.wait_ge(w_landed[s], 16 * (u0 // STAGES + 1) + 16 // STAGES * step)
            nc.scalar.wait_ge(unit_done, u0 + 1 + step)
            nc.scalar.activation(w_hi[:, r, 0:kt, :], stage[:, s, 0:kt, :], ACT.Copy).then_inc(hi_ready, 1)

        def rest_unit(u0, step, kt):
            s, r = u0 % STAGES, u0 % SPLITS
            nc.vector.wait_ge(hi_ready, u0 + 1 + step)
            nc.vector.tensor_tensor(w_lo[:, r, 0:kt, :], stage[:, s, 0:kt, :], w_hi[:, r, 0:kt, :].bitcast(F32),
                                    ALU.subtract).then_inc(unit_split, 1)

        def multiply_unit(u0, step, o0, ostep, kt, rhs, start=True, stop=True):
            r = u0 % SPLITS
            out = acc(o0)
            if start:
                nc.tensor.wait_ge(acc_read, o0 + 1 + ostep)
            nc.tensor.wait_ge(unit_split, STAGES + u0 + 1 + step)
            for k in range(kt):
                hi, lo = rhs(k)
                for n, (wt, v) in enumerate(((w_hi, hi), (w_hi, lo), (w_lo, hi))):
                    for h in range(2):
                        mm = nc.tensor.matmul(out[:, h, :], wt[:, r, k, :], v[:, h * HALF:(h + 1) * HALF],
                                              start=start and k == 0 and n == 0,
                                              stop=stop and k == kt - 1 and n == 2)
            mm.then_inc(unit_done, 1)

        def xg(k):
            return xg_hi[:, k, :], xg_lo[:, k, :]

        def wait_unit(dve, u0, step=0):
            dve.wait_ge(unit_done, SPLITS + u0 + 1 + step)

        def wait_output(eng, o0, step=0):
            eng.wait_ge(acc_read, 2 + o0 + 1 + step)

        sc_gated = sem("sc_gated")
        sc_tail_copied = sem("sc_tail_copied")

        def wait_sctail(eng):
            eng.wait_ge(sc_tail_copied, SC_T)

        def branches_stored(eng):
            for written in state_written:
                eng.wait_ge(written, 16 * SC_T)
            eng.wait_ge(hfin_written[0], 16 * SSD_T)
            eng.wait_ge(out_written, 96)

        w_in_att = [COL_Q, COL_K, COL_V, COL_Z, COL_Z + P, COL_XBC, COL_XBC + P, COL_XBC + 2 * P]
        w_in_step = [P, P, P, 2 * P, 2 * P, 3 * P, 3 * P, 3 * P]

        block = ctx.enter_context(nc.Block())

        @block.sync
        def _(sp):
            for s in signals:
                sp.sem_inc(s.sem, s.n)
            sp.sem_inc(kv_written, 32)
            sp.dma_start(x[:, :, :], ins["x_t"]).then_inc(landed, 16)
            for name, tile in (("norms", norms[:, :, :]), ("gate_b", gate_b[:, :]), ("conv_w", conv_w[:, :, :]),
                               ("sc_w", sc_w[:, :, :]), ("qk_g", qk_g[:, :]), ("ssd_cols", ssd_cols[:, :, :]),
                               ("ssd_rows", ssd_rows[:, :]), ("table", table[:, :])):
                sp.dma_start(tile, ins[name]).then_inc(landed, 16)
            sp.dma_start(sb_bias[:, :], ins["sb_bias"].partition_broadcast(P)).then_inc(landed, 16)

            def ffn_loads(n, u_a, u_b):
                wg, wu, wd = w[f"ffn{n}_w_gate"], w[f"ffn{n}_w_up"], w[f"ffn{n}_w_down"]
                with sp.Fori(0, FT // 2) as i:
                    for j in range(4):
                        load_unit(u_a + j, 4 * i, (wg, wu)[j % 2][:, :, ds((i * 2 + j // 2) * P, P)], DT)
                with sp.Fori(0, 2) as i:
                    for j in range(12):
                        k0, kt = DOWN_K[j % 3]
                        load_unit(u_b + j, 12 * i, wd[:, k0:k0 + kt, ds((i * 4 + j // 3) * P, P)], kt)
            ffn_loads(1, U_FFN1A, U_FFN1B)
            load_unit(U_DT, 0, w["w_in"][:, :, COL_DT:COL_DT + P], DT)
            sp.wait_ge(xg_ready, 2 * DT)
            sp.dma_start(x_kept, x[:, :, :]).then_inc(x_saved, 16)
            with sp.Fori(0, SB_T) as t:
                for j in range(8):
                    load_unit(U_ATT + j, 8 * t, w["w_in"][:, :, ds(t * w_in_step[j] + w_in_att[j], P)], DT)
                    if j == 5:
                        sp.wait_ge(qk_normed.sem, qk_normed.now(t, 1))
                        sp.dma_start(outs["k_t"][:, ds(t, 1), :], kh[:, :].unsqueeze(1)).then_inc(kv_written, 16)
                        sp.dma_start(outs["v_t"][:, ds(t, 1), :], vr[:, :].unsqueeze(1)).then_inc(kv_written, 16)

            def load_sc(n):
                col = (COL_SCC, COL_SCX, COL_SCB)[n % 3] + n // 3 * P
                load_unit(U_SSD + n, 0, w["w_in"][:, :, col:col + P], DT)
            for n in range(3):
                load_sc(n)

            def load_pages(cache, used):
                with sp.Fori(0, NS // 2) as i:
                    for b in range(2):
                        sp.wait_ge(used.sem, used.before(i, b))
                        for p in range(PAGES):
                            page = sp.value_load(table[0:1, ds(i * (2 * PAGES) + b * PAGES + p, 1)], min_val=0,
                                                 max_val=cache.shape[1] - 1)
                            sp.dma_start(pages[:, b, p, :], cache[0, ds(page, 1)].rearrange("o t h d -> (o t) (h d)")
                                         ).then_inc(page_landed[b], 16)
            sp.wait_ge(yc_ready.sem, yc_ready.now(SB_T - 1))
            sp.wait_ge(kv_written, 32 * SB_T + 32)
            load_pages(ins["cache_sb_k"], pages_used)
            sp.wait_ge(pages_used.sem, pages_used.now(NS // 2 - 1, 1))
            load_pages(ins["cache_sb_v"], pvd_done)

            sp.wait_ge(pvd_done.sem, pvd_done.now(NS // 2 - 1, 1))
            sp.dma_start(sprev[:, :, :, :], ins["ssd_prev"]).then_inc(conv_in, 16)
            sp.dma_start(scprev[:, :, :, :], ins["sc_prev"]).then_inc(conv_in, 16)
            sp.dma_start(outs["ssd_conv_p"], xb[:, :, NP:NP + 3]).then_inc(out_written, 16)
            sp.dma_start(outs["ssd_conv_s"][:, :, 2, :], xb[:, :, 3 + NP:3 + T]).then_inc(out_written, 16)
            sp.wait_ge(conv_in, 32)
            sp.dma_start(outs["ssd_conv_s"][:, :, 0:2, :], sprev[:, :, 1:3, :]).then_inc(out_written, 16)
            sp.dma_start(outs["sc_conv_s"][:, :, 0, :], scprev[:, :, 1, :]).then_inc(out_written, 16)
            for n in range(3, 3 * SC_T):
                load_sc(n)
            wait_sctail(sp)
            sp.dma_start(outs["sc_conv_p"], sctail[:, :, 0:2]).then_inc(out_written, 16)
            sp.dma_start(outs["sc_conv_s"][:, :, 1, :], sctail[:, :, 2:2 + NS]).then_inc(out_written, 16)
            with sp.Fori(0, DT // 2) as i:
                for c in range(2):
                    m = i * (2 * P) + c * P
                    for j, src in enumerate((w["w_in"][:, :, ds(m, P)], w["w_proj_a"][:, :, ds(m, P)],
                                             w["w_in"][:, :, ds(m + D, P)], w["w_proj_b"][:, :, ds(m, P)],
                                             w["w_in"][:, :, ds(m + 2 * D, P)], w["w_proj_c"][:, :, ds(m, P)])):
                        load_unit(U_MERGE + 6 * c + j, 12 * i, src, MERGE_K[j])
            sp.wait_ge(y_split, 4)
            sp.wait_ge(out_written, 96)
            sp.wait_ge(x_saved, 16)
            sp.dma_start(x[:, :, :], x_kept).then_inc(x_back, 16)
            with sp.Fori(0, 2) as i:
                for j in range(4):
                    load_unit(U_OUT + j, 4 * i, w["w_out"][:, :, ds(i * (4 * P) + j * P, P)], DT)
            ffn_loads(2, U_FFN2A, U_FFN2B)
            for c in range(DT):
                wait_output(sp, O_FFN2B + c)
                sp.dma_start(outs["y_t"][:, c, :], x[:, c, :]).then_inc(out_written, 16)
            sp.wait_ge(out_written, 96 + 16 * DT)

        @block.scalar
        def _(act):
            link = Chain(act, act_step)
            act.sem_inc(unit_done, SPLITS)

            def square(n, k):
                act.wait_ge(xg_ready, n * DT + k + 1)
                act.wait_ge(sumsq_ready, n * DT + k)
                nc.scalar.activation(sq[:, :], x[:, k, :], ACT.Square).then_inc(sq_ready, 1)

            def root(n):
                act.wait_ge(stats_ready, n + 1)
                nc.scalar.activation(halves(rstd[:, :]), ps[:, 4:6, 0:HALF], ACT.Sqrt, bias=eps[:, 0:1],
                                     scale=1.0 / D).then_inc(rms_ready, 1)

            def ffn_a(n, u_a, o_a):
                done = (n - 1) * FT
                act.preload_act_table(ACT.Silu)
                with act.Fori(0, FT // 2) as i:
                    for j in range(4):
                        m = j // 2
                        round_unit(u_a + j + 1, 4 * i, DT)
                        wait_output(act, o_a + j, 4 * i)
                        if j % 2 == 0:
                            nc.scalar.activation(silu[:, :], silu[:, :], ACT.Silu).then_inc(silu_ready, 1)
                        else:
                            nc.scalar.activation(hid_hi[:, ds(2 * i + m, 1), :], prod[:, :].unsqueeze(1), ACT.Copy
                                                 ).then_inc(hid_hi_ready, 1)

            def ffn_b(n, u_b):
                for k in range(3 * DT):
                    if u_b + k + 1 < U_END:
                        round_unit(u_b + k + 1, 0, DOWN_K[(k + 1) % 3][1])
                    if k % 3 == 2 and n == 1:
                        square(1, k // 3)

            act.wait_ge(landed, 10 * 16)
            act.wait_ge(consts_set, CONSTS)
            for k in range(DT):
                square(0, k)
            round_unit(0, 0, DT)
            root(0)
            ffn_a(1, U_FFN1A, O_FFN1A)
            ffn_b(1, U_FFN1B)
            root(1)
            round_unit(U_ATT, 0, DT)

            act.preload_act_table_set("natural_log_exp_and_others")
            with act.Fori(0, SB_T) as t:
                link.loop(t, 2 + 2 * 2)
                up = 8 * t

                def rms_inverse(k, dst):
                    act.wait_ge(qk_summed.sem, qk_summed.now(t, k))
                    link(nc.scalar.activation(halves(dst), ps[:, 4 + 2 * k:6 + 2 * k, 0:HALF], ACT.Ln,
                                              bias=eps[:, 0:1], scale=1.0 / HD))
                    nc.scalar.activation(dst, dst, ACT.Exp, scale=-0.5).then_inc(qk_root.sem, 1)

                def softplus_log(e):
                    act.wait_ge(z_biased.sem, z_biased.now(t, e))
                    link(nc.scalar.activation(lg[:, e, :], zb[:, e, :], ACT.Abs))
                    link(nc.scalar.activation(lg[:, e, :], lg[:, e, :], ACT.Exp, scale=-1.0))
                    nc.scalar.activation(lg[:, e, :], lg[:, e, :], ACT.Ln, bias=one[:, 0:1]).then_inc(log_ready.sem, 1)

                def weights(e):
                    act.wait_ge(tail_taken.sem, tail_taken.now(t, e))
                    nc.scalar.activation(zb[:, e, :], zb[:, e, :], ACT.Exp).then_inc(w_exped.sem, 1)

                round_unit(U_ATT + 1, up, DT)
                round_unit(U_ATT + 2, up, DT)
                wait_output(act, O_ATT, up)
                act.wait_ge(qk_normed.sem, qk_normed.before(t, 1))
                nc.scalar.activation(sq[:, :], qr[:, :], ACT.Square).then_inc(qk_squared.sem, 1)
                round_unit(U_ATT + 3, up, DT)
                wait_output(act, O_ATT + 1, up)
                nc.scalar.activation(prod[:, :], kr[:, :], ACT.Square).then_inc(qk_squared.sem, 1)
                rms_inverse(0, sq[:, :])
                rms_inverse(1, prod[:, :])
                round_unit(U_ATT + 4, up, DT)
                round_unit(U_ATT + 5, up, DT)
                softplus_log(0)
                round_unit(U_ATT + 6, up, DT)
                weights(0)
                round_unit(U_ATT + 7, up, DT)
                softplus_log(1)
                round_unit(U_ATT + 8, up, DT)
                weights(1)
            link.end(SB_T)

            with act.Fori(0, NS // 2) as i:
                for b in range(2):
                    act.wait_ge(qb_spread.sem, qb_spread.now(i, b))
                    act.wait_ge(kq_ready.sem, kq_ready.before(i, b))
                    nc.scalar.activation(qb[:, b, :], ps[:, 4 + b, :], ACT.Copy).then_inc(qb_ready.sem, 1)
            act.wait_ge(zd_ready, 1)
            link(nc.scalar.activation(lgd[:, :, :, :], zd[:, :, :, :], ACT.Abs))
            link(nc.scalar.activation(lgd[:, :, :, :], lgd[:, :, :, :], ACT.Exp, scale=-1.0))
            nc.scalar.activation(lgd[:, :, :, :], lgd[:, :, :, :], ACT.Ln, bias=one[:, 0:1]).then_inc(lgd_ready, 1)
            act.wait_ge(wd_raw, 1)
            nc.scalar.activation(zd[:, :, :, :], zd[:, :, :, :], ACT.Exp).then_inc(wd_ready, 1)

            act.wait_ge(prep_d, 1)
            link(nc.scalar.activation(silu[0:SSD_HEADS, :], dt_t[:, :], ACT.Abs))
            nc.scalar.activation(silu[0:SSD_HEADS, :], silu[0:SSD_HEADS, :], ACT.Exp, scale=-1.0).then_inc(prep_a, 1)
            nc.scalar.activation(ssd_rows[:, 1:2], ssd_rows[:, 1:2], ACT.Exp).then_inc(prep_a, 1)
            act.wait_ge(prep_d, 2)
            nc.scalar.activation(sq[0:SSD_HEADS, :], prod[0:SSD_HEADS, :], ACT.Ln).then_inc(prep_a, 1)
            act.wait_ge(prep_d, 3)
            nc.scalar.activation(dtda_t[:, 1, :], la_t[:, NP:T], ACT.Exp).then_inc(prep_a, 1)
            act.wait_ge(prep_d, 5)
            nc.scalar.activation(to_end[:, :, :], to_end[:, :, :], ACT.Exp).then_inc(prep_a, 1)
            nc.scalar.activation(ch_dec[:, :, :], flat[:, 7 * 512:7 * 512 + CH * SSD_HEADS].rearrange(
                "p (c h) -> p c h", c=CH), ACT.Exp).then_inc(prep_a, 1)
            for k, dst in enumerate((bt, bt, ct, ct)):
                act.wait_ge(prep_d, 8 + k)
                src = (gbuf, csc)[k // 2][:, k % 2, :]
                nc.scalar.activation(dst[:, k % 2, :], src, ACT.Silu).then_inc(prep_a, 1)
            act.wait_ge(prep_d, 12)
            nc.scalar.activation(cdec[:, :, :], cdec[:, :, :], ACT.Silu).then_inc(prep_a, 1)

            for it in range(SC_T):
                g = it // 2
                if it % 2 == 0:
                    act.wait_ge(cb_made, g + 1)
                    nc.scalar.activation(cb[:, :], ps[:, 5, :], ACT.Copy).then_inc(cb_ready, 1)
                    for k, dst in enumerate((bb, cbb)):
                        act.wait_ge(bc_spread, 2 * g + k + 1)
                        nc.scalar.activation(dst[:, :, :], ps[:, 6:8, :].rearrange("p a (b n) -> p (a b) n", n=P),
                                             ACT.Copy).then_inc(bc_ready, 1)

                def silus(k):
                    t = 2 * it + k
                    act.wait_ge(conv_ready.sem, conv_ready.now(it, k))
                    link(nc.scalar.activation(zs[:, t, :], zs[:, t, :], ACT.Silu))
                    if t:
                        act.wait_ge(y_ready.sem, y_ready.now(it, 0) if k else y_ready.before(it, 1))
                    nc.scalar.activation(xs[:, :], cv[:, :], ACT.Silu).then_inc(xs_ready.sem, 1)

                def pick(k, e):
                    h = 4 * it + 2 * k + e
                    if it or k or e:
                        act.wait_ge(cs_spread.sem, cs_spread.now(it, 2 * k + e - 1) if k or e else cs_spread.before(it, 3))
                    nc.scalar.activation(head_cs, cs_t[:, :], ACT.Copy, scale=ident[0:SSD_HEADS, h:h + 1]
                                         ).then_inc(head_cs_ready.sem, 1)

                def decays(k, e):
                    act.wait_ge(seg_ready.sem, seg_ready.now(it, 2 * k + e))
                    nc.scalar.activation(csc[:, e, :], ps[:, (6, 4)[e], :], ACT.Exp).then_inc(ecs_ready.sem, 1)
                    nc.scalar.activation(gbuf[:, e, :], gbuf[:, e, :], ACT.Exp).then_inc(decay_ready.sem, 1)

                silus(0)
                pick(0, 0)
                round_unit(U_SSD + 3 * it + 1, 0, DT)
                decays(0, 0)
                pick(0, 1)
                round_unit(U_SSD + 3 * it + 2, 0, DT)
                decays(0, 1)
                silus(1)
                pick(1, 0)
                round_unit(U_SSD + 3 * it + 3, 0, DT)
                decays(1, 0)
                pick(1, 1)
                decays(1, 1)

            def split_y(first, src, n, tiles):
                act.wait_ge(yprod_ready, n + 1)
                nc.scalar.activation(y_hi[:, first:first + tiles, :], src, ACT.Copy).then_inc(yhi_ready, 1)
            split_y(8, yb[:, :, :], 0, 4)
            split_y(12, yc[:, :, :], 1, 4)
            for t in range(SSD_T):
                if t >= 2:
                    act.wait_ge(ysum_ready, t - 1)
                nc.scalar.activation((sq, silu)[t % 2][:, :], zs[:, t, :], ACT.Square).then_inc(ysq_ready, 1)
            for g in range(GROUPS):
                dst = (sumsq, prod)[g][:, :]
                act.wait_ge(ysum_ready, GT * (g + 1))
                link(nc.scalar.activation(halves(dst), ps[:, 4 + 2 * g:6 + 2 * g, 0:HALF], ACT.Ln, bias=eps[:, 0:1],
                                          scale=1.0 / (GT * P)))
                nc.scalar.activation(dst, dst, ACT.Exp, scale=-0.5).then_inc(yroot_ready, 1)
            for g in range(GROUPS):
                split_y(GT * g, zs[:, GT * g:GT * g + GT, :], 2 + g, GT)

            act.preload_act_table(ACT.Sigmoid)
            with act.Fori(0, DT // 2) as i:
                for c in range(2):
                    for j in range(6):
                        round_unit(U_MERGE + 6 * c + j + 1, 12 * i, MERGE_K[(j + 1) % 6])
                        if j % 2 == 0:
                            wait_output(act, O_MERGE + 6 * c + j, 12 * i)
                            nc.scalar.activation(silu[:, :], silu[:, :], ACT.Sigmoid,
                                                 bias=gate_b[:, ds(2 * i + (c + DT * (j // 2)), 1)]
                                                 ).then_inc(gate_open, 1)
                    act.wait_ge(merged, 2 * i + (c + 2))
                    nc.scalar.activation(m_hi[:, ds(2 * i + c, 1), :], prod[:, :].unsqueeze(1), ACT.Copy
                                         ).then_inc(m_hi_ready, 1)
            for c in range(DT):
                round_unit(U_OUT + c + 1, 0, DT)
                square(2, c)
            root(2)
            ffn_a(2, U_FFN2A, O_FFN2A)
            ffn_b(2, U_FFN2B)

        @block.vector
        def _(dve):
            link = Chain(dve, dve_step)
            dve.sem_inc(unit_split, STAGES)
            dve.sem_inc(acc_read, 2)
            dve.sem_inc(merged, 1)
            nc.vector.memset(eps[:, :], EPS).then_inc(consts_set, 1)
            nc.vector.memset(one[:, :], 1.0).then_inc(consts_set, 1)
            link(nc.vector.memset(blocks[:, :], 0.0))
            nc.vector.memset(blocks[0:HD, 0:HD], 1.0)
            nc.vector.memset(blocks[HD:P, HD:P], 1.0).then_inc(consts_set, 1)
            dve.wait_ge(landed, 10 * 16)
            link(nc.vector.tensor_scalar(qk_g[:, 0:1], qk_g[:, 0:1], HD ** -0.5, None, ALU.mult))
            dve.wait_ge(consts_set, CONSTS)

            def make_xg(c, n, count):
                nc.vector.tensor_scalar(xg_hi[:, c, :], x[:, c, :], norms[:, n, c:c + 1], None, ALU.mult
                                        ).then_inc(xg_hi_ready, 1)
                dve.wait_ge(xg_hi_ready, count + 1)
                nc.vector.scalar_tensor_tensor(xg_lo[:, c, :], x[:, c, :], norms[:, n, c:c + 1],
                                               xg_hi[:, c, :].bitcast(F32), ALU.mult, ALU.subtract
                                               ).then_inc(xg_ready, 1)

            def invert_rms(n):
                dve.wait_ge(rms_ready, n + 1)
                nc.vector.reciprocal(rstd[:, :], rstd[:, :]).then_inc(rstd_ready, 1)
                dve.wait_ge(rstd_ready, n + 1)

            def scaled(dst, o):
                return nc.vector.tensor_tensor(dst, acc(o), halves(rstd[:, :]), ALU.mult)

            def ffn_a(n, u_a, o_a):
                with dve.Fori(0, FT // 2) as i:
                    link.loop(i, 2)
                    for j in range(4):
                        m = j // 2
                        rest_unit(u_a + j + 1, 4 * i, DT)
                        if j % 2 == 0:
                            wait_unit(dve, u_a + j, 4 * i)
                            scaled(halves(silu[:, :]), o_a + j).then_inc(acc_read, 1)
                        else:
                            dve.wait_ge(silu_ready, m + 1 + (n - 1) * FT + 2 * i)
                            link(nc.vector.tensor_tensor(silu[:, :], silu[:, :], rstd[:, :], ALU.mult))
                            wait_unit(dve, u_a + j, 4 * i)
                            nc.vector.tensor_tensor(halves(prod[:, :]), acc(o_a + j), halves(silu[:, :]), ALU.mult
                                                    ).then_inc(acc_read, 1)
                            dve.wait_ge(hid_hi_ready, m + 1 + (n - 1) * FT + 2 * i)
                            nc.vector.tensor_tensor(hid_lo[:, ds(2 * i + m, 1), :], prod[:, :].unsqueeze(1),
                                                    hid_hi[:, ds(2 * i + m, 1), :].bitcast(F32), ALU.subtract
                                                    ).then_inc(hid_ready, 1)
                link.end(FT // 2)

            def add_to_x(c, o, factor, n):
                nc.vector.scalar_tensor_tensor(halves(x[:, c, :]), acc(o), factor, halves(x[:, c, :]),
                                               ALU.mult, ALU.add).then_inc(acc_read, 1)
                if n < 3:
                    wait_output(dve, o)
                    make_xg(c, n, n * DT + c)

            def ffn_b(n, u_b, o_b):
                for k in range(3 * DT):
                    if u_b + k + 1 < U_END:
                        rest_unit(u_b + k + 1, 0, DOWN_K[(k + 1) % 3][1])
                    if k % 3 == 2:
                        wait_unit(dve, u_b + k)
                        add_to_x(k // 3, o_b + k // 3, 0.5, 1 if n == 1 else 3)

            for c in range(DT):
                make_xg(c, 0, c)
            rest_unit(0, 0, DT)
            invert_rms(0)
            ffn_a(1, U_FFN1A, O_FFN1A)
            ffn_b(1, U_FFN1B, O_FFN1B)
            invert_rms(1)
            rest_unit(U_ATT, 0, DT)
            wait_unit(dve, U_DT)
            dve.wait_ge(x_saved, 16)
            nc.vector.tensor_tensor(halves(dt_t[:, :]), acc(O_DT)[0:SSD_HEADS], halves(rstd[0:SSD_HEADS, :]), ALU.mult
                                    ).then_inc(acc_read, 1)
            nc.vector.memset(xb[:, :, 0:3], 0.0)
            link(nc.vector.tensor_tensor(strict[:, :], upto[:, :], ident[:, :], ALU.subtract))

            with dve.Fori(0, SB_T) as t:
                link.loop(t, 2 * 2 + 1)
                up = 8 * t

                def take(j, dst):
                    rest_unit(U_ATT + j + 1, up, DT)
                    wait_unit(dve, U_ATT + j, up)
                    scaled(dst, O_ATT + j).then_inc(acc_read, 1)

                def take_z(j):
                    take(3 + j, zs[:, ds(2 * t + j, 1), :].rearrange("p o (a b) -> p (o a) b", a=2))

                def take_x(j):
                    take(5 + j, xb[:, ds(3 * t + j, 1), 3:3 + T].rearrange("p o (a b) -> p (o a) b", a=2))

                def bias_z(e):
                    dve.wait_ge(scored.sem, scored.now(t, e))
                    nc.vector.tensor_scalar(zb[:, e, :], flat[:, 2048:2048 + SCORES],
                                            sb_bias[:, ds(2 * t + e, 1)], None, ALU.add).then_inc(z_biased.sem, 1)

                def mask_diagonals(buf):
                    a = buf[:, 0:1024].rearrange("p (j i) -> p j i", j=2)[:, :, 0:P]
                    m = strict[:, :].unsqueeze(1).broadcast_to([P, 2, P])
                    nc.vector.tensor_tensor(a, a, m, ALU.mult)
                    b = buf[:, 896:1152].rearrange("p (j i) -> p j i", j=2)
                    return nc.vector.tensor_tensor(b, b, m, ALU.mult)

                def softplus(e):
                    dve.wait_ge(log_ready.sem, log_ready.now(t, e))
                    link(nc.vector.scalar_tensor_tensor(spl[:, e, :], zb[:, e, :], 0.0, lg[:, e, :], ALU.max, ALU.add))
                    mask_diagonals(spl[:, e, :]).then_inc(sp_ready.sem, 1)
                    link(nc.vector.scalar_tensor_tensor(zb[:, e, :], zb[:, e, :], 0.0, lg[:, e, :], ALU.min,
                                                        ALU.subtract))

                def take_tail(e):
                    dve.wait_ge(tail_summed.sem, tail_summed.now(t, e))
                    nc.vector.tensor_tensor(zb[:, e, :], zb[:, e, :], flat[:, 2048:2048 + SCORES], ALU.subtract
                                            ).then_inc(tail_taken.sem, 1)

                def mask_weights(e):
                    dve.wait_ge(w_exped.sem, w_exped.now(t, e))
                    mask_diagonals(zb[:, e, :]).then_inc(w_ready.sem, 1)

                take(0, halves(qr[:, :]))
                dve.wait_ge(kv_written, 32 * t + 32)
                take(1, halves(kr[:, :]))
                take(2, halves(vr[:, :]))
                for k, (raw, hat, inv) in enumerate(((qr, qh, sq), (kr, kh, prod))):
                    dve.wait_ge(qk_root.sem, qk_root.now(t, k))
                    nc.vector.scalar_tensor_tensor(hat[:, :], raw[:, :], qk_g[:, k:k + 1], inv[:, :], ALU.mult,
                                                   ALU.mult).then_inc(qk_normed.sem, 1)
                dve.wait_ge(qk_normed.sem, qk_normed.now(t, 0))
                link(nc.vector.tensor_copy(qdec[:, ds(t, 1), :], qh[:, NP:T].unsqueeze(1)))
                dve.wait_ge(v_turned.sem, v_turned.now(t))
                nc.vector.tensor_copy(v_tok[:, :, :], ps[:, 7, :].rearrange("p (c d) -> p c d", c=CH)
                                      ).then_inc(v_tok_ready.sem, 1)
                take_z(0)
                bias_z(0)
                rest_unit(U_ATT + 5, up, DT)
                softplus(0)
                wait_unit(dve, U_ATT + 4, up)
                scaled(zs[:, ds(2 * t + 1, 1), :].rearrange("p o (a b) -> p (o a) b", a=2), O_ATT + 4
                       ).then_inc(acc_read, 1)
                take_tail(0)
                rest_unit(U_ATT + 6, up, DT)
                wait_unit(dve, U_ATT + 5, up)
                scaled(xb[:, ds(3 * t, 1), 3:3 + T].rearrange("p o (a b) -> p (o a) b", a=2), O_ATT + 5
                       ).then_inc(acc_read, 1)
                bias_z(1)
                mask_weights(0)
                rest_unit(U_ATT + 7, up, DT)
                softplus(1)
                wait_unit(dve, U_ATT + 6, up)
                scaled(xb[:, ds(3 * t + 1, 1), 3:3 + T].rearrange("p o (a b) -> p (o a) b", a=2), O_ATT + 6
                       ).then_inc(acc_read, 1)
                take_tail(1)
                rest_unit(U_ATT + 8, up, DT)
                mask_weights(1)
                wait_unit(dve, U_ATT + 7, up)
                scaled(xb[:, ds(3 * t + 2, 1), 3:3 + T].rearrange("p o (a b) -> p (o a) b", a=2), O_ATT + 7
                       ).then_inc(acc_read, 1)
                dve.wait_ge(pv_done.sem, pv_done.now(t, 1))
                nc.vector.tensor_copy(yc[:, ds(t, 1), 0:NP], ps[:, 7:8, :]).then_inc(yc_ready.sem, 1)
            link.end(SB_T)

            with dve.Fori(0, NS // 2) as i:
                for b in range(2):
                    dve.wait_ge(qb_spread.sem, qb_spread.before(i, b))
                    nc.vector.tensor_tensor(qdiag[:, b, :, :], ident[:, :].unsqueeze(1).broadcast_to([P, SB_T, P]),
                                            qdec[:, :, ds(2 * i + b, 1)].broadcast_to([P, SB_T, P]),
                                            ALU.mult).then_inc(qdiag_ready.sem, 1)
                for b in range(2):
                    dve.wait_ge(kq_ready.sem, kq_ready.now(i, b))
                    nc.vector.tensor_reduce(zd[:, :, ds(2 * i + b, 1), :].rearrange("p g o h -> p (g o) h"),
                                            pages[:, b, :, :].rearrange("p g (h d) -> p g h d", d=HD), AX_X, ALU.add
                                            ).then_inc(pages_used.sem, 1)
            dve.wait_ge(pages_used.sem, pages_used.now(NS // 2 - 1, 1))
            nc.vector.tensor_tensor(zd[:, :, :, :].rearrange("p g b h -> p (g b) h"),
                                    zd[:, :, :, :].rearrange("p g b h -> p (g b) h"),
                                    sb_bias[:, :].unsqueeze(1).broadcast_to([P, PAGES * NS, SB_HEADS]), ALU.add
                                    ).then_inc(zd_ready, 1)
            dve.wait_ge(lgd_ready, 1)
            nc.vector.scalar_tensor_tensor(spd[:, :, :, :], zd[:, :, :, :], 0.0, lgd[:, :, :, :], ALU.max, ALU.add
                                           ).then_inc(spd_ready, 1)
            link(nc.vector.scalar_tensor_tensor(zd[:, :, :, :], zd[:, :, :, :], 0.0, lgd[:, :, :, :], ALU.min,
                                                ALU.subtract))
            dve.wait_ge(taild_ready, 1)
            nc.vector.tensor_tensor(zd[:, :, :, :], zd[:, :, :, :],
                                    ps[:, 6, 0:PAGES * NS * SB_HEADS].rearrange("p (g b h) -> p g b h", g=PAGES, b=NS),
                                    ALU.subtract).then_inc(wd_raw, 1)
            dve.wait_ge(pvd_done.sem, pvd_done.now(NS // 2 - 1, 1))
            pvd = ps[:, 7, 0:NS * SB_HEADS].rearrange("p (b t e) -> p e t b", b=NS, t=SB_T)
            for e in range(2):
                rows = slice(HD * e, HD * e + HD)
                link(nc.vector.tensor_copy(yc[rows, :, NP:T], pvd[rows, e]))

            R = SSD_HEADS
            nc.vector.tensor_scalar(dt_t[:, :], dt_t[:, :], ssd_rows[:, 0:1], None, ALU.add).then_inc(prep_d, 1)
            dve.wait_ge(prep_a, 1)
            nc.vector.tensor_scalar(prod[0:R, :], silu[0:R, :], 1.0, None, ALU.add).then_inc(prep_d, 1)
            dve.wait_ge(prep_d, 2)
            link(nc.vector.scalar_tensor_tensor(la_t[:, :], prod[0:R, :], -1.0, silu[0:R, :], ALU.add, ALU.subtract))
            dve.wait_ge(prep_a, 3)
            link(nc.vector.reciprocal(prod[0:R, :], prod[0:R, :]))
            link(nc.vector.tensor_tensor(la_t[:, :], la_t[:, :], prod[0:R, :], ALU.mult))
            link(nc.vector.tensor_tensor(sq[0:R, :], sq[0:R, :], la_t[:, :], ALU.subtract))
            link(nc.vector.scalar_tensor_tensor(dt_t[:, :], dt_t[:, :], 0.0, sq[0:R, :], ALU.max, ALU.add))
            nc.vector.tensor_copy(dtda_t[:, 0, :], dt_t[:, NP:T])
            nc.vector.tensor_scalar(la_t[:, :], dt_t[:, :], ssd_rows[:, 1:2], -1.0, ALU.mult, ALU.mult
                                    ).then_inc(prep_d, 1)
            dve.wait_ge(prep_p, 1)
            tok = "p (c h) -> p c h"
            nc.vector.tensor_copy(dt_tok[:, :, :], ps[:, 4, 0:CH * R].rearrange(tok, c=CH))
            nc.vector.tensor_copy(la_tok[:, :, :], ps[:, 5, 0:CH * R].rearrange(tok, c=CH)).then_inc(prep_d, 1)
            dve.wait_ge(prep_p, 2)
            link(nc.vector.tensor_copy(cs_tok[:, :, :], ps[:, 6, 0:CH * R].rearrange(tok, c=CH)))
            nc.vector.tensor_tensor(to_end[:, :, :], ps[:, 7, 0:CH * R].rearrange(tok, c=CH), cs_tok[:, :, :],
                                    ALU.subtract).then_inc(prep_d, 1)
            dve.wait_ge(prep_p, 3)
            nc.vector.tensor_copy(cs_t[:, :], ps[0:R, 4, :]).then_inc(prep_d, 1)
            nc.vector.tensor_copy(dtda[:, :, :, :], ps[:, 5, 0:SSD_T * 2 * NS].rearrange(
                "p (t k b) -> p t k b", t=SSD_T, k=2)).then_inc(prep_d, 1)

            def conv(dst, t):
                link(nc.vector.tensor_scalar(dst, xb[:, t, 0:NP], conv_w[:, 0, t:t + 1], conv_w[:, 4, t:t + 1],
                                             ALU.mult, ALU.add))
                for k in range(1, 4):
                    last = nc.vector.scalar_tensor_tensor(dst, xb[:, t, k:k + NP], conv_w[:, k, t:t + 1], dst,
                                                          ALU.mult, ALU.add)
                    if k < 3:
                        link(last)
                return last
            for k in range(4):
                conv((gbuf, csc)[k // 2][:, k % 2, :], SSD_T + k).then_inc(prep_d, 1)
            dve.wait_ge(conv_in, 32)

            def tap(k):
                return conv_w[:, k, :].unsqueeze(2).broadcast_to([P, XBC_T, NS])
            link(nc.vector.tensor_tensor(cdec[:, :, :], sprev[:, :, 0, :], tap(0), ALU.mult))
            for src, k in ((sprev[:, :, 1, :], 1), (sprev[:, :, 2, :], 2), (xb[:, :, 3 + NP:3 + T], 3)):
                link(nc.vector.tensor_tensor(ctmp[:, :, :], src, tap(k), ALU.mult))
                link(nc.vector.tensor_tensor(cdec[:, :, :], cdec[:, :, :], ctmp[:, :, :], ALU.add))
            nc.vector.tensor_tensor(cdec[:, :, :], cdec[:, :, :], tap(4), ALU.add).then_inc(prep_d, 1)
            nc.vector.memset(hin[:, 0, :], 0.0)
            nc.vector.memset(scx[:, 0:2], 0.0)
            link(nc.vector.tensor_scalar(neg[:, :], upto[:, :], -1.0, 1e30, ALU.add, ALU.mult))
            dve.wait_ge(prep_a, 11)
            link(nc.vector.tensor_tensor(xdd[:, :, :], cdec[:, 0:SSD_T, :], dtda[:, :, 0, :], ALU.mult))
            for g in range(GROUPS):
                dve.wait_ge(prep_p, 4 + g)
                nc.vector.tensor_copy(b_tok[:, g, :, :], ps[:, 6 + g, :].rearrange("p (c n) -> p c n", c=CH)
                                      ).then_inc(prep_d, 1)

            for it in range(SC_T):
                g = it // 2
                if it % 2 == 0:
                    for k in range(2):
                        if it or k:
                            dve.wait_ge(bc_spread, 2 * g + k)
                        nc.vector.tensor_tensor(stmp[:, :, :], ident[:, :].unsqueeze(1).broadcast_to([P, NS, P]),
                                                cdec[:, SSD_T + GROUPS * k + g, :].unsqueeze(2).broadcast_to([P, NS, P]),
                                                ALU.mult).then_inc(bc_diag, 1)
                    dve.wait_ge(bc_ready, 2 * g + 2)
                    dve.wait_ge(cb_ready, g + 1)

                def tile_conv(k):
                    if it or k:
                        dve.wait_ge(xs_ready.sem, xs_ready.now(it, 0) if k else xs_ready.before(it, 1))
                    conv(cv[:, :], 2 * it + k).then_inc(conv_ready.sem, 1)

                def tile_xd(k):
                    t = 2 * it + k
                    dve.wait_ge(xs_turned.sem, xs_turned.now(it, k))
                    nc.vector.tensor_tensor(xd[:, :, :].rearrange("p c (h d) -> p c h d", h=2),
                                            ps[:, 4, :].rearrange("p (c h d) -> p c h d", c=CH, h=2),
                                            dt_tok[:, :, 2 * t:2 * t + 2].unsqueeze(3).broadcast_to([P, CH, 2, HD]),
                                            ALU.mult).then_inc(xd_ready.sem, 1)

                def tile_states(k):
                    t = 2 * it + k
                    dve.wait_ge(states_ready.sem, states_ready.now(it, k))
                    if 2 * it + k >= 1:
                        dve.wait_ge(hfin_written[0], 16 * (2 * it + k))
                    ins_ = nc.vector.tensor_copy(hin[:, 1, :], ps[:, 5, 0:P])
                    for c in range(1, CH):
                        link(ins_)
                        for e in range(2):
                            cols = slice(HD * e, HD * e + HD)
                            ins_ = nc.vector.scalar_tensor_tensor(
                                hin[:, c + 1, cols], hin[:, c, cols], ch_dec[:, c, 2 * t + e:2 * t + e + 1],
                                ps[:, 5, P * c + HD * e:P * c + HD * e + HD], ALU.mult, ALU.add)
                    ins_.then_inc(hin_ready.sem, 1)

                def head_seg(k, e):
                    h = 4 * it + 2 * k + e
                    dve.wait_ge(cs_spread.sem, cs_spread.now(it, 2 * k + e))
                    v = gbuf[:, e, :].rearrange("p (c l) -> p c l", c=CH)
                    link(nc.vector.tensor_tensor(v, ps[:, (6, 4)[e], :].rearrange("p (c l) -> p c l", c=CH),
                                                 cs_tok[:, :, h:h + 1].broadcast_to([P, CH, P]), ALU.subtract))
                    nc.vector.scalar_tensor_tensor(v, v, 0.0, neg[:, :].unsqueeze(1).broadcast_to([P, CH, P]),
                                                   ALU.min, ALU.add).then_inc(seg_ready.sem, 1)

                def head_g(k, e):
                    dve.wait_ge(decay_ready.sem, decay_ready.now(it, 2 * k + e))
                    nc.vector.tensor_tensor(gbuf[:, e, :], gbuf[:, e, :], cb[:, :], ALU.mult).then_inc(g_ready.sem, 1)

                def tile_y(k):
                    t = 2 * it + k
                    dve.wait_ge(y_summed.sem, y_summed.now(it, k))
                    link(nc.vector.scalar_tensor_tensor(xs[:, :], xs[:, :], ssd_cols[:, 0, t:t + 1], ps[:, 7, :],
                                                        ALU.mult, ALU.add))
                    nc.vector.tensor_tensor(zs[:, t, 0:NP], zs[:, t, 0:NP], xs[:, :], ALU.mult).then_inc(y_ready.sem, 1)

                def sample_outer(k):
                    t = 2 * it + k
                    nc.vector.tensor_tensor(stmp[:, :, :], bb[:, :, :],
                                            xdd[:, t, :].unsqueeze(2).broadcast_to([P, NS, P]), ALU.mult
                                            ).then_inc(outer_ready.sem, 1)

                def sample_y(k):
                    t = 2 * it + k
                    dve.wait_ge(state_ready.sem, state_ready.now(it, k))
                    link(nc.vector.tensor_tensor(stmp[:, :, :], state[:, k, :, :], cbb[:, :, :], ALU.mult))
                    link(nc.vector.tensor_reduce(ydec[:, :], stmp[:, :, :], AX_X, ALU.add))
                    link(nc.vector.scalar_tensor_tensor(ydec[:, :], cdec[:, t, :], ssd_cols[:, 0, t:t + 1], ydec[:, :],
                                                        ALU.mult, ALU.add))
                    nc.vector.tensor_tensor(zs[:, t, NP:T], zs[:, t, NP:T], ydec[:, :], ALU.mult
                                            ).then_inc(sample_done.sem, 1)

                def sc_unit(j):
                    u, o = U_SSD + 3 * it + j, O_SSD + 3 * it + j
                    wait_unit(dve, u)
                    if j == 0:
                        scaled(halves(silu[:, :]), o).then_inc(acc_read, 1)
                        wait_output(dve, o)
                        link(nc.vector.tensor_tensor(silu[:, :], silu[:, :], rstd[:, :], ALU.mult))
                    elif j == 1:
                        nc.vector.tensor_tensor(halves(scx[:, 2:2 + T]), acc(o), halves(silu[:, :]), ALU.mult
                                                ).then_inc(acc_read, 1)
                        wait_output(dve, o)
                        nc.vector.tensor_copy(sctail[:, it, :], scx[:, NP:2 + T]).then_inc(sc_tail_copied, 1)
                        link(nc.vector.tensor_scalar(prod[:, 0:NP], scx[:, 0:NP], sc_w[:, 0, it:it + 1], None, ALU.mult))
                        for n in range(1, 3):
                            link(nc.vector.scalar_tensor_tensor(prod[:, 0:NP], scx[:, n:n + NP], sc_w[:, n, it:it + 1],
                                                                prod[:, 0:NP], ALU.mult, ALU.add))
                        link(nc.vector.tensor_scalar(prod[:, NP:T], scx[:, 2 + NP:2 + T], sc_w[:, 2, it:it + 1], None,
                                                     ALU.mult))
                        for n in range(2):
                            link(nc.vector.scalar_tensor_tensor(prod[:, NP:T], scprev[:, it, n, :],
                                                                sc_w[:, n, it:it + 1], prod[:, NP:T], ALU.mult, ALU.add))
                        link(nc.vector.tensor_tensor(prod[:, :], prod[:, :], rstd[:, :], ALU.mult))
                    else:
                        nc.vector.tensor_tensor(halves(yb[:, it, :]), acc(o), halves(prod[:, :]), ALU.mult
                                                ).then_inc(acc_read, 1)

                tile_conv(0)
                sample_outer(0)
                tile_xd(0)
                rest_unit(U_SSD + 3 * it + 1, 0, DT)
                head_seg(0, 0)
                sc_unit(0)
                tile_states(0)
                head_g(0, 0)
                rest_unit(U_SSD + 3 * it + 2, 0, DT)
                head_seg(0, 1)
                sc_unit(1)
                head_g(0, 1)
                sample_y(0)
                sample_outer(1)
                tile_conv(1)
                tile_y(0)
                tile_xd(1)
                rest_unit(U_SSD + 3 * it + 3, 0, DT)
                head_seg(1, 0)
                sc_unit(2)
                tile_states(1)
                head_g(1, 0)
                head_seg(1, 1)
                head_g(1, 1)
                sample_y(1)
                tile_y(1)

            def low_y(first, src, n, tiles):
                dve.wait_ge(yhi_ready, n + 1)
                nc.vector.tensor_tensor(y_lo[:, first:first + tiles, :], src,
                                        y_hi[:, first:first + tiles, :].bitcast(F32), ALU.subtract).then_inc(y_split, 1)
            branches_stored(dve)
            nc.vector.drain().then_inc(yprod_ready, 2)
            low_y(8, yb[:, :, :], 0, 4)
            low_y(12, yc[:, :, :], 1, 4)
            for g in range(GROUPS):
                dve.wait_ge(yroot_ready, g + 1)
                inv = (sumsq, prod)[g]
                for t in range(GT * g, GT * g + GT):
                    last = nc.vector.scalar_tensor_tensor(zs[:, t, :], zs[:, t, :], ssd_cols[:, 1, t:t + 1], inv[:, :],
                                                          ALU.mult, ALU.mult)
                last.then_inc(yprod_ready, 1)
                low_y(GT * g, zs[:, GT * g:GT * g + GT, :], 2 + g, GT)

            with dve.Fori(0, DT // 2) as i:
                link.loop(i, 2)
                for c in range(2):
                    for j in range(6):
                        u, o = U_MERGE + 6 * c + j, O_MERGE + 6 * c + j
                        rest_unit(u + 1, 12 * i, MERGE_K[(j + 1) % 6])
                        wait_unit(dve, u, 12 * i)
                        if j % 2 == 0:
                            if j:
                                wait_output(dve, o - 1, 12 * i)
                            else:
                                dve.wait_ge(merged, 2 * i + (c + 1))
                            scaled(halves(silu[:, :]), o).then_inc(acc_read, 1)
                            continue
                        dve.wait_ge(gate_open, 3 * c + j // 2 + 1 + 6 * i)
                        if j == 1:
                            nc.vector.tensor_tensor(halves(prod[:, :]), acc(o), halves(silu[:, :]), ALU.mult
                                                    ).then_inc(acc_read, 1)
                            continue
                        nc.vector.tensor_tensor(halves(silu[:, :]), acc(o), halves(silu[:, :]), ALU.mult
                                                ).then_inc(acc_read, 1)
                        wait_output(dve, o, 12 * i)
                        add = nc.vector.tensor_tensor(prod[:, :], prod[:, :], silu[:, :], ALU.add)
                        if j == 3:
                            link(add)
                        else:
                            add.then_inc(merged, 1)
                    dve.wait_ge(m_hi_ready, 2 * i + (c + 1))
                    nc.vector.tensor_tensor(m_lo[:, ds(2 * i + c, 1), :], prod[:, :].unsqueeze(1),
                                            m_hi[:, ds(2 * i + c, 1), :].bitcast(F32), ALU.subtract).then_inc(m_ready, 1)
            link.end(DT // 2)
            dve.wait_ge(x_back, 16)
            for c in range(DT):
                rest_unit(U_OUT + c + 1, 0, DT)
                wait_unit(dve, U_OUT + c)
                add_to_x(c, O_OUT + c, 1.0, 2)
            invert_rms(2)
            ffn_a(2, U_FFN2A, O_FFN2A)
            ffn_b(2, U_FFN2B, O_FFN2B)

        @block.gpsimd
        def _(pool):
            link = Chain(pool, pool_step)
            link(nc.gpsimd.memset(ones[:, :], 1.0))
            link(nc.gpsimd.memset(ident[:, :], 0.0))
            nc.gpsimd.affine_select(out=ident[:, :], in_=ident[:, :], compare_op=ALU.not_equal, fill=1.0, base=0,
                                    pattern=[[-1, P]], channel_multiplier=1).then_inc(consts_set, 1)
            nc.gpsimd.affine_select(out=upto[:, :], in_=ones[:, :], compare_op=ALU.is_ge, fill=0.0, base=0,
                                    pattern=[[1, P]], channel_multiplier=-1).then_inc(consts_set, 1)
            nc.gpsimd.affine_select(out=after[:, :], in_=ones[:, :], compare_op=ALU.is_ge, fill=0.0, base=-1,
                                    pattern=[[-1, P]], channel_multiplier=1).then_inc(consts_set, 1)

            def add_squares(n):
                for k in range(DT):
                    pool.wait_ge(sq_ready, n * DT + k + 1)
                    if k == 0:
                        nc.gpsimd.tensor_copy(sumsq[:, :], sq[:, :]).then_inc(sumsq_ready, 1)
                    else:
                        pool.wait_ge(sumsq_ready, n * DT + k)
                        nc.gpsimd.tensor_tensor(sumsq[:, :], sumsq[:, :], sq[:, :], ALU.add).then_inc(sumsq_ready, 1)
            add_squares(0)
            pool.wait_ge(stats_ready, 1)
            add_squares(1)

            with pool.Fori(0, NS // 2) as i:
                for b in range(2):
                    pool.wait_ge(qb_ready.sem, qb_ready.now(i, b))
                    pool.wait_ge(page_landed[b], 64 * i + 64)
                    nc.gpsimd.tensor_tensor(pages[:, b, :, :], pages[:, b, :, :],
                                            qb[:, b, :].unsqueeze(1).broadcast_to([P, PAGES, 512]), ALU.mult
                                            ).then_inc(kq_ready.sem, 1)

            pool.wait_ge(pvd_done.sem, pvd_done.now(NS // 2 - 1, 1))
            e2 = expand[:, :, :].rearrange("h t m -> h (t m)")
            link(nc.gpsimd.memset(e2, 1.0))
            link(nc.gpsimd.affine_select(out=e2, in_=e2, compare_op=ALU.is_ge, fill=0.0, base=0,
                                         pattern=[[1, SSD_T * P]], channel_multiplier=-HD))
            nc.gpsimd.affine_select(out=e2, in_=e2, compare_op=ALU.is_ge, fill=0.0, base=HD - 1,
                                    pattern=[[-1, SSD_T * P]], channel_multiplier=HD).then_inc(expand_set, 1)

            def state_ap(dram, t):
                return dram[0, :, 2 * t:2 * t + 2].rearrange("b e p n -> (e p) b n")

            pool.wait_ge(prep_a, 11)
            pool.wait_ge(prep_d, 7)
            for it in range(SC_T):
                g = it // 2
                for k in range(2):
                    if it:
                        pool.wait_ge(state_written[k], 16 * it)
                        pool.wait_ge(sample_done.sem, sample_done.before(it, k))
                    pool.dma_start(state[:, k, :, :], state_ap(ins["state_ssd"], 2 * it + k)).then_inc(state_landed[k], 16)

                def ends(k):
                    t = 2 * it + k
                    pool.wait_ge(xd_ready.sem, xd_ready.now(it, k))
                    if it or k:
                        pool.wait_ge(states_ready.sem, states_ready.now(it, 0) if k else states_ready.before(it, 1))
                    nc.gpsimd.tensor_tensor(xde[:, :, :].rearrange("p c (h d) -> p c h d", h=2),
                                            xd[:, :, :].rearrange("p c (h d) -> p c h d", h=2),
                                            to_end[:, :, 2 * t:2 * t + 2].unsqueeze(3).broadcast_to([P, CH, 2, HD]),
                                            ALU.mult).then_inc(xde_ready.sem, 1)

                def decayed_c(k, e):
                    pool.wait_ge(ecs_ready.sem, ecs_ready.now(it, 2 * k + e))
                    nc.gpsimd.tensor_tensor(csc[:, e, :], csc[:, e, :], ct[:, g, :], ALU.mult).then_inc(csc_ready.sem, 1)

                def sample_state(k):
                    t = 2 * it + k
                    pool.wait_ge(state_landed[k], 16 * (it + 1))
                    link(nc.gpsimd.tensor_tensor(state[:, k, :, :], state[:, k, :, :],
                                                 dtda[:, t, 1, :].unsqueeze(2).broadcast_to([P, NS, P]), ALU.mult))
                    pool.wait_ge(outer_ready.sem, outer_ready.now(it, k))
                    nc.gpsimd.tensor_tensor(state[:, k, :, :], state[:, k, :, :], stmp[:, :, :], ALU.add
                                            ).then_inc(state_ready.sem, 1)
                    pool.wait_ge(state_ready.sem, state_ready.now(it, k))
                    pool.dma_start(state_ap(outs["ssd_s"], t), state[:, k, :, :]).then_inc(state_written[k], 16)

                def final_state(k):
                    t = 2 * it + k
                    pool.wait_ge(hin_ready.sem, hin_ready.now(it, k))
                    pool.dma_start(outs["ssd_p"][:, P * t:P * t + P], hin[:, CH, :]).then_inc(hfin_written[0], 16)

                ends(0)
                decayed_c(0, 0)
                final_state(0)
                sample_state(0)
                decayed_c(0, 1)
                ends(1)
                decayed_c(1, 0)
                final_state(1)
                decayed_c(1, 1)
                sample_state(1)
            pool.wait_ge(hfin_written[0], 16 * SSD_T)
            for k in range(2):
                pool.wait_ge(state_written[k], 16 * SC_T)
            pool.wait_ge(y_split, 4)
            add_squares(2)

        @block.tensor
        def _(pe):
            def stats(n):
                pe.wait_ge(sumsq_ready, DT * (n + 1))
                for h in range(2):
                    mm = nc.tensor.matmul(ps[:, 4 + h, 0:HALF], ones[:, :], sumsq[:, h * HALF:(h + 1) * HALF],
                                          start=True, stop=True)
                mm.then_inc(stats_ready, 1)

            def ffn(n, u_a, o_a, u_b, o_b):
                with pe.Fori(0, FT // 2) as i:
                    for j in range(4):
                        multiply_unit(u_a + j, 4 * i, o_a + j, 4 * i, DT, xg)
                pe.wait_ge(hid_ready, n * FT)
                with pe.Fori(0, 2) as i:
                    for j in range(12):
                        k0, kt = DOWN_K[j % 3]
                        multiply_unit(u_b + j, 12 * i, o_b + j // 3, 4 * i, kt,
                                      lambda k: (hid_hi[:, k0 + k, :], hid_lo[:, k0 + k, :]), j % 3 == 0, j % 3 == 2)

            pe.wait_ge(consts_set, CONSTS)
            stats(0)
            pe.wait_ge(xg_ready, DT)
            ffn(1, U_FFN1A, O_FFN1A, U_FFN1B, O_FFN1B)
            stats(1)
            pe.wait_ge(xg_ready, 2 * DT)
            multiply_unit(U_DT, 0, O_DT, 0, DT, xg)

            with pe.Fori(0, SB_T) as t:
                def unit(j):
                    multiply_unit(U_ATT + j, 8 * t, O_ATT + j, 8 * t, DT, xg)

                def head_sums(k, src):
                    pe.wait_ge(qk_squared.sem, qk_squared.now(t, k))
                    if k == 0:
                        pe.wait_ge(tail_taken.sem, tail_taken.before(t, 1))
                    else:
                        pe.wait_ge(yc_ready.sem, yc_ready.before(t))
                    for h in range(2):
                        mm = nc.tensor.matmul(ps[:, 4 + 2 * k + h, 0:HALF], blocks[:, :],
                                              src[:, h * HALF:(h + 1) * HALF], start=True, stop=True)
                    mm.then_inc(qk_summed.sem, 1)

                def scores(e):
                    pe.wait_ge(qk_normed.sem, qk_normed.now(t, 1))
                    if e:
                        pe.wait_ge(tail_taken.sem, tail_taken.now(t, 0))
                    rows = slice(HD * e, HD * e + HD)
                    for j in range(CH):
                        mm = nc.tensor.matmul(flat[:, 2048 + SCORE_AT[j]:2048 + SCORE_AT[j] + SCORE_W[j]],
                                              kh[rows, P * j:P * j + P], qh[rows, P * j:NP], start=True, stop=True)
                    mm.then_inc(scored.sem, 1)

                def tails(e):
                    pe.wait_ge(sp_ready.sem, sp_ready.now(t, e))
                    for j in range(CH):
                        at = SCORE_AT[j]
                        mm = nc.tensor.matmul(flat[:, 2048 + at:2048 + at + SCORE_W[j]], after[:, :],
                                              spl[:, e, at:at + SCORE_W[j]], start=True, stop=j == CH - 1)
                        for later in range(j + 1, CH):
                            skip = P * (later - j)
                            mm = nc.tensor.matmul(flat[:, 2048 + at + skip:2048 + at + SCORE_W[j]], ones[:, :],
                                                  spl[:, e, SCORE_AT[later]:SCORE_AT[later] + SCORE_W[later]],
                                                  start=False, stop=later == CH - 1)
                    mm.then_inc(tail_summed.sem, 1)

                def values(e):
                    pe.wait_ge(w_ready.sem, w_ready.now(t, e))
                    pe.wait_ge(v_tok_ready.sem, v_tok_ready.now(t))
                    cols = slice(HD * e, HD * e + HD)
                    for j in range(CH):
                        mm = nc.tensor.matmul(ps[cols, 7, P * j:NP], v_tok[:, j, cols],
                                              zb[:, e, SCORE_AT[j]:SCORE_AT[j] + SCORE_W[j]],
                                              start=j == 0, stop=j == CH - 1)
                    mm.then_inc(pv_done.sem, 1)

                unit(0)
                unit(1)
                head_sums(0, sq)
                unit(2)
                head_sums(1, prod)
                wait_output(pe, O_ATT + 2, 8 * t)
                pe.wait_ge(qk_root.sem, qk_root.now(t, 1))
                for c in range(CH):
                    mm = nc.tensor.transpose(ps[:, 7, P * c:P * c + P], vr[:, P * c:P * c + P], ident[:, :])
                mm.then_inc(v_turned.sem, 1)
                unit(3)
                scores(0)
                unit(4)
                tails(0)
                unit(5)
                scores(1)
                values(0)
                unit(6)
                tails(1)
                unit(7)
                values(1)

            with pe.Fori(0, NS // 2) as i:
                for b in range(2):
                    pe.wait_ge(qdiag_ready.sem, qdiag_ready.now(i, b))
                    pe.wait_ge(qb_ready.sem, qb_ready.before(i, b))
                    nc.tensor.matmul(ps[:, 4 + b, :], ones[:, :], qdiag[:, b, :, :].rearrange("p t f -> p (t f)"),
                                     start=True, stop=True).then_inc(qb_spread.sem, 1)
            pe.wait_ge(spd_ready, 1)
            W8 = NS * SB_HEADS
            for g in range(PAGES):
                for later in range(g, PAGES):
                    mm = nc.tensor.matmul(ps[:, 6, W8 * g:W8 * g + W8], (after if later == g else ones)[:, :],
                                          spd[:, later, :, :].rearrange("p b h -> p (b h)"), start=later == g,
                                          stop=later == PAGES - 1)
            mm.then_inc(taild_ready, 1)
            pe.wait_ge(wd_ready, 1)
            pe.wait_ge(yc_ready.sem, yc_ready.now(SB_T - 1))
            with pe.Fori(0, NS // 2) as i:
                for b in range(2):
                    pe.wait_ge(page_landed[b], 64 * i + 64 * (NS // 2 + 1))
                    for t in range(SB_T):
                        for g in range(PAGES):
                            mm = nc.tensor.matmul(ps[:, 7, ds(i * (4 * SB_T) + 2 * (SB_T * b + t), 2)],
                                                  pages[:, b, g, P * t:P * t + P],
                                                  zd[:, g, ds(2 * i + b, 1), 2 * t:2 * t + 2].rearrange("p o h -> p (o h)"),
                                                  start=g == 0, stop=g == PAGES - 1)
                    mm.then_inc(pvd_done.sem, 1)

            R = SSD_HEADS
            pe.wait_ge(prep_d, 3)
            for c in range(CH):
                for bank, src in ((4, dt_t), (5, la_t)):
                    mm = nc.tensor.transpose(ps[:, bank, R * c:R * c + R], src[:, P * c:P * c + P], ident[0:R, 0:R])
            mm.then_inc(prep_p, 1)
            pe.wait_ge(prep_d, 4)
            lt = la_tok[:, :, :].rearrange("p c h -> p (c h)")
            nc.tensor.matmul(ps[:, 6, 0:CH * R], upto[:, :], lt, start=True, stop=True)
            nc.tensor.matmul(ps[:, 7, 0:CH * R], ones[:, :], lt, start=True, stop=True).then_inc(prep_p, 1)
            pe.wait_ge(prep_d, 5)
            for c in range(CH):
                nc.tensor.transpose(ps[0:R, 4, P * c:P * c + P], cs_tok[:, c, :], ident[:, :])
            pe.wait_ge(expand_set, 1)
            pe.wait_ge(prep_a, 4)
            for t in range(SSD_T):
                mm = nc.tensor.matmul(ps[:, 5, 2 * NS * t:2 * NS * t + 2 * NS], expand[:, t, :],
                                      dtda_t[:, :, :].rearrange("p k b -> p (k b)"), start=True, stop=True)
            mm.then_inc(prep_p, 1)
            pe.wait_ge(prep_a, 10)
            for g in range(GROUPS):
                for c in range(CH):
                    mm = nc.tensor.transpose(ps[:, 6 + g, P * c:P * c + P], bt[:, g, P * c:P * c + P], ident[:, :])
                mm.then_inc(prep_p, 1)

            for it in range(SC_T):
                g = it // 2

                def unit(j):
                    multiply_unit(U_SSD + 3 * it + j, 0, O_SSD + 3 * it + j, 0, DT, xg)

                if it % 2 == 0:
                    pe.wait_ge(prep_d, 14)
                    if it:
                        pe.wait_ge(hin_ready.sem, hin_ready.before(it, 1))
                        pe.wait_ge(y_ready.sem, y_ready.before(it, 1))
                    for c in range(CH):
                        cols = slice(P * c, P * c + P)
                        mm = nc.tensor.matmul(ps[:, 5, cols], bt[:, g, cols], ct[:, g, cols], start=True, stop=True)
                    mm.then_inc(cb_made, 1)
                    for k in range(2):
                        pe.wait_ge(bc_diag, 2 * g + k + 1)
                        if k:
                            pe.wait_ge(bc_ready, 2 * g + 1)
                        for half in range(2):
                            mm = nc.tensor.matmul(ps[:, 6 + half, :], ones[:, :],
                                                  stmp[:, 4 * half:4 * half + 4, :].rearrange("p b n -> p (b n)"),
                                                  start=True, stop=True)
                        mm.then_inc(bc_spread, 1)
                    pe.wait_ge(bc_ready, 2 * g + 2)
                    pe.wait_ge(cb_ready, g + 1)

                def turn(k):
                    pe.wait_ge(xs_ready.sem, xs_ready.now(it, k))
                    if it or k:
                        head = (it, 1) if k else (it - 1, 3)
                        pe.wait_ge(g_ready.sem, g_ready.now(*head))
                        pe.wait_ge(csc_ready.sem, csc_ready.now(*head))
                    for c in range(CH):
                        mm = nc.tensor.transpose(ps[:, 4, P * c:P * c + P], xs[:, P * c:P * c + P], ident[:, :])
                    mm.then_inc(xs_turned.sem, 1)

                def chunk_states(k):
                    pe.wait_ge(xde_ready.sem, xde_ready.now(it, k))
                    if k:
                        pe.wait_ge(hin_ready.sem, hin_ready.now(it, 0))
                    elif it:
                        pe.wait_ge(hin_ready.sem, hin_ready.before(it, 1))
                    for c in range(CH):
                        mm = nc.tensor.matmul(ps[:, 5, P * c:P * c + P], b_tok[:, g, c, :], xde[:, c, :], start=True,
                                              stop=True)
                    mm.then_inc(states_ready.sem, 1)

                def spread(k, e):
                    pe.wait_ge(head_cs_ready.sem, head_cs_ready.now(it, 2 * k + e))
                    if e:
                        pe.wait_ge(xd_ready.sem, xd_ready.now(it, k))
                    elif k or it:
                        head = (it, 0) if k else (it - 1, 2)
                        pe.wait_ge(g_ready.sem, g_ready.now(*head))
                        pe.wait_ge(csc_ready.sem, csc_ready.now(*head))
                    nc.tensor.matmul(ps[:, (6, 4)[e], :], ones[0:R, :], head_cs, start=True, stop=True
                                     ).then_inc(cs_spread.sem, 1)

                def outputs(k, e):
                    pe.wait_ge(g_ready.sem, g_ready.now(it, 2 * k + e))
                    pe.wait_ge(csc_ready.sem, csc_ready.now(it, 2 * k + e))
                    pe.wait_ge(hin_ready.sem, hin_ready.now(it, k))
                    if e == 0 and k:
                        pe.wait_ge(y_ready.sem, y_ready.now(it, 0))
                    elif e == 0 and it:
                        pe.wait_ge(y_ready.sem, y_ready.before(it, 1))
                    rows = slice(HD * e, HD * e + HD)
                    for c in range(CH):
                        cols = slice(P * c, P * c + P)
                        nc.tensor.matmul(ps[rows, 7, cols], xd[:, c, rows], gbuf[:, e, cols], start=True, stop=False)
                        mm = nc.tensor.matmul(ps[rows, 7, cols], hin[:, c, rows], csc[:, e, cols], start=False,
                                              stop=True)
                    if e:
                        mm.then_inc(y_summed.sem, 1)

                turn(0)
                spread(0, 0)
                unit(0)
                chunk_states(0)
                spread(0, 1)
                unit(1)
                outputs(0, 0)
                outputs(0, 1)
                turn(1)
                spread(1, 0)
                unit(2)
                chunk_states(1)
                spread(1, 1)
                outputs(1, 0)
                outputs(1, 1)

            for t in range(SSD_T):
                g = t // GT
                pe.wait_ge(ysq_ready, t + 1)
                for h in range(2):
                    mm = nc.tensor.matmul(ps[:, 4 + 2 * g + h, 0:HALF], ones[:, :],
                                          (sq, silu)[t % 2][:, h * HALF:(h + 1) * HALF], start=t % GT == 0,
                                          stop=t % GT == GT - 1)
                mm.then_inc(ysum_ready, 1)
            pe.wait_ge(y_split, 4)
            with pe.Fori(0, DT // 2) as i:
                for c in range(2):
                    for j in range(6):
                        first = (0, 0, 0, 8, 0, 12)[j]
                        rhs = xg if j % 2 == 0 else (lambda k: (y_hi[:, first + k, :], y_lo[:, first + k, :]))
                        multiply_unit(U_MERGE + 6 * c + j, 12 * i, O_MERGE + 6 * c + j, 12 * i, MERGE_K[j], rhs)
            pe.wait_ge(m_ready, DT)
            with pe.Fori(0, 2) as i:
                for j in range(4):
                    multiply_unit(U_OUT + j, 4 * i, O_OUT + j, 4 * i, DT, lambda k: (m_hi[:, k, :], m_lo[:, k, :]))
            stats(2)
            pe.wait_ge(xg_ready, 3 * DT)
            ffn(2, U_FFN2A, O_FFN2A, U_FFN2B, O_FFN2B)


def kernel(**inputs):
    import numpy as np
    import concourse.bacc as bacc
    from concourse.bass_utils import run_bass_kernel_spmd as run

    a = {k: np.asarray(v) for k, v in inputs.items()}

    def cols(v):
        return v.reshape(-1, P).T

    def flat(parts):
        return np.ascontiguousarray(np.stack(parts, 1))
    tok = np.concatenate([a["x_prompt"].reshape(-1, D), a["x_sample"].reshape(-1, D)], 0)
    laid = {
        "x_t": np.ascontiguousarray(tok.T.reshape(DT, P, T).transpose(1, 0, 2)),
        "norms": flat([cols(a["ffn1_norm"]), cols(a["mix_norm"]), cols(a["ffn2_norm"])]),
        "gate_b": np.ascontiguousarray(cols(a["gate_bias"])),
        "conv_w": flat([cols(a["ssd_conv_w"][0, k]) for k in range(4)] + [cols(a["ssd_conv_b"])]),
        "sc_w": flat([cols(a["sc_conv_w"][0, k]) for k in range(3)]),
        "qk_g": np.ascontiguousarray(np.stack([np.tile(a["sb_q_norm"][0], 2), np.tile(a["sb_k_norm"][0], 2)], 1)),
        "ssd_cols": flat([cols(np.repeat(a["ssd_d"][0], HD)), cols(a["ssd_norm"])]),
        "ssd_rows": np.ascontiguousarray(np.stack([a["ssd_dt_bias"][0], a["ssd_a_log"][0]], 1)),
        "table": a["page_table"].reshape(1, -1),
        "sb_bias": a["sb_logit_bias"].reshape(-1),
        "ssd_prev": np.ascontiguousarray(a["state_ssd_conv"][0].reshape(NS, 3, XBC_T, P).transpose(3, 2, 1, 0)),
        "sc_prev": np.ascontiguousarray(a["state_sc_conv"][0].reshape(NS, 2, SC_T, P).transpose(3, 2, 1, 0)),
    }
    for name in ("cache_sb_k", "cache_sb_v", "state_ssd", "ffn1_w_gate", "ffn1_w_up", "ffn1_w_down", "w_in",
                 "w_proj_a", "w_proj_b", "w_proj_c", "w_out", "ffn2_w_gate", "ffn2_w_up", "ffn2_w_down"):
        laid[name] = a[name]
    shapes = {"y_t": (P, DT, T), "k_t": (P, SB_T, T), "v_t": (P, SB_T, T), "ssd_p": (P, SSD_T * P),
              "ssd_s": (1, NS, SSD_HEADS, HD, P), "ssd_conv_p": (P, XBC_T, 3), "ssd_conv_s": (P, XBC_T, 3, NS),
              "sc_conv_p": (P, SC_T, 2), "sc_conv_s": (P, SC_T, 2, NS)}
    nc = bacc.Bacc("TRN2", target_bir_lowering=False, num_devices=1)
    ins = {k: nc.dram_tensor("in_" + k, v.shape, mybir.dt.from_np(v.dtype), kind="ExternalInput").ap()
           for k, v in laid.items()}
    outs = {k: nc.dram_tensor("out_" + k, s, F32, kind="ExternalOutput").ap() for k, s in shapes.items()}
    build(nc, ins, outs)
    r = run(nc, [{"in_" + k: v for k, v in laid.items()}], core_ids=[0]).results[0]

    def tokens(name):
        v = r["out_" + name].transpose(2, 1, 0).reshape(T, -1)
        return v[:NP], v[NP:]
    (yp, ys), (kp, ks), (vp, vs) = tokens("y_t"), tokens("k_t"), tokens("v_t")
    return (yp.reshape(1, NP, D), ys.reshape(NS, 1, D),
            kp.reshape(1, 1, NP, SB_HEADS, HD), vp.reshape(1, 1, NP, SB_HEADS, HD),
            ks.reshape(1, NS, 1, SB_HEADS, HD), vs.reshape(1, NS, 1, SB_HEADS, HD),
            r["out_ssd_p"].T.reshape(1, 1, SSD_HEADS, HD, P), r["out_ssd_s"],
            r["out_ssd_conv_p"].transpose(2, 1, 0).reshape(1, 1, 3, XBC_T * P),
            r["out_ssd_conv_s"].transpose(3, 2, 1, 0).reshape(1, NS, 3, XBC_T * P),
            r["out_sc_conv_p"].transpose(2, 1, 0).reshape(1, 1, 2, SC_T * P),
            r["out_sc_conv_s"].transpose(3, 2, 1, 0).reshape(1, NS, 2, SC_T * P))
```

```python
from contextlib import ExitStack

import concourse.bass as bass
from concourse import mybir

F32 = mybir.dt.float32
F32R = mybir.dt.float32r
I32 = mybir.dt.int32
ALU = mybir.AluOpType
ACT = mybir.ActivationFunctionType
AX_X = mybir.AxisListType.X
ds = bass.ds

P = 128
D = 1024
NP = 512
NS = 8
T = NP + NS
HALF = T // 2
DT = D // P
D_FF = 2816
FT = D_FF // P
EPS = 1e-6
HD = 64
SB_HEADS = 8
SB_T = SB_HEADS * HD // P
PAGES = 4
SSD_HEADS = 16
SSD_T = SSD_HEADS * HD // P
GROUPS = 2
GT = SSD_T // GROUPS
CH = NP // P
XBC_T = SSD_T + 2 * GROUPS
SC_T = 4

COL_GATE = 0
COL_Z = 3 * D
COL_XBC = COL_Z + D
COL_DT = COL_XBC + XBC_T * P
COL_SCB = COL_DT + SSD_HEADS
COL_SCC = COL_SCB + SC_T * P
COL_SCX = COL_SCC + SC_T * P
COL_Q = COL_SCX + SC_T * P
COL_K = COL_Q + SB_T * P
COL_V = COL_K + SB_T * P

KMAX = 8
STAGES = 4
SPLITS = 2
DOWN_K = [(0, 8), (8, 7), (15, 7)]
GATES = 3 * DT
G_PRE, G_K, G_V, G_POST = 4, NS, NS, 2
G_PREP = GATES - G_PRE - G_K - G_V - G_POST
G0_PREP = G_PRE + G_K
G0_V = G0_PREP + G_PREP
GATE_SLOTS = 4
SLOTS = 4

U_FFN1A, O_FFN1A = 0, 0
U_FFN1B, O_FFN1B = 2 * FT, 2 * FT
U_DT, O_DT = U_FFN1B + 3 * DT, O_FFN1B + DT
U_ATT, O_ATT = U_DT + 1, O_DT + 1
U_GATE, O_GATE = U_ATT + 8 * SB_T, O_ATT + 8 * SB_T
U_SSD, O_SSD = U_GATE + GATES - G_POST, O_GATE + GATES - G_POST
U_POST, O_POST = U_SSD + 3 * SC_T, O_SSD + 3 * SC_T
U_MERGE, O_MERGE = U_POST + G_POST, O_POST + G_POST
U_MERGE_A, O_MERGE_A = U_MERGE + DT, O_MERGE + 2 * DT
U_OUT, O_OUT = U_MERGE_A + DT, O_MERGE_A + DT
U_FFN2A, O_FFN2A = U_OUT + DT, O_OUT + DT
U_FFN2B, O_FFN2B = U_FFN2A + 2 * FT, O_FFN2A + 2 * FT
U_END = U_FFN2B + 3 * DT

SCORE_AT = [0, 512, 1024, 896]
SCORE_W = [512, 384, 256, 128]
SCORES = 1280
SCORE_PARTS = (slice(0, 640), slice(640, SCORES))
CONSTS = 6


class Signal:

    def __init__(self, sem, n):
        self.sem, self.n = sem, n

    def now(self, i, k=0):
        return self.n * i + (self.n + k + 1)

    def before(self, i, k=0):
        return self.n * i + (k + 1)


class Chain:

    def __init__(self, eng, sem):
        self.eng, self.sem, self.n, self.step = eng, sem, 0, 0

    def __call__(self, ins):
        ins.then_inc(self.sem, 1)
        self.n += 1
        self.eng.wait_ge(self.sem, self.n + self.step)

    def loop(self, i, per):
        self.step, self.first, self.per = per * i, self.n, per

    def end(self, turns):
        assert self.n == self.first + self.per, (self.n - self.first, self.per)
        self.step, self.n = 0, self.first + self.per * turns


def build(nc, ins, outs):
    ctx = ExitStack()
    with ctx:
        def sb(name, shape, dt=F32):
            return ctx.enter_context(nc.sbuf_tensor(name, shape, dt))

        def sem(name):
            return ctx.enter_context(nc.semaphore(name))

        ARENA = 128 * 1024
        arena_at = (nc.sbuf_base + 31) // 32 * 32
        arena = sb("arena", [P, ARENA // 4])
        xg_hi = sb("xg_hi", [P, DT, T], F32R)
        xg_lo = sb("xg_lo", [P, DT, T], F32R)
        stage = sb("stage", [P, STAGES, KMAX, P])
        w_hi = sb("w_hi", [P, SPLITS, KMAX, P], F32R)
        w_lo = sb("w_lo", [P, SPLITS, KMAX, P], F32R)
        rstd = sb("rstd", [P, T])
        sumsq = sb("sumsq", [P, T])
        sq = sb("sq", [P, T])
        silu = sb("silu", [P, T])
        prod = sb("prod", [P, T])
        ones = sb("ones", [P, P])
        ident = sb("ident", [P, P])
        upto = sb("upto", [P, P])
        after = sb("after", [P, P])
        blocks = sb("blocks", [P, P])
        norms = sb("norms", [P, 3, DT])
        gate_b = sb("gate_b", [P, 3 * DT])
        conv_w = sb("conv_w", [P, 5, XBC_T])
        sc_w = sb("sc_w", [P, 3, SC_T])
        qk_g = sb("qk_g", [P, 2])
        sb_bias = sb("sb_bias", [P, SB_HEADS])
        ssd_cols = sb("ssd_cols", [P, 2, SSD_T])
        ssd_rows = sb("ssd_rows", [SSD_HEADS, 2])
        eps = sb("eps", [P, 1])
        one = sb("one", [P, 1])
        table = sb("table", [1, NS * PAGES], I32)
        ps = ctx.enter_context(nc.psum_tensor("ps", [P, 8, 512], F32))
        flat = ps[:, :, :].rearrange("p b c -> p (b c)")

        def plan(at, *tenants):
            made = []
            for name, shape, dt in tenants:
                size = 4
                for n in shape[1:]:
                    size *= n
                made.append(nc.alloc_sbuf_tensor_at(name, shape, dt, offset=arena_at + at))
                at += (size + 31) // 32 * 32
            assert at <= ARENA, (tenants[0][0], at, ARENA)
            return made + [at]
        x, after_x = plan(0, ("x", [P, DT, T], F32))
        hid_hi, hid_lo, _ = plan(after_x, ("hid_hi", [P, FT, T], F32R), ("hid_lo", [P, FT, T], F32R))
        m_hi, m_lo, y_hi, y_lo, _ = plan(ARENA - 4 * T * 48, ("m_hi", [P, DT, T], F32R), ("m_lo", [P, DT, T], F32R),
                                         ("y_hi", [P, 16, T], F32R), ("y_lo", [P, 16, T], F32R))
        part, _ = plan(ARENA - 4 * T * 40, ("part", [P, DT, T], F32))
        gates, end_gates = plan(after_x, ("gates", [P, GATE_SLOTS, T], F32))
        assert end_gates <= ARENA - 4 * T * 48
        zs, yc, yb, xb, qdec, dt_t, la_t, end_branch = plan(
            0, ("zs", [P, SSD_T, T], F32), ("yc", [P, SB_T, T], F32), ("yb", [P, SC_T, T], F32),
            ("xb", [P, XBC_T, 3 + T], F32), ("qdec", [P, SB_T, NS], F32), ("dt_t", [SSD_HEADS, T], F32),
            ("la_t", [SSD_HEADS, T], F32))
        ysq, ysum, _ = plan(4 * T * (SSD_T + SB_T + SC_T), ("ysq", [P, 2, T], F32), ("ysum", [P, GROUPS, T], F32))
        qr, kr, vr, qh, kh, v_tok, zb, lg, spl, strict, _ = plan(
            end_branch, ("qr", [P, T], F32), ("kr", [P, T], F32), ("vr", [P, T], F32), ("qh", [P, T], F32),
            ("kh", [P, T], F32), ("v_tok", [P, CH, P], F32), ("zb", [P, 2, SCORES], F32),
            ("lg", [P, 2, SCORES], F32), ("spl", [P, 2, SCORES], F32), ("strict", [P, P], F32))
        pages, q_row, qb, zd, lgd, spd, end_sample = plan(
            end_branch, ("pages", [P, SLOTS, PAGES, 512], F32), ("q_row", [SB_T * NS, P], F32),
            ("qb", [P, SB_T, NS, P], F32), ("zd", [P, PAGES, NS, SB_HEADS], F32),
            ("lgd", [P, PAGES, NS, SB_HEADS], F32), ("spd", [P, PAGES, NS, SB_HEADS], F32))
        expand, own, own_v, token_rows, wd4, at_ = plan(
            end_sample - 4 * 3 * 256 - 4 * NS * 512, ("expand", [SSD_HEADS, SSD_T, P], F32),
            ("own", [P, SB_HEADS, HD], F32), ("own_v", [P, NS // SLOTS, SB_HEADS * HD], F32),
            ("token_rows", [P, SLOTS], F32), ("wd4", [P, PAGES, SLOTS * SB_HEADS], F32))
        assert at_ <= end_sample - 4 * 3 * 256
        (bt, ct, dt_tok, la_tok, cs_tok, to_end, ch_dec, cs_t, sprev, scprev, cdec, ctmp, dtda, dtda_t, xdd, bc_row,
         _) = plan(
            end_sample, ("bt", [P, GROUPS, NP], F32), ("ct", [P, GROUPS, NP], F32),
            ("dt_tok", [P, CH, SSD_HEADS], F32), ("la_tok", [P, CH, SSD_HEADS], F32),
            ("cs_tok", [P, CH, SSD_HEADS], F32), ("to_end", [P, CH, SSD_HEADS], F32),
            ("ch_dec", [P, CH, SSD_HEADS], F32), ("cs_t", [SSD_HEADS, T], F32),
            ("sprev", [P, XBC_T, 3, NS], F32), ("scprev", [P, SC_T, 2, NS], F32), ("cdec", [P, XBC_T, NS], F32),
            ("ctmp", [P, XBC_T, NS], F32), ("dtda", [P, SSD_T, 2, NS], F32), ("dtda_t", [SSD_HEADS, 2, NS], F32),
            ("xdd", [P, SSD_T, NS], F32), ("bc_row", [2 * GROUPS * NS, P], F32))
        (b_tok, cb, xd, xde, hin, gbuf, csc, state, stmp, outer, bb, cbb, ydec, scx, sctail, end_ssd) = plan(
            end_branch, ("b_tok", [P, GROUPS, CH, P], F32), ("cb", [P, GROUPS, NP], F32),
            ("xd", [P, 2, CH, P], F32), ("xde", [P, CH, P], F32),
            ("hin", [P, CH + 1, P], F32), ("gbuf", [P, 2, NP], F32), ("csc", [P, 2, NP], F32),
            ("state", [P, 2, NS, P], F32), ("stmp", [P, NS, P], F32), ("outer", [P, NS, P], F32), ("bb", [P, NS, P], F32),
            ("cbb", [P, NS, P], F32), ("ydec", [P, NS], F32), ("scx", [P, 2 + T], F32),
            ("sctail", [P, SC_T, 2 + NS], F32))
        assert end_ssd <= end_sample
        head_cs = la_t[:, 0:NP], dt_t[:, 0:NP]

        def x_tile(t):
            return xb[:, t, 0:NP]
        x_kept = nc.dram_tensor("x_kept", (P, DT, T), F32, kind="Internal").ap()
        bc_kept = nc.dram_tensor("bc_kept", (2 * GROUPS * NS, P), F32, kind="Internal").ap()
        q_kept = nc.dram_tensor("q_kept", (SB_T * NS, P), F32, kind="Internal").ap()
        gates_kept = nc.dram_tensor("gates_kept", (P, GATES, T), F32, kind="Internal").ap()

        row_e, row_s, row_l = sq[0:SSD_HEADS, :], sumsq[0:SSD_HEADS, :], cs_t[:, :]

        def acc(o):
            return ps[:, 2 * (o % 2):2 * (o % 2) + 2, 0:HALF]

        def halves(ap):
            return ap.rearrange("p (a b) -> p a b", a=2)

        landed = sem("landed")
        norms_landed = sem("norms_landed")
        x_landed = [sem(f"x_landed{k}") for k in range(DT)]
        consts_set = sem("consts_set")
        w_landed = [sem(f"w_landed{s}") for s in range(STAGES)]
        unit_split = sem("unit_split")
        hi_ready = sem("hi_ready")
        unit_done = sem("unit_done")
        acc_read = sem("acc_read")
        silu_ready = sem("silu_ready")
        silu_scaled = sem("silu_scaled")
        hid_hi_ready = sem("hid_hi_ready")
        hid_ready = sem("hid_ready")
        xg_hi_ready = sem("xg_hi_ready")
        xg_ready = sem("xg_ready")
        sq_ready = sem("sq_ready")
        sumsq_ready = sem("sumsq_ready")
        stats_ready = sem("stats_ready")
        rms_ready = sem("rms_ready")
        rstd_ready = sem("rstd_ready")
        x_saved = sem("x_saved")
        x_back = sem("x_back")
        out_written = sem("out_written")
        dve_step = sem("dve_step")
        act_step = sem("act_step")
        pool_step = sem("pool_step")
        signals = []

        def signal(name, n):
            signals.append(Signal(sem(name), n))
            return signals[-1]
        qk_squared = signal("qk_squared", 2)
        qk_summed = signal("qk_summed", 2)
        qk_root = signal("qk_root", 2)
        qk_normed = signal("qk_normed", 2)
        kv_written = sem("kv_written")
        v_turned = signal("v_turned", 1)
        v_tok_ready = signal("v_tok_ready", 1)
        scored = signal("scored", 2)
        z_biased = signal("z_biased", 4)
        log_ready = signal("log_ready", 4)
        sp_ready = signal("sp_ready", 2)
        tail_summed = signal("tail_summed", 2)
        tail_taken = signal("tail_taken", 2)
        w_exped = signal("w_exped", 2)
        w_ready = signal("w_ready", 2)
        pv_done = signal("pv_done", 2)
        yc_ready = signal("yc_ready", 1)
        page_landed = [sem(f"page_landed{b}") for b in range(SLOTS)]
        q_turned = sem("q_turned")
        q_row_ready = sem("q_row_ready")
        q_row_kept = sem("q_row_kept")
        qb_landed = sem("qb_landed")
        pages_used = signal("pages_used", SLOTS)
        kq_ready = signal("kq_ready", SLOTS)
        gate_kept = [sem("gate_kept0"), sem("gate_kept1")]
        spd_ready = sem("spd_ready")
        zd_ready = sem("zd_ready")
        lgd_ready = sem("lgd_ready")
        taild_ready = sem("taild_ready")
        wd_raw = sem("wd_raw")
        wd_ready = sem("wd_ready")
        wd4_ready = signal("wd4_ready", 1)
        own_set = sem("own_set")
        own_v_ready = sem("own_v_ready")
        v_summed = sem("v_summed")
        pvd_done = signal("pvd_done", SLOTS)
        expand_set = sem("expand_set")
        bc_conved = sem("bc_conved")
        b_turned = sem("b_turned")
        b_tok_ready = sem("b_tok_ready")
        cb_made = sem("cb_made")
        cb_ready = sem("cb_ready")
        yc_sampled = sem("yc_sampled")
        bc_turned = sem("bc_turned")
        bc_row_ready = sem("bc_row_ready")
        bc_row_kept = sem("bc_row_kept")
        bc_landed = [sem("b_landed"), sem("c_landed")]
        prep_d = sem("prep_d")
        prep_a = sem("prep_a")
        s_used = sem("s_used")
        inverse_ready = sem("inverse_ready")
        prep_p = sem("prep_p")
        conv_in = sem("conv_in")
        zs_ready = sem("zs_ready")
        cdec_conved = sem("cdec_conved")
        xdd_ready = sem("xdd_ready")
        ssd_written = sem("ssd_written")
        conv_ready = signal("conv_ready", SLOTS)
        xs_ready = signal("xs_ready", SLOTS)
        xs_turned = signal("xs_turned", 2)
        xd_ready = signal("xd_ready", 2)
        xde_ready = signal("xde_ready", 2)
        states_ready = signal("states_ready", 2)
        hin_ready = signal("hin_ready", 2)
        hfin_written = [sem("hfin_written0"), sem("hfin_written1")]
        head_cs_ready = signal("head_cs_ready", 4)
        cs_spread = signal("cs_spread", 4)
        seg_ready = signal("seg_ready", 4)
        decay_ready = signal("decay_ready", 4)
        ecs_ready = signal("ecs_ready", 4)
        csc_ready = signal("csc_ready", 4)
        g_ready = signal("g_ready", 4)
        y_summed = signal("y_summed", 2)
        y_ready = signal("y_ready", 2)
        state_landed = [sem("state_landed0"), sem("state_landed1")]
        state_written = [sem("state_written0"), sem("state_written1")]
        state_ready = signal("state_ready", 2)
        sample_done = signal("sample_done", 2)
        ysq_ready = sem("ysq_ready")
        ysum_ready = sem("ysum_ready")
        ysum_spread = sem("ysum_spread")
        yroot_ready = sem("yroot_ready")
        yhi_ready = sem("yhi_ready")
        yprod_ready = sem("yprod_ready")
        y_split = sem("y_split")
        gate_landed = [sem(f"gate_landed{b}") for b in range(GATE_SLOTS)]
        gate_open = sem("gate_open")
        b_done = sem("b_done")
        part_made = sem("part_made")
        merged = sem("merged")
        m_hi_ready = sem("m_hi_ready")
        m_ready = sem("m_ready")

        def kpm(w):
            return w.rearrange("l (k p) m -> (l p) k m", p=P)
        w = {n: kpm(ins[n]) for n in ("ffn1_w_gate", "ffn1_w_up", "ffn1_w_down", "w_in", "w_proj_a", "w_proj_bc", "w_out",
                                      "ffn2_w_gate", "ffn2_w_up", "ffn2_w_down")}

        def load_unit(u0, step, src, kt):
            s = u0 % STAGES
            nc.sync.wait_ge(unit_split, u0 + 1 + step)
            nc.sync.dma_start(stage[:, s, 0:kt, :], src).then_inc(w_landed[s], 16)

        def round_unit(u0, step, kt):
            s, r = u0 % STAGES, u0 % SPLITS
            nc.scalar.wait_ge(w_landed[s], 16 * (u0 // STAGES + 1) + 16 // STAGES * step)
            nc.scalar.wait_ge(unit_done, u0 + 1 + step)
            nc.scalar.activation(w_hi[:, r, 0:kt, :], stage[:, s, 0:kt, :], ACT.Copy).then_inc(hi_ready, 1)

        def rest_unit(u0, step, kt):
            s, r = u0 % STAGES, u0 % SPLITS
            nc.vector.wait_ge(hi_ready, u0 + 1 + step)
            nc.vector.tensor_tensor(w_lo[:, r, 0:kt, :], stage[:, s, 0:kt, :], w_hi[:, r, 0:kt, :].bitcast(F32),
                                    ALU.subtract).then_inc(unit_split, 1)

        def multiply_unit(u0, step, o0, ostep, kt, rhs, start=True, stop=True, ready=None):
            r = u0 % SPLITS
            out = acc(o0)
            if start:
                nc.tensor.wait_ge(acc_read, o0 + 1 + ostep)
            nc.tensor.wait_ge(unit_split, STAGES + u0 + 1 + step)
            for k in range(kt):
                hi, lo = rhs(k)
                if ready:
                    nc.tensor.wait_ge(*ready(k))
                for n, (wt, v) in enumerate(((w_hi, hi), (w_hi, lo), (w_lo, hi))):
                    for h in range(2):
                        mm = nc.tensor.matmul(out[:, h, :], wt[:, r, k, :], v[:, h * HALF:(h + 1) * HALF],
                                              start=start and k == 0 and n == 0,
                                              stop=stop and k == kt - 1 and n == 2)
            mm.then_inc(unit_done, 1)

        def evac_buffer(g):
            return (silu, prod)[g % 2]

        def take_gate(u0, o0, g, step=0):
            nc.vector.wait_ge(gate_kept[g % 2], 16 * (g // 2 + 1) + 8 * step)
            wait_unit(nc.vector, u0, step)
            nc.vector.tensor_tensor(halves(evac_buffer(g)[:, :]), acc(o0), halves(rstd[:, :]), ALU.mult
                                    ).then_inc(acc_read, 1)

        def keep_gate(o0, g, step=0):
            wait_output(nc.scalar, o0, step)
            nc.scalar.dma_start(gates_kept[:, ds(step + g, 1), :], evac_buffer(g)[:, :].unsqueeze(1)
                                ).then_inc(gate_kept[g % 2], 16)

        def gates_stored(eng, count):
            for b in range(2):
                eng.wait_ge(gate_kept[b], 16 + 8 * count)

        def xg(k):
            return xg_hi[:, k, :], xg_lo[:, k, :]

        def wait_unit(dve, u0, step=0):
            dve.wait_ge(unit_done, SPLITS + u0 + 1 + step)

        def wait_output(eng, o0, step=0):
            eng.wait_ge(acc_read, 2 + o0 + 1 + step)

        sc_gated = sem("sc_gated")
        sc_tail_copied = sem("sc_tail_copied")

        def wait_sctail(eng):
            eng.wait_ge(sc_tail_copied, SC_T)

        def branches_stored(eng):
            for written in state_written:
                eng.wait_ge(written, 16 * SC_T)
            eng.wait_ge(hfin_written[0], 16 * SSD_T)
            eng.wait_ge(out_written, 96)

        w_in_att = [COL_Q, COL_K, COL_V, COL_Z, COL_Z + P, COL_XBC, COL_XBC + P, COL_XBC + 2 * P]
        w_in_step = [P, P, P, 2 * P, 2 * P, 3 * P, 3 * P, 3 * P]

        block = ctx.enter_context(nc.Block())

        @block.sync
        def _(sp):
            for s in signals:
                sp.sem_inc(s.sem, s.n)
            sp.sem_inc(kv_written, 32)
            for kept in gate_kept:
                sp.sem_inc(kept, 16)
            load_unit(0, 0, w["ffn1_w_gate"][:, :, 0:P], DT)
            sp.dma_start(norms[:, :, :], ins["norms"]).then_inc(norms_landed, 16)
            for k in range(DT):
                sp.dma_start(x[:, k, :], ins["x_t"][:, k, :]).then_inc(x_landed[k], 16)

            def ffn_loads(n, u_a, u_b):
                wg, wu, wd = w[f"ffn{n}_w_gate"], w[f"ffn{n}_w_up"], w[f"ffn{n}_w_down"]
                for j in range(n == 1, 4):
                    load_unit(u_a + j, 0, (wg, wu)[j % 2][:, :, j // 2 * P:j // 2 * P + P], DT)
                with sp.Fori(0, FT // 2 - 1) as i:
                    for j in range(4):
                        load_unit(u_a + 4 + j, 4 * i, (wg, wu)[j % 2][:, :, ds((i * 2 + j // 2 + 2) * P, P)], DT)
                with sp.Fori(0, 2) as i:
                    for j in range(12):
                        k0, kt = DOWN_K[j % 3]
                        load_unit(u_b + j, 12 * i, wd[:, k0:k0 + kt, ds((i * 4 + j // 3) * P, P)], kt)
            ffn_loads(1, U_FFN1A, U_FFN1B)
            load_unit(U_DT, 0, w["w_in"][:, :, COL_DT:COL_DT + P], DT)
            with sp.Fori(0, SB_T) as t:
                for j in range(8):
                    load_unit(U_ATT + j, 8 * t, w["w_in"][:, :, ds(t * w_in_step[j] + w_in_att[j], P)], DT)
                    if j == 5:
                        sp.wait_ge(qk_normed.sem, qk_normed.now(t, 1))
                        sp.dma_start(outs["k_t"][:, ds(t, 1), :], kh[:, :].unsqueeze(1)).then_inc(kv_written, 16)
                        sp.dma_start(outs["v_t"][:, ds(t, 1), :], vr[:, :].unsqueeze(1)).then_inc(kv_written, 16)

            def load_gate(g, step=0, first=U_GATE):
                load_unit(first + g, step, w["w_in"][:, :, ds(step * P + g * P, P)], DT)

            def load_sc(n):
                col = (COL_SCC, COL_SCX, COL_SCB)[n % 3] + n // 3 * P
                load_unit(U_SSD + n, 0, w["w_in"][:, :, col:col + P], DT)

            def load_pages(cache, i, b):
                for p in range(PAGES):
                    page = sp.value_load(table[0:1, ds(i * (SLOTS * PAGES) + b * PAGES + p, 1)], min_val=0,
                                         max_val=cache.shape[1] - 1)
                    sp.dma_start(pages[:, b, p, :], cache[0, ds(page, 1)].rearrange("o t h d -> (o t) (h d)")
                                 ).then_inc(page_landed[b], 16)

            sp.wait_ge(landed, 8 * 16)
            AHEAD = 4
            for g in range(AHEAD):
                load_gate(g)
            sp.wait_ge(q_row_ready, 1)
            sp.dma_start(q_kept, q_row[:, :]).then_inc(q_row_kept, 16)
            sp.wait_ge(yc_ready.sem, yc_ready.now(SB_T - 1))
            sp.dma_start(sprev[:, :, :, :], ins["ssd_prev"]).then_inc(conv_in, 16)
            sp.dma_start(scprev[:, :, :, :], ins["sc_prev"]).then_inc(conv_in, 16)
            sp.wait_ge(kv_written, 32 * SB_T + 32)
            sp.wait_ge(q_row_kept, 16)
            sp.dma_start(qb[:, :, :, :].rearrange("p t b f -> p (t b f)"),
                         q_kept.rearrange("r f -> (r f)").partition_broadcast(P)).then_inc(qb_landed, 16)
            with sp.Fori(0, NS // SLOTS) as i:
                for b in range(SLOTS):
                    sp.wait_ge(pages_used.sem, pages_used.before(i, b))
                    load_pages(ins["cache_sb_k"], i, b)
                    load_gate(AHEAD + b, SLOTS * i)
            for g in range(AHEAD + G_K, G0_V):
                load_gate(g)
            with sp.Fori(0, NS // SLOTS) as i:
                for b in range(SLOTS):
                    sp.wait_ge(pages_used.sem, pages_used.now(NS // SLOTS - 1, b))
                    sp.wait_ge(pvd_done.sem, pvd_done.before(i, b))
                    load_pages(ins["cache_sb_v"], i, b)
                    load_gate(G0_V + b, SLOTS * i)
            for n in range(3):
                load_sc(n)
            sp.wait_ge(pvd_done.sem, pvd_done.now(NS // SLOTS - 1, SLOTS - 1))

            def state_ap(dram, t):
                return dram[0, :, 2 * t:2 * t + 2].rearrange("b e p n -> (e p) b n")

            def load_state(t):
                k = t % 2
                if t >= 2:
                    sp.wait_ge(state_written[k], 16 * (t // 2))
                    sp.wait_ge(sample_done.sem, sample_done.now(0, t - 2))
                sp.dma_start(state[:, k, :, :], state_ap(ins["state_ssd"], t)).then_inc(state_landed[k], 16)

            def load_bc(g, k):
                rows = bc_kept[(GROUPS * k + g) * NS:(GROUPS * k + g + 1) * NS, :]
                sp.dma_start((bb, cbb)[k][:, :, :].rearrange("p b n -> p (b n)"),
                             rows.rearrange("b n -> (b n)").partition_broadcast(P)).then_inc(bc_landed[k], 16)

            def load_next(n):
                if n < 3 * SC_T:
                    load_sc(n)
                elif n < 3 * SC_T + G_POST:
                    load_gate(GATES - G_POST + n - 3 * SC_T, first=U_POST - (GATES - G_POST))
            sp.wait_ge(bc_row_kept, 16)
            load_state(0)
            sp.wait_ge(v_summed, 1)
            load_bc(0, 0)
            load_bc(0, 1)
            sp.dma_start(outs["ssd_conv_p"], xb[:, :, NP:NP + 3]).then_inc(out_written, 16)
            sp.dma_start(outs["ssd_conv_s"][:, :, 2, :], xb[:, :, 3 + NP:3 + T]).then_inc(out_written, 16)
            sp.wait_ge(conv_in, 32)
            sp.dma_start(outs["ssd_conv_s"][:, :, 0:2, :], sprev[:, :, 1:3, :]).then_inc(out_written, 16)
            sp.dma_start(outs["sc_conv_s"][:, :, 0, :], scprev[:, :, 1, :]).then_inc(out_written, 16)
            for t in range(SSD_T):
                for n in ((3,), (4, 5))[t % 2]:
                    load_next(t // 2 * 3 + n)
                if t == GT:
                    load_bc(1, 0)
                    sp.wait_ge(sample_done.sem, sample_done.now(0, t - 1))
                    load_bc(1, 1)
                if t < SSD_T - 1:
                    load_state(t + 1)
                sp.wait_ge(hin_ready.sem, hin_ready.now(0, t))
                sp.dma_start(outs["ssd_p"][:, P * t:P * t + P], hin[:, CH, :]).then_inc(hfin_written[0], 16)
                sp.wait_ge(state_ready.sem, state_ready.now(0, t))
                sp.dma_start(state_ap(outs["ssd_s"], t), state[:, t % 2, :, :]).then_inc(state_written[t % 2], 16)
            wait_sctail(sp)
            sp.dma_start(outs["sc_conv_p"], sctail[:, :, 0:2]).then_inc(out_written, 16)
            sp.dma_start(outs["sc_conv_s"][:, :, 1, :], sctail[:, :, 2:2 + NS]).then_inc(out_written, 16)
            for w_proj, u0 in (("w_proj_bc", U_MERGE), ("w_proj_a", U_MERGE_A)):
                with sp.Fori(0, DT // 4) as i:
                    for c in range(4):
                        load_unit(u0 + c, 4 * i, w[w_proj][:, :, ds(i * (4 * P) + c * P, P)], DT)
            sp.wait_ge(y_split, 4)
            sp.wait_ge(out_written, 96)
            sp.wait_ge(x_saved, 16)
            sp.dma_start(x[:, :, :], x_kept).then_inc(x_back, 16)
            with sp.Fori(0, 2) as i:
                for j in range(4):
                    load_unit(U_OUT + j, 4 * i, w["w_out"][:, :, ds(i * (4 * P) + j * P, P)], DT)
            ffn_loads(2, U_FFN2A, U_FFN2B)
            for c in range(DT):
                wait_output(sp, O_FFN2B + c)
                sp.dma_start(outs["y_t"][:, c, :], x[:, c, :]).then_inc(out_written, 16)
            sp.wait_ge(out_written, 96 + 16 * DT)

        @block.scalar
        def _(act):
            link = Chain(act, act_step)
            act.sem_inc(unit_done, SPLITS)

            def square(n, k):
                if n:
                    act.wait_ge(xg_ready, n * DT + k + 1)
                else:
                    act.wait_ge(x_landed[k], 16)
                act.wait_ge(sumsq_ready, n * DT + k)
                nc.scalar.activation(sq[:, :], x[:, k, :], ACT.Square).then_inc(sq_ready, 1)

            def inverse_rms(n):
                act.preload_act_table_set("natural_log_exp_and_others")
                act.wait_ge(stats_ready, n + 1)
                nc.scalar.activation(halves(rstd[:, :]), ps[:, 4:6, 0:HALF], ACT.Ln, bias=eps[:, 0:1], scale=1.0 / D
                                     ).then_inc(rms_ready, 1)
                act.wait_ge(rms_ready, n + 1)
                nc.scalar.activation(rstd[:, :], rstd[:, :], ACT.Exp, scale=-0.5).then_inc(rstd_ready, 1)

            def ffn_a(n, u_a, o_a):
                def turn(a, i):
                    for j in range(4):
                        m = j // 2
                        h = 2 * i + (2 * a + m)
                        u, o = u_a + 4 * a + j, o_a + 4 * a + j
                        round_unit(u + 1, 4 * i, DT)
                        if a == 0 and j == 0:
                            inverse_rms(2 * (n - 1))
                            act.preload_act_table(ACT.Silu)
                        wait_output(act, o, 4 * i)
                        if j % 2 == 0:
                            nc.scalar.activation(silu[:, :], silu[:, :], ACT.Silu).then_inc(silu_ready, 1)
                        else:
                            nc.scalar.activation(hid_hi[:, ds(h, 1), :], prod[:, :].unsqueeze(1), ACT.Copy
                                                 ).then_inc(hid_hi_ready, 1)
                turn(0, 0)
                with act.Fori(0, FT // 2 - 1) as i:
                    turn(1, i)

            def ffn_b(n, u_b):
                for k in range(3 * DT):
                    if u_b + k + 1 < U_END:
                        round_unit(u_b + k + 1, 0, DOWN_K[(k + 1) % 3][1])
                    if k % 3 == 2 and n == 1:
                        square(1, k // 3)

            round_unit(0, 0, DT)
            act.wait_ge(consts_set, CONSTS)
            for k in range(DT):
                square(0, k)
            for name, tile in (("gate_b", gate_b[:, :]), ("conv_w", conv_w[:, :, :]), ("sc_w", sc_w[:, :, :]),
                               ("qk_g", qk_g[:, :]), ("ssd_cols", ssd_cols[:, :, :]), ("ssd_rows", ssd_rows[:, :]),
                               ("table", table[:, :])):
                act.dma_start(tile, ins[name]).then_inc(landed, 16)
            act.dma_start(sb_bias[:, :], ins["sb_bias"].partition_broadcast(P)).then_inc(landed, 16)
            ffn_a(1, U_FFN1A, O_FFN1A)
            ffn_b(1, U_FFN1B)
            round_unit(U_ATT, 0, DT)
            inverse_rms(1)
            act.wait_ge(landed, 8 * 16)

            with act.Fori(0, SB_T) as t:
                link.loop(t, 2 + 2 * 2 * 2)
                up = 8 * t

                def rms_inverse(k, dst):
                    act.wait_ge(qk_summed.sem, qk_summed.now(t, k))
                    link(nc.scalar.activation(halves(dst), ps[:, 4 + 2 * k:6 + 2 * k, 0:HALF], ACT.Ln,
                                              bias=eps[:, 0:1], scale=1.0 / HD))
                    nc.scalar.activation(dst, dst, ACT.Exp, scale=-0.5).then_inc(qk_root.sem, 1)

                def softplus_log(e):
                    for n, part in enumerate(SCORE_PARTS):
                        act.wait_ge(z_biased.sem, z_biased.now(t, 2 * e + n))
                        link(nc.scalar.activation(lg[:, e, part], zb[:, e, part], ACT.Abs))
                        link(nc.scalar.activation(lg[:, e, part], lg[:, e, part], ACT.Exp, scale=-1.0))
                        nc.scalar.activation(lg[:, e, part], lg[:, e, part], ACT.Ln, bias=one[:, 0:1]
                                             ).then_inc(log_ready.sem, 1)

                def weights(e):
                    act.wait_ge(tail_taken.sem, tail_taken.now(t, e))
                    nc.scalar.activation(zb[:, e, :], zb[:, e, :], ACT.Exp).then_inc(w_exped.sem, 1)

                round_unit(U_ATT + 1, up, DT)
                round_unit(U_ATT + 2, up, DT)
                wait_output(act, O_ATT, up)
                act.wait_ge(qk_normed.sem, qk_normed.before(t, 1))
                nc.scalar.activation(sq[:, :], qr[:, :], ACT.Square).then_inc(qk_squared.sem, 1)
                round_unit(U_ATT + 3, up, DT)
                wait_output(act, O_ATT + 1, up)
                nc.scalar.activation(prod[:, :], kr[:, :], ACT.Square).then_inc(qk_squared.sem, 1)
                rms_inverse(0, sq[:, :])
                rms_inverse(1, prod[:, :])
                round_unit(U_ATT + 4, up, DT)
                round_unit(U_ATT + 5, up, DT)
                softplus_log(0)
                round_unit(U_ATT + 6, up, DT)
                weights(0)
                round_unit(U_ATT + 7, up, DT)
                softplus_log(1)
                round_unit(U_ATT + 8, up, DT)
                weights(1)
            link.end(SB_T)

            def pass_gate(g, step=0, first=(U_GATE, O_GATE)):
                round_unit(first[0] + g + 1, step, DT)
                keep_gate(first[1] + g, g, step)
            def round_gate(g):
                round_unit(U_GATE + g, 0, DT)
            round_gate(1)
            act.wait_ge(prep_d, 1)
            link(nc.scalar.activation(row_e, dt_t[:, :], ACT.Abs))
            nc.scalar.activation(row_e, row_e, ACT.Exp, scale=-1.0).then_inc(prep_a, 1)
            nc.scalar.activation(ssd_rows[:, 1:2], ssd_rows[:, 1:2], ACT.Exp).then_inc(prep_a, 1)
            act.wait_ge(prep_d, 2)
            nc.scalar.activation(row_l, row_s, ACT.Ln).then_inc(prep_a, 1)
            act.wait_ge(prep_a, 3)
            act.wait_ge(s_used, 1)
            nc.scalar.activation(row_s, row_l, ACT.Exp, scale=-1.0).then_inc(inverse_ready, 1)
            round_gate(2)
            keep_gate(O_GATE, 0)
            act.wait_ge(prep_d, 3)
            nc.scalar.activation(dtda_t[:, 1, :], la_t[:, NP:T], ACT.Exp).then_inc(prep_a, 1)
            round_gate(3)
            keep_gate(O_GATE + 1, 1)
            act.preload_act_table(ACT.Silu)
            for g in range(2):
                for k in range(GROUPS):
                    part = (bt, ct)[g][:, k, :]
                    act.wait_ge(bc_conved, GROUPS * g + k + 1)
                    nc.scalar.activation(part, part, ACT.Silu).then_inc(prep_a, 1)
                if g == 0:
                    round_gate(4)
                    keep_gate(O_GATE + 2, 2)
            act.wait_ge(cdec_conved, 1)
            nc.scalar.activation(cdec[:, :, :], cdec[:, :, :], ACT.Silu).then_inc(prep_a, 1)
            keep_gate(O_GATE + 3, 3)
            nc.scalar.activation(zs[:, :, :], zs[:, :, :], ACT.Silu).then_inc(zs_ready, 1)
            assert G_PRE == 4 and G_PREP == 2
            act.preload_act_table_set("natural_log_exp_and_others")
            with act.Fori(0, NS // SLOTS) as i:
                for b in range(SLOTS):
                    pass_gate(G_PRE + b, SLOTS * i)
            act.wait_ge(zd_ready, 1)
            link(nc.scalar.activation(lgd[:, :, :, :], zd[:, :, :, :], ACT.Abs))
            link(nc.scalar.activation(lgd[:, :, :, :], lgd[:, :, :, :], ACT.Exp, scale=-1.0))
            nc.scalar.activation(lgd[:, :, :, :], lgd[:, :, :, :], ACT.Ln, bias=one[:, 0:1]).then_inc(lgd_ready, 1)
            round_unit(U_GATE + G0_PREP + 1, 0, DT)
            act.wait_ge(prep_d, 5)
            nc.scalar.activation(to_end[:, :, :], to_end[:, :, :], ACT.Exp).then_inc(prep_a, 1)
            nc.scalar.activation(ch_dec[:, :, :], flat[:, 7 * 512:7 * 512 + CH * SSD_HEADS].rearrange(
                "p (c h) -> p c h", c=CH), ACT.Exp).then_inc(prep_a, 1)
            keep_gate(O_GATE + G0_PREP, G0_PREP)
            act.wait_ge(wd_raw, 1)
            nc.scalar.activation(zd[:, :, :, :], zd[:, :, :, :], ACT.Exp).then_inc(wd_ready, 1)
            pass_gate(G0_PREP + 1)
            act.preload_act_table(ACT.Silu)

            def pick(t, e):
                h = 2 * t + e
                act.wait_ge(cs_spread.sem, cs_spread.now(0, h - 2))
                nc.scalar.activation(head_cs[e], cs_t[:, 0:NP], ACT.Copy, scale=ident[0:SSD_HEADS, h:h + 1]
                                     ).then_inc(head_cs_ready.sem, 1)

            def decays(t, e):
                act.wait_ge(seg_ready.sem, seg_ready.now(0, 2 * t + e))
                nc.scalar.activation(csc[:, e, :], ps[:, (6, 4)[e], :], ACT.Exp).then_inc(ecs_ready.sem, 1)
                nc.scalar.activation(gbuf[:, e, :], gbuf[:, e, :], ACT.Exp).then_inc(decay_ready.sem, 1)

            act.wait_ge(prep_d, 7)
            for e in range(2):
                pick(0, e)
            with act.Fori(0, NS // SLOTS) as i:
                for b in range(SLOTS):
                    pass_gate(G0_V + b, SLOTS * i)
                    act.wait_ge(conv_ready.sem, conv_ready.now(i, b))
                    nc.scalar.activation(xb[:, ds(SLOTS * i + b, 1), 0:NP], (sq, sumsq)[b % 2][:, 0:NP].unsqueeze(1),
                                         ACT.Silu).then_inc(xs_ready.sem, 1)

            def square_y(t):
                act.wait_ge(y_ready.sem, y_ready.now(0, t))
                act.wait_ge(sample_done.sem, sample_done.now(0, t))
                if t >= 2:
                    act.wait_ge(ysum_ready, t - 1)
                nc.scalar.activation(ysq[:, t % 2, :], zs[:, t, :], ACT.Square).then_inc(ysq_ready, 1)

            for t in range(SSD_T):
                u = U_SSD + 3 * (t // 2)
                decays(t, 0)
                decays(t, 1)
                if t % 2:
                    round_unit(u + 2, 0, DT)
                if t < SSD_T - 1:
                    pick(t + 1, 0)
                    pick(t + 1, 1)
                round_unit(u + (1, 3)[t % 2], 0, DT)
                if t == GT:
                    act.wait_ge(out_written, 64)
                if t >= GT:
                    for n in range(2 * (t - GT), min(2 * (t - GT) + 2, SSD_T - 1)):
                        square_y(n)

            def split_y(first, src, n, tiles):
                act.wait_ge(yprod_ready, n + 1)
                nc.scalar.activation(y_hi[:, first:first + tiles, :], src, ACT.Copy).then_inc(yhi_ready, 1)
            post = (U_POST - (GATES - G_POST), O_POST - (GATES - G_POST))
            pass_gate(GATES - 2, first=post)
            square_y(SSD_T - 1)
            split_y(8, yb[:, :, :], 0, 4)
            split_y(12, yc[:, :, :], 1, 4)
            pass_gate(GATES - 1, first=post)

            def open_gate(n):
                c = n // 2 if n < 2 * DT else n - 2 * DT
                column = (1 + n % 2) * DT + c if n < 2 * DT else c
                slot = n % GATE_SLOTS
                act.wait_ge(gate_landed[slot], 16 * (n // GATE_SLOTS + 1))
                nc.scalar.activation(gates[:, slot, :], gates[:, slot, :], ACT.Sigmoid, bias=gate_b[:, column:column + 1]
                                     ).then_inc(gate_open, 1)
            for c in range(DT):
                round_unit(U_MERGE + c + 1, 0, DT)
                open_gate(2 * c)
                open_gate(2 * c + 1)
                if c == 0:
                    act.preload_act_table_set("natural_log_exp_and_others")
                    for g in range(GROUPS):
                        act.wait_ge(ysum_spread, g + 1)
                        link(nc.scalar.activation(halves(ysum[:, g, :]), ps[:, 4 + 2 * g:6 + 2 * g, 0:HALF], ACT.Ln,
                                                  bias=eps[:, 0:1], scale=1.0 / (GT * P)))
                        nc.scalar.activation(ysum[:, g, :], ysum[:, g, :], ACT.Exp, scale=-0.5).then_inc(yroot_ready, 1)
                if c in (2, 4):
                    g = c // 2 - 1
                    split_y(GT * g, zs[:, GT * g:GT * g + GT, :], 2 + g, GT)
            for c in range(DT):
                round_unit(U_MERGE_A + c + 1, 0, DT)
                open_gate(2 * DT + c)
                act.wait_ge(merged, c + 1)
                nc.scalar.activation(m_hi[:, c, :], (prod, silu)[c % 2][:, :], ACT.Copy).then_inc(m_hi_ready, 1)
            for c in range(DT):
                round_unit(U_OUT + c + 1, 0, DT)
                square(2, c)
            ffn_a(2, U_FFN2A, O_FFN2A)
            ffn_b(2, U_FFN2B)

        @block.vector
        def _(dve):
            link = Chain(dve, dve_step)
            dve.sem_inc(unit_split, STAGES)
            dve.sem_inc(acc_read, 2)
            nc.vector.memset(eps[:, :], EPS).then_inc(consts_set, 1)
            nc.vector.memset(one[:, :], 1.0).then_inc(consts_set, 1)
            link(nc.vector.memset(blocks[:, :], 0.0))
            nc.vector.memset(blocks[0:HD, 0:HD], 1.0)
            nc.vector.memset(blocks[HD:P, HD:P], 1.0).then_inc(consts_set, 1)
            dve.wait_ge(norms_landed, 16)

            def make_xg(c, n, count):
                nc.vector.tensor_scalar(xg_hi[:, c, :], x[:, c, :], norms[:, n, c:c + 1], None, ALU.mult
                                        ).then_inc(xg_hi_ready, 1)
                dve.wait_ge(xg_hi_ready, count + 1)
                nc.vector.scalar_tensor_tensor(xg_lo[:, c, :], x[:, c, :], norms[:, n, c:c + 1],
                                               xg_hi[:, c, :].bitcast(F32), ALU.mult, ALU.subtract
                                               ).then_inc(xg_ready, 1)

            def scaled(dst, o):
                return nc.vector.tensor_tensor(dst, acc(o), halves(rstd[:, :]), ALU.mult)

            def ffn_a(n, u_a, o_a):
                def turn(a, i):
                    for j in range(4):
                        m = j // 2
                        h = 2 * i + (2 * a + m)
                        u, o = u_a + 4 * a + j, o_a + 4 * a + j
                        rest_unit(u + 1, 4 * i, DT)
                        if a == 0 and j == 0:
                            dve.wait_ge(rstd_ready, 2 * n - 1)
                        if j % 2 == 0:
                            wait_unit(dve, u, 4 * i)
                            scaled(halves(silu[:, :]), o).then_inc(acc_read, 1)
                        else:
                            dve.wait_ge(silu_ready, h + (1 + (n - 1) * FT))
                            link(nc.vector.tensor_tensor(silu[:, :], silu[:, :], rstd[:, :], ALU.mult))
                            wait_unit(dve, u, 4 * i)
                            nc.vector.tensor_tensor(halves(prod[:, :]), acc(o), halves(silu[:, :]), ALU.mult
                                                    ).then_inc(acc_read, 1)
                            dve.wait_ge(hid_hi_ready, h + (1 + (n - 1) * FT))
                            nc.vector.tensor_tensor(hid_lo[:, ds(h, 1), :], prod[:, :].unsqueeze(1),
                                                    hid_hi[:, ds(h, 1), :].bitcast(F32), ALU.subtract
                                                    ).then_inc(hid_ready, 1)
                turn(0, 0)
                with dve.Fori(0, FT // 2 - 1) as i:
                    link.loop(i, 2)
                    turn(1, i)
                link.end(FT // 2 - 1)

            def add_to_x(c, o, factor, n):
                nc.vector.scalar_tensor_tensor(halves(x[:, c, :]), acc(o), factor, halves(x[:, c, :]),
                                               ALU.mult, ALU.add).then_inc(acc_read, 1)
                if n < 3:
                    wait_output(dve, o)
                    make_xg(c, n, n * DT + c)

            def ffn_b(n, u_b, o_b):
                for k in range(3 * DT):
                    if u_b + k + 1 < U_END:
                        rest_unit(u_b + k + 1, 0, DOWN_K[(k + 1) % 3][1])
                    if k % 3 == 2:
                        wait_unit(dve, u_b + k)
                        add_to_x(k // 3, o_b + k // 3, 0.5, 1 if n == 1 else 3)

            rest_unit(0, 0, DT)
            for c in range(DT):
                dve.wait_ge(x_landed[c], 16)
                make_xg(c, 0, c)
            ffn_a(1, U_FFN1A, O_FFN1A)
            ffn_b(1, U_FFN1B, O_FFN1B)
            rest_unit(U_ATT, 0, DT)
            dve.wait_ge(rstd_ready, 2)
            dve.wait_ge(landed, 8 * 16)
            dve.wait_ge(consts_set, CONSTS)
            link(nc.vector.tensor_scalar(qk_g[:, 0:1], qk_g[:, 0:1], HD ** -0.5, None, ALU.mult))
            wait_unit(dve, U_DT)
            dve.wait_ge(x_saved, 16)
            nc.vector.tensor_tensor(halves(dt_t[:, :]), acc(O_DT)[0:SSD_HEADS], halves(rstd[0:SSD_HEADS, :]), ALU.mult
                                    ).then_inc(acc_read, 1)
            nc.vector.memset(xb[:, :, 0:3], 0.0)
            link(nc.vector.tensor_tensor(strict[:, :], upto[:, :], ident[:, :], ALU.subtract))

            with dve.Fori(0, SB_T) as t:
                link.loop(t, 2 * 2 + 1)
                up = 8 * t

                def take(j, dst):
                    rest_unit(U_ATT + j + 1, up, DT)
                    wait_unit(dve, U_ATT + j, up)
                    scaled(dst, O_ATT + j).then_inc(acc_read, 1)

                def take_z(j):
                    take(3 + j, zs[:, ds(2 * t + j, 1), :].rearrange("p o (a b) -> p (o a) b", a=2))

                def take_x(j):
                    take(5 + j, xb[:, ds(3 * t + j, 1), 3:3 + T].rearrange("p o (a b) -> p (o a) b", a=2))

                def bias_z(e):
                    dve.wait_ge(scored.sem, scored.now(t, e))
                    for part in SCORE_PARTS:
                        nc.vector.tensor_scalar(zb[:, e, part], flat[:, 2048 + part.start:2048 + part.stop],
                                                sb_bias[:, ds(2 * t + e, 1)], None, ALU.add).then_inc(z_biased.sem, 1)

                def mask_diagonals(buf):
                    a = buf[:, 0:1024].rearrange("p (j i) -> p j i", j=2)[:, :, 0:P]
                    m = strict[:, :].unsqueeze(1).broadcast_to([P, 2, P])
                    nc.vector.tensor_tensor(a, a, m, ALU.mult)
                    b = buf[:, 896:1152].rearrange("p (j i) -> p j i", j=2)
                    return nc.vector.tensor_tensor(b, b, m, ALU.mult)

                def softplus(e):
                    for n, part in enumerate(SCORE_PARTS):
                        dve.wait_ge(log_ready.sem, log_ready.now(t, 2 * e + n))
                        last = nc.vector.scalar_tensor_tensor(spl[:, e, part], zb[:, e, part], 0.0, lg[:, e, part],
                                                              ALU.max, ALU.add)
                    link(last)
                    mask_diagonals(spl[:, e, :]).then_inc(sp_ready.sem, 1)
                    link(nc.vector.scalar_tensor_tensor(zb[:, e, :], zb[:, e, :], 0.0, lg[:, e, :], ALU.min,
                                                        ALU.subtract))

                def take_tail(e):
                    dve.wait_ge(tail_summed.sem, tail_summed.now(t, e))
                    nc.vector.tensor_tensor(zb[:, e, :], zb[:, e, :], flat[:, 2048:2048 + SCORES], ALU.subtract
                                            ).then_inc(tail_taken.sem, 1)

                def mask_weights(e):
                    dve.wait_ge(w_exped.sem, w_exped.now(t, e))
                    mask_diagonals(zb[:, e, :]).then_inc(w_ready.sem, 1)

                take(0, halves(qr[:, :]))
                dve.wait_ge(kv_written, 32 * t + 32)
                take(1, halves(kr[:, :]))
                take(2, halves(vr[:, :]))
                for k, (raw, hat, inv) in enumerate(((qr, qh, sq), (kr, kh, prod))):
                    dve.wait_ge(qk_root.sem, qk_root.now(t, k))
                    nc.vector.scalar_tensor_tensor(hat[:, :], raw[:, :], qk_g[:, k:k + 1], inv[:, :], ALU.mult,
                                                   ALU.mult).then_inc(qk_normed.sem, 1)
                dve.wait_ge(qk_normed.sem, qk_normed.now(t, 0))
                link(nc.vector.tensor_copy(qdec[:, ds(t, 1), :], qh[:, NP:T].unsqueeze(1)))
                take_z(0)
                bias_z(0)
                rest_unit(U_ATT + 5, up, DT)
                softplus(0)
                wait_unit(dve, U_ATT + 4, up)
                scaled(zs[:, ds(2 * t + 1, 1), :].rearrange("p o (a b) -> p (o a) b", a=2), O_ATT + 4
                       ).then_inc(acc_read, 1)
                dve.wait_ge(v_turned.sem, v_turned.now(t))
                nc.vector.tensor_copy(v_tok[:, :, :], ps[:, 7, :].rearrange("p (c d) -> p c d", c=CH)
                                      ).then_inc(v_tok_ready.sem, 1)
                take_tail(0)
                rest_unit(U_ATT + 6, up, DT)
                wait_unit(dve, U_ATT + 5, up)
                scaled(xb[:, ds(3 * t, 1), 3:3 + T].rearrange("p o (a b) -> p (o a) b", a=2), O_ATT + 5
                       ).then_inc(acc_read, 1)
                bias_z(1)
                mask_weights(0)
                rest_unit(U_ATT + 7, up, DT)
                softplus(1)
                wait_unit(dve, U_ATT + 6, up)
                scaled(xb[:, ds(3 * t + 1, 1), 3:3 + T].rearrange("p o (a b) -> p (o a) b", a=2), O_ATT + 6
                       ).then_inc(acc_read, 1)
                take_tail(1)
                rest_unit(U_ATT + 8, up, DT)
                mask_weights(1)
                wait_unit(dve, U_ATT + 7, up)
                scaled(xb[:, ds(3 * t + 2, 1), 3:3 + T].rearrange("p o (a b) -> p (o a) b", a=2), O_ATT + 7
                       ).then_inc(acc_read, 1)
                dve.wait_ge(pv_done.sem, pv_done.now(t, 1))
                nc.vector.tensor_copy(yc[:, ds(t, 1), 0:NP], ps[:, 7:8, :]).then_inc(yc_ready.sem, 1)
            link.end(SB_T)

            dve.wait_ge(q_turned, 1)
            nc.vector.tensor_copy(q_row[:, :], ps[0:SB_T * NS, 4, 0:P]).then_inc(q_row_ready, 1)
            dve.wait_ge(qk_normed.sem, qk_normed.now(SB_T - 1, 1))

            def pass_gate(g, step=0, first=(U_GATE, O_GATE)):
                rest_unit(first[0] + g + 1, step, DT)
                take_gate(first[0] + g, first[1] + g, g, step)
            def conv(dst, t):
                link(nc.vector.tensor_scalar(dst, xb[:, t, 0:NP], conv_w[:, 0, t:t + 1], conv_w[:, 4, t:t + 1],
                                             ALU.mult, ALU.add))
                for k in range(1, 4):
                    last = nc.vector.scalar_tensor_tensor(dst, xb[:, t, k:k + NP], conv_w[:, k, t:t + 1], dst,
                                                          ALU.mult, ALU.add)
                    if k < 3:
                        link(last)
                return last
            R = SSD_HEADS
            nc.vector.tensor_scalar(dt_t[:, :], dt_t[:, :], ssd_rows[:, 0:1], None, ALU.add).then_inc(prep_d, 1)
            rest_unit(U_GATE + 1, 0, DT)
            dve.wait_ge(prep_a, 1)
            nc.vector.tensor_scalar(row_s, row_e, 1.0, None, ALU.add).then_inc(prep_d, 1)
            dve.wait_ge(prep_d, 2)
            nc.vector.scalar_tensor_tensor(la_t[:, :], row_s, -1.0, row_e, ALU.add, ALU.subtract).then_inc(s_used, 1)
            take_gate(U_GATE, O_GATE, 0)
            rest_unit(U_GATE + 2, 0, DT)
            dve.wait_ge(inverse_ready, 1)
            dve.wait_ge(s_used, 1)
            link(nc.vector.tensor_tensor(la_t[:, :], la_t[:, :], row_s, ALU.mult))
            link(nc.vector.tensor_tensor(row_l, row_l, la_t[:, :], ALU.subtract))
            link(nc.vector.scalar_tensor_tensor(dt_t[:, :], dt_t[:, :], 0.0, row_l, ALU.max, ALU.add))
            nc.vector.tensor_copy(dtda_t[:, 0, :], dt_t[:, NP:T])
            nc.vector.tensor_scalar(la_t[:, :], dt_t[:, :], ssd_rows[:, 1:2], -1.0, ALU.mult, ALU.mult
                                    ).then_inc(prep_d, 1)
            take_gate(U_GATE + 1, O_GATE + 1, 1)
            rest_unit(U_GATE + 3, 0, DT)
            for k in range(GROUPS):
                conv(bt[:, k, :], SSD_T + k).then_inc(bc_conved, 1)
            take_gate(U_GATE + 2, O_GATE + 2, 2)
            rest_unit(U_GATE + 4, 0, DT)
            for k in range(GROUPS):
                conv(ct[:, k, :], SSD_T + GROUPS + k).then_inc(bc_conved, 1)
            dve.wait_ge(conv_in, 32)

            def tap(k):
                return conv_w[:, k, :].unsqueeze(2).broadcast_to([P, XBC_T, NS])
            link(nc.vector.tensor_tensor(cdec[:, :, :], sprev[:, :, 0, :], tap(0), ALU.mult))
            for src, k in ((sprev[:, :, 1, :], 1), (sprev[:, :, 2, :], 2), (xb[:, :, 3 + NP:3 + T], 3)):
                link(nc.vector.tensor_tensor(ctmp[:, :, :], src, tap(k), ALU.mult))
                link(nc.vector.tensor_tensor(cdec[:, :, :], cdec[:, :, :], ctmp[:, :, :], ALU.add))
            nc.vector.tensor_tensor(cdec[:, :, :], cdec[:, :, :], tap(4), ALU.add).then_inc(cdec_conved, 1)
            take_gate(U_GATE + 3, O_GATE + 3, 3)
            with dve.Fori(0, NS // SLOTS) as i:
                for b in range(SLOTS):
                    pass_gate(G_PRE + b, SLOTS * i)
                    dve.wait_ge(kq_ready.sem, kq_ready.now(i, b))
                    nc.vector.tensor_reduce(zd[:, :, ds(SLOTS * i + b, 1), :].rearrange("p g o h -> p (g o) h"),
                                            pages[:, b, :, :].rearrange("p g (h d) -> p g h d", d=HD), AX_X, ALU.add
                                            ).then_inc(pages_used.sem, 1)
            dve.wait_ge(pages_used.sem, pages_used.now(NS // SLOTS - 1, SLOTS - 1))
            nc.vector.tensor_tensor(zd[:, :, :, :].rearrange("p g b h -> p (g b) h"),
                                    zd[:, :, :, :].rearrange("p g b h -> p (g b) h"),
                                    sb_bias[:, :].unsqueeze(1).broadcast_to([P, PAGES * NS, SB_HEADS]), ALU.add
                                    ).then_inc(zd_ready, 1)
            dve.wait_ge(prep_p, 1)
            tok = "p (c h) -> p c h"
            nc.vector.tensor_copy(dt_tok[:, :, :], ps[:, 4, 0:CH * R].rearrange(tok, c=CH))
            nc.vector.tensor_copy(la_tok[:, :, :], ps[:, 5, 0:CH * R].rearrange(tok, c=CH)).then_inc(prep_d, 1)
            rest_unit(U_GATE + G0_PREP + 1, 0, DT)
            dve.wait_ge(lgd_ready, 1)
            nc.vector.scalar_tensor_tensor(spd[:, :, :, :], zd[:, :, :, :], 0.0, lgd[:, :, :, :], ALU.max, ALU.add
                                           ).then_inc(spd_ready, 1)
            link(nc.vector.scalar_tensor_tensor(zd[:, :, :, :], zd[:, :, :, :], 0.0, lgd[:, :, :, :], ALU.min,
                                                ALU.subtract))
            dve.wait_ge(prep_p, 2)
            link(nc.vector.tensor_copy(cs_tok[:, :, :], ps[:, 4, 0:CH * R].rearrange(tok, c=CH)))
            nc.vector.tensor_tensor(to_end[:, :, :], ps[:, 7, 0:CH * R].rearrange(tok, c=CH), cs_tok[:, :, :],
                                    ALU.subtract).then_inc(prep_d, 1)
            take_gate(U_GATE + G0_PREP, O_GATE + G0_PREP, G0_PREP)
            dve.wait_ge(taild_ready, 1)
            nc.vector.tensor_tensor(zd[:, :, :, :], zd[:, :, :, :],
                                    ps[:, 6, 0:PAGES * NS * SB_HEADS].rearrange("p (g b h) -> p g b h", g=PAGES, b=NS),
                                    ALU.subtract).then_inc(wd_raw, 1)
            pass_gate(G0_PREP + 1)
            dve.wait_ge(prep_p, 3)
            nc.vector.tensor_copy(cs_t[:, 0:NP], ps[0:R, 4, :]).then_inc(prep_d, 1)
            nc.vector.tensor_copy(dtda[:, :, :, :], ps[:, 5, 0:SSD_T * 2 * NS].rearrange(
                "p (t k b) -> p t k b", t=SSD_T, k=2)).then_inc(prep_d, 1)

            dve.wait_ge(prep_a, 9)
            dve.wait_ge(prep_d, 7)
            nc.vector.tensor_tensor(xdd[:, :, :], cdec[:, 0:SSD_T, :], dtda[:, :, 0, :], ALU.mult).then_inc(xdd_ready, 1)
            dve.wait_ge(bc_turned, 1)
            nc.vector.tensor_copy(bc_row[:, :], ps[0:2 * GROUPS * NS, 4, 0:P]).then_inc(bc_row_ready, 1)
            with dve.Fori(0, NS // SLOTS) as i:
                link.loop(i, 3 * SLOTS)
                dve.wait_ge(wd_ready, 1)
                nc.vector.tensor_copy(wd4[:, :, :].rearrange("p g (b h) -> p g b h", b=SLOTS),
                                      zd[:, :, ds(SLOTS * i, SLOTS), :]).then_inc(wd4_ready.sem, 1)
                for b in range(SLOTS):
                    pass_gate(G0_V + b, SLOTS * i)
                    t = ds(SLOTS * i + b, 1)
                    conved = (sq, sumsq)[b % 2][:, 0:NP].unsqueeze(1)
                    if b < 2:
                        dve.wait_ge(xs_ready.sem, xs_ready.before(i, b + 2))
                    else:
                        dve.wait_ge(xs_ready.sem, xs_ready.now(i, b - 2))
                    link(nc.vector.tensor_scalar(conved, xb[:, t, 0:NP], conv_w[:, 0, t], conv_w[:, 4, t], ALU.mult,
                                                 ALU.add))
                    for k in range(1, 4):
                        tap_ = nc.vector.scalar_tensor_tensor(conved, xb[:, t, k:k + NP], conv_w[:, k, t], conved,
                                                              ALU.mult, ALU.add)
                        if k < 3:
                            link(tap_)
                    tap_.then_inc(conv_ready.sem, 1)
                dve.wait_ge(own_set, 1)
                dve.wait_ge(pvd_done.sem, pvd_done.now(i, SLOTS - 1))
                nc.vector.tensor_tensor(own_v[:, ds(i, 1), :], ps[:, 7:8, :],
                                        own[:, :, :].rearrange("p h d -> p (h d)").unsqueeze(1), ALU.mult
                                        ).then_inc(own_v_ready, 1)
                dve.wait_ge(own_v_ready, i + 1)
            link.end(NS // SLOTS)

            dve.wait_ge(pvd_done.sem, pvd_done.now(NS // SLOTS - 1, SLOTS - 1))
            nc.vector.memset(hin[:, 0, :], 0.0)
            nc.vector.memset(scx[:, 0:2], 0.0)
            for g in range(GROUPS):
                dve.wait_ge(b_turned, g + 1)
                nc.vector.tensor_copy(b_tok[:, g, :, :], ps[:, 4 + g, :].rearrange("p (c n) -> p c n", c=CH)
                                      ).then_inc(b_tok_ready, 1)
            dve.wait_ge(v_summed, 1)
            nc.vector.tensor_copy(yc[:, :, NP:T].rearrange("p t (i b) -> p t i b", i=NS // SLOTS),
                                  ps[:, 6, 0:SB_T * NS].rearrange("p (i t b) -> p t i b", i=NS // SLOTS, t=SB_T)
                                  ).then_inc(yc_sampled, 1)
            for g in range(GROUPS):
                dve.wait_ge(cb_made, g + 1)
                chunks = "p (c l) -> p c l"
                nc.vector.tensor_tensor(cb[:, g, :].rearrange(chunks, c=CH), ps[:, 7 - g, :].rearrange(chunks, c=CH),
                                        upto[:, :].unsqueeze(1).broadcast_to([P, CH, P]), ALU.mult
                                        ).then_inc(cb_ready, 1)
            dve.wait_ge(cb_ready, GROUPS)
            gates_stored(dve, GATES - G_POST)
            dve.wait_ge(zs_ready, 1)

            def tile_xd(t):
                dve.wait_ge(xs_turned.sem, xs_turned.now(0, t))
                nc.vector.tensor_tensor(xd[:, t % 2, :, :].rearrange("p c (h d) -> p c h d", h=2),
                                        ps[:, 4, :].rearrange("p (c h d) -> p c h d", c=CH, h=2),
                                        dt_tok[:, :, 2 * t:2 * t + 2].unsqueeze(3).broadcast_to([P, CH, 2, HD]),
                                        ALU.mult).then_inc(xd_ready.sem, 1)

            def tile_states(t):
                dve.wait_ge(states_ready.sem, states_ready.now(0, t))
                if t:
                    dve.wait_ge(hfin_written[0], 16 * t)
                last = nc.vector.tensor_copy(hin[:, 1, :], ps[:, 5, 0:P])
                for c in range(1, CH):
                    link(last)
                    for e in range(2):
                        cols = slice(HD * e, HD * e + HD)
                        last = nc.vector.scalar_tensor_tensor(
                            hin[:, c + 1, cols], hin[:, c, cols], ch_dec[:, c, 2 * t + e:2 * t + e + 1],
                            ps[:, 5, P * c + HD * e:P * c + HD * e + HD], ALU.mult, ALU.add)
                last.then_inc(hin_ready.sem, 1)

            def head_seg(t, e):
                h = 2 * t + e
                dve.wait_ge(cs_spread.sem, cs_spread.now(0, h))
                for c in range(CH):
                    last = nc.vector.tensor_scalar(gbuf[:, e, P * c:P * c + P], ps[:, (6, 4)[e], P * c:P * c + P],
                                                   cs_tok[:, c, h:h + 1], 0.0, ALU.subtract, ALU.min)
                last.then_inc(seg_ready.sem, 1)

            def head_g(t, e):
                dve.wait_ge(decay_ready.sem, decay_ready.now(0, 2 * t + e))
                nc.vector.tensor_tensor(gbuf[:, e, :], gbuf[:, e, :], cb[:, t // GT, :], ALU.mult
                                        ).then_inc(g_ready.sem, 1)

            def tile_y(t):
                x_t = x_tile(t)
                dve.wait_ge(y_summed.sem, y_summed.now(0, t))
                link(nc.vector.scalar_tensor_tensor(x_t, x_t, ssd_cols[:, 0, t:t + 1], ps[:, 7, :], ALU.mult, ALU.add))
                nc.vector.tensor_tensor(zs[:, t, 0:NP], zs[:, t, 0:NP], x_t, ALU.mult).then_inc(y_ready.sem, 1)

            def sample_y(t):
                if t % GT == 0:
                    dve.wait_ge(bc_landed[1], 16 * (t // GT + 1))
                dve.wait_ge(state_ready.sem, state_ready.now(0, t))
                link(nc.vector.tensor_tensor(stmp[:, :, :], state[:, t % 2, :, :], cbb[:, :, :], ALU.mult))
                link(nc.vector.tensor_reduce(ydec[:, :], stmp[:, :, :], AX_X, ALU.add))
                link(nc.vector.scalar_tensor_tensor(ydec[:, :], cdec[:, t, :], ssd_cols[:, 0, t:t + 1], ydec[:, :],
                                                    ALU.mult, ALU.add))
                nc.vector.tensor_tensor(zs[:, t, NP:T], zs[:, t, NP:T], ydec[:, :], ALU.mult
                                        ).then_inc(sample_done.sem, 1)

            def sc_unit(it, j):
                u, o = U_SSD + 3 * it + j, O_SSD + 3 * it + j
                wait_unit(dve, u)
                if j == 0:
                    scaled(halves(silu[:, :]), o).then_inc(acc_read, 1)
                    wait_output(dve, o)
                    link(nc.vector.tensor_tensor(silu[:, :], silu[:, :], rstd[:, :], ALU.mult))
                elif j == 1:
                    nc.vector.tensor_tensor(halves(scx[:, 2:2 + T]), acc(o), halves(silu[:, :]), ALU.mult
                                            ).then_inc(acc_read, 1)
                    wait_output(dve, o)
                    nc.vector.tensor_copy(sctail[:, it, :], scx[:, NP:2 + T]).then_inc(sc_tail_copied, 1)
                    link(nc.vector.tensor_scalar(prod[:, 0:NP], scx[:, 0:NP], sc_w[:, 0, it:it + 1], None, ALU.mult))
                    for n in range(1, 3):
                        link(nc.vector.scalar_tensor_tensor(prod[:, 0:NP], scx[:, n:n + NP], sc_w[:, n, it:it + 1],
                                                            prod[:, 0:NP], ALU.mult, ALU.add))
                    link(nc.vector.tensor_scalar(prod[:, NP:T], scx[:, 2 + NP:2 + T], sc_w[:, 2, it:it + 1], None,
                                                 ALU.mult))
                    for n in range(2):
                        link(nc.vector.scalar_tensor_tensor(prod[:, NP:T], scprev[:, it, n, :],
                                                            sc_w[:, n, it:it + 1], prod[:, NP:T], ALU.mult, ALU.add))
                    link(nc.vector.tensor_tensor(prod[:, :], prod[:, :], rstd[:, :], ALU.mult))
                else:
                    nc.vector.tensor_tensor(halves(yb[:, it, :]), acc(o), halves(prod[:, :]), ALU.mult
                                            ).then_inc(acc_read, 1)

            for t in range(SSD_T):
                it = t // 2
                u = U_SSD + 3 * it
                tile_xd(t)
                head_seg(t, 0)
                head_seg(t, 1)
                if t:
                    tile_y(t - 1)
                if t and t % 2 == 0:
                    sc_unit(it - 1, 2)
                tile_states(t)
                head_g(t, 0)
                head_g(t, 1)
                if t % 2:
                    rest_unit(u + 2, 0, DT)
                if t:
                    sample_y(t - 1)
                sc_unit(it, t % 2)
                rest_unit(u + (1, 3)[t % 2], 0, DT)
            sc_unit(SC_T - 1, 2)
            tile_y(SSD_T - 1)
            sample_y(SSD_T - 1)

            def low_y(first, src, n, tiles):
                dve.wait_ge(yhi_ready, n + 1)
                nc.vector.tensor_tensor(y_lo[:, first:first + tiles, :], src,
                                        y_hi[:, first:first + tiles, :].bitcast(F32), ALU.subtract).then_inc(y_split, 1)
            post = (U_POST - (GATES - G_POST), O_POST - (GATES - G_POST))
            pass_gate(GATES - 2, first=post)
            branches_stored(dve)
            nc.vector.drain().then_inc(yprod_ready, 2)
            low_y(8, yb[:, :, :], 0, 4)
            low_y(12, yc[:, :, :], 1, 4)
            pass_gate(GATES - 1, first=post)
            gates_stored(dve, GATES)
            for c in range(DT):
                rest_unit(U_MERGE + c + 1, 0, DT)
                for n, (done, dst) in enumerate(((b_done, part[:, c, :]), (unit_done, silu[:, :]))):
                    dve.wait_ge(gate_open, 2 * c + n + 1)
                    dve.wait_ge(done, c + 1 if n == 0 else SPLITS + U_MERGE + c + 1)
                    nc.vector.tensor_tensor(halves(dst), acc(O_MERGE + n), halves(gates[:, (2 * c + n) % GATE_SLOTS, :]),
                                            ALU.mult).then_inc(acc_read, 1)
                wait_output(dve, O_MERGE + 2 * c + 1)
                link(nc.vector.tensor_tensor(part[:, c, :], part[:, c, :], silu[:, :], ALU.add))
                if c in (1, 3):
                    g = c // 2
                    dve.wait_ge(yroot_ready, g + 1)
                    for t in range(GT * g, GT * g + GT):
                        last = nc.vector.scalar_tensor_tensor(zs[:, t, :], zs[:, t, :], ssd_cols[:, 1, t:t + 1],
                                                              ysum[:, g, :], ALU.mult, ALU.mult)
                    last.then_inc(yprod_ready, 1)
                if c in (2, 4):
                    g = c // 2 - 1
                    low_y(GT * g, zs[:, GT * g:GT * g + GT, :], 2 + g, GT)
            for c in range(DT):
                total = (prod, silu)[c % 2]
                rest_unit(U_MERGE_A + c + 1, 0, DT)
                dve.wait_ge(gate_open, 2 * DT + c + 1)
                wait_unit(dve, U_MERGE_A + c)
                if c >= 2:
                    dve.wait_ge(m_ready, c - 1)
                nc.vector.tensor_tensor(halves(total[:, :]), acc(O_MERGE_A + c),
                                        halves(gates[:, (2 * DT + c) % GATE_SLOTS, :]), ALU.mult).then_inc(acc_read, 1)
                wait_output(dve, O_MERGE_A + c)
                nc.vector.tensor_tensor(total[:, :], total[:, :], part[:, c, :], ALU.add
                                        ).then_inc(merged, 1)
                dve.wait_ge(m_hi_ready, c + 1)
                nc.vector.tensor_tensor(m_lo[:, c, :], total[:, :], m_hi[:, c, :].bitcast(F32), ALU.subtract
                                        ).then_inc(m_ready, 1)
            dve.wait_ge(x_back, 16)
            for c in range(DT):
                rest_unit(U_OUT + c + 1, 0, DT)
                wait_unit(dve, U_OUT + c)
                add_to_x(c, O_OUT + c, 1.0, 2)
            ffn_a(2, U_FFN2A, O_FFN2A)
            ffn_b(2, U_FFN2B, O_FFN2B)

        @block.gpsimd
        def _(pool):
            link = Chain(pool, pool_step)
            link(nc.gpsimd.memset(ones[:, :], 1.0))
            link(nc.gpsimd.memset(ident[:, :], 0.0))
            nc.gpsimd.affine_select(out=ident[:, :], in_=ident[:, :], compare_op=ALU.not_equal, fill=1.0, base=0,
                                    pattern=[[-1, P]], channel_multiplier=1).then_inc(consts_set, 1)
            nc.gpsimd.affine_select(out=upto[:, :], in_=ones[:, :], compare_op=ALU.is_ge, fill=0.0, base=0,
                                    pattern=[[1, P]], channel_multiplier=-1).then_inc(consts_set, 1)
            nc.gpsimd.affine_select(out=after[:, :], in_=ones[:, :], compare_op=ALU.is_ge, fill=0.0, base=-1,
                                    pattern=[[-1, P]], channel_multiplier=1).then_inc(consts_set, 1)

            def add_squares(n):
                for k in range(DT):
                    pool.wait_ge(sq_ready, n * DT + k + 1)
                    if k == 0:
                        nc.gpsimd.tensor_copy(sumsq[:, :], sq[:, :]).then_inc(sumsq_ready, 1)
                    else:
                        pool.wait_ge(sumsq_ready, n * DT + k)
                        nc.gpsimd.tensor_tensor(sumsq[:, :], sumsq[:, :], sq[:, :], ALU.add).then_inc(sumsq_ready, 1)
            add_squares(0)
            pool.wait_ge(stats_ready, 1)
            add_squares(1)
            pool.wait_ge(xg_ready, 2 * DT)
            pool.dma_start(x_kept, x[:, :, :]).then_inc(x_saved, 16)

            pool.wait_ge(qb_landed, 16)
            with pool.Fori(0, NS // SLOTS) as i:
                for b in range(SLOTS):
                    pool.wait_ge(page_landed[b], 64 * i + 64)
                    tiles = pages[:, b, :, :].rearrange("p g (t f) -> p g t f", f=P)
                    query = qb[:, :, ds(SLOTS * i + b, 1), :].rearrange("p t o f -> p (o t) f")
                    nc.gpsimd.tensor_tensor(tiles, tiles, query.unsqueeze(1).broadcast_to([P, PAGES, SB_T, P]),
                                            ALU.mult).then_inc(kq_ready.sem, 1)

            pool.wait_ge(kq_ready.sem, kq_ready.now(NS // SLOTS - 1, SLOTS - 1))
            e2 = expand[:, :, :].rearrange("h t m -> h (t m)")
            link(nc.gpsimd.memset(e2, 1.0))
            link(nc.gpsimd.affine_select(out=e2, in_=e2, compare_op=ALU.is_ge, fill=0.0, base=0,
                                         pattern=[[1, SSD_T * P]], channel_multiplier=-HD))
            nc.gpsimd.affine_select(out=e2, in_=e2, compare_op=ALU.is_ge, fill=0.0, base=HD - 1,
                                    pattern=[[-1, SSD_T * P]], channel_multiplier=HD).then_inc(expand_set, 1)
            link(nc.gpsimd.memset(own[:, :, :], 0.0))
            link(nc.gpsimd.memset(token_rows[:, :], 0.0))
            for b in range(SLOTS):
                rows = slice(32 * b, 32 * b + 32)
                nc.gpsimd.affine_select(out=own[rows, :, :], in_=own[rows, :, :], compare_op=ALU.not_equal, fill=1.0,
                                        base=-SB_HEADS * b, pattern=[[-1, SB_HEADS], [0, HD]], channel_multiplier=1)
                last = nc.gpsimd.memset(token_rows[rows, b:b + 1], 1.0)
            last.then_inc(own_set, 1)

            pool.wait_ge(bc_row_ready, 1)
            pool.dma_start(bc_kept, bc_row[:, :]).then_inc(bc_row_kept, 16)
            def add_y(t):
                total = ysum[:, t // GT, :]
                pool.wait_ge(ysq_ready, t + 1)
                if t % GT == 0:
                    nc.gpsimd.tensor_copy(total, ysq[:, t % 2, :]).then_inc(ysum_ready, 1)
                else:
                    pool.wait_ge(ysum_ready, t)
                    nc.gpsimd.tensor_tensor(total, total, ysq[:, t % 2, :], ALU.add).then_inc(ysum_ready, 1)
            pool.wait_ge(pvd_done.sem, pvd_done.now(NS // SLOTS - 1, SLOTS - 1))
            pool.wait_ge(prep_a, 11)
            pool.wait_ge(prep_d, 7)
            pool.wait_ge(xdd_ready, 1)
            for t in range(SSD_T):
                pool.wait_ge(xd_ready.sem, xd_ready.now(0, t))
                pool.wait_ge(states_ready.sem, states_ready.now(0, t - 1))
                nc.gpsimd.tensor_tensor(xde[:, :, :].rearrange("p c (h d) -> p c h d", h=2),
                                        xd[:, t % 2, :, :].rearrange("p c (h d) -> p c h d", h=2),
                                        to_end[:, :, 2 * t:2 * t + 2].unsqueeze(3).broadcast_to([P, CH, 2, HD]),
                                        ALU.mult).then_inc(xde_ready.sem, 1)
                for e in range(2):
                    pool.wait_ge(ecs_ready.sem, ecs_ready.now(0, 2 * t + e))
                    nc.gpsimd.tensor_tensor(csc[:, e, :], csc[:, e, :], ct[:, t // GT, :], ALU.mult
                                            ).then_inc(csc_ready.sem, 1)
                k = t % 2
                pool.wait_ge(state_landed[k], 16 * (t // 2 + 1))
                link(nc.gpsimd.tensor_tensor(state[:, k, :, :], state[:, k, :, :],
                                             dtda[:, t, 1, :].unsqueeze(2).broadcast_to([P, NS, P]), ALU.mult))
                if t % GT == 0:
                    pool.wait_ge(bc_landed[0], 16 * (t // GT + 1))
                link(nc.gpsimd.tensor_tensor(outer[:, :, :], bb[:, :, :],
                                             xdd[:, t, :].unsqueeze(2).broadcast_to([P, NS, P]), ALU.mult))
                nc.gpsimd.tensor_tensor(state[:, k, :, :], state[:, k, :, :], outer[:, :, :], ALU.add
                                        ).then_inc(state_ready.sem, 1)
                if t >= GT:
                    for n in range(2 * (t - GT), 2 * (t - GT) + 2):
                        add_y(n)

            def load_back(n):
                c = n // 2 if n < 2 * DT else n - 2 * DT
                g = (1 + n % 2) * DT + c if n < 2 * DT else c
                slot = n % GATE_SLOTS
                if n >= GATE_SLOTS:
                    wait_output(pool, O_MERGE + n - GATE_SLOTS)
                pool.dma_start(gates[:, slot, :], gates_kept[:, g, :]).then_inc(gate_landed[slot], 16)
            pool.wait_ge(y_split, 2)
            gates_stored(pool, GATES - G_POST)
            for n in range(GATE_SLOTS):
                load_back(n)
            gates_stored(pool, GATES)
            for n in range(GATE_SLOTS, GATES):
                load_back(n)
            pool.wait_ge(y_split, 4)
            add_squares(2)

        @block.tensor
        def _(pe):
            def stats(n):
                pe.wait_ge(sumsq_ready, DT * (n + 1))
                for h in range(2):
                    mm = nc.tensor.matmul(ps[:, 4 + h, 0:HALF], ones[:, :], sumsq[:, h * HALF:(h + 1) * HALF],
                                          start=True, stop=True)
                mm.then_inc(stats_ready, 1)

            def ffn(n, u_a, o_a, u_b, o_b):
                for j in range(4):
                    multiply_unit(u_a + j, 0, o_a + j, 0, DT, xg,
                                  ready=(lambda k: (xg_ready, 2 * (n - 1) * DT + k + 1)) if j == 0 else None)
                    if j == 0:
                        stats(2 * (n - 1))
                with pe.Fori(0, FT // 2 - 1) as i:
                    for j in range(4):
                        multiply_unit(u_a + 4 + j, 4 * i, o_a + 4 + j, 4 * i, DT, xg)
                with pe.Fori(0, 2) as i:
                    for j in range(12):
                        k0, kt = DOWN_K[j % 3]
                        multiply_unit(u_b + j, 12 * i, o_b + j // 3, 4 * i, kt,
                                      lambda k: (hid_hi[:, k0 + k, :], hid_lo[:, k0 + k, :]), j % 3 == 0, j % 3 == 2,
                                      ready=(lambda k: (hid_ready, (n - 1) * FT + k0 + k + 1)) if j < 3 else None)

            pe.wait_ge(consts_set, CONSTS)
            ffn(1, U_FFN1A, O_FFN1A, U_FFN1B, O_FFN1B)
            multiply_unit(U_DT, 0, O_DT, 0, DT, xg, ready=lambda k: (xg_ready, DT + k + 1))
            stats(1)

            with pe.Fori(0, SB_T) as t:
                def unit(j):
                    multiply_unit(U_ATT + j, 8 * t, O_ATT + j, 8 * t, DT, xg)

                def head_sums(k, src):
                    pe.wait_ge(qk_squared.sem, qk_squared.now(t, k))
                    if k == 0:
                        pe.wait_ge(tail_taken.sem, tail_taken.before(t, 1))
                    else:
                        pe.wait_ge(yc_ready.sem, yc_ready.before(t))
                    for h in range(2):
                        mm = nc.tensor.matmul(ps[:, 4 + 2 * k + h, 0:HALF], blocks[:, :],
                                              src[:, h * HALF:(h + 1) * HALF], start=True, stop=True)
                    mm.then_inc(qk_summed.sem, 1)

                def scores(e):
                    pe.wait_ge(qk_normed.sem, qk_normed.now(t, 1))
                    if e:
                        pe.wait_ge(tail_taken.sem, tail_taken.now(t, 0))
                    rows = slice(HD * e, HD * e + HD)
                    for j in range(CH):
                        mm = nc.tensor.matmul(flat[:, 2048 + SCORE_AT[j]:2048 + SCORE_AT[j] + SCORE_W[j]],
                                              kh[rows, P * j:P * j + P], qh[rows, P * j:NP], start=True, stop=True)
                    mm.then_inc(scored.sem, 1)

                def tails(e):
                    pe.wait_ge(sp_ready.sem, sp_ready.now(t, e))
                    for j in range(CH):
                        at = SCORE_AT[j]
                        mm = nc.tensor.matmul(flat[:, 2048 + at:2048 + at + SCORE_W[j]], after[:, :],
                                              spl[:, e, at:at + SCORE_W[j]], start=True, stop=j == CH - 1)
                        for later in range(j + 1, CH):
                            skip = P * (later - j)
                            mm = nc.tensor.matmul(flat[:, 2048 + at + skip:2048 + at + SCORE_W[j]], ones[:, :],
                                                  spl[:, e, SCORE_AT[later]:SCORE_AT[later] + SCORE_W[later]],
                                                  start=False, stop=later == CH - 1)
                    mm.then_inc(tail_summed.sem, 1)

                def values(e):
                    pe.wait_ge(w_ready.sem, w_ready.now(t, e))
                    pe.wait_ge(v_tok_ready.sem, v_tok_ready.now(t))
                    cols = slice(HD * e, HD * e + HD)
                    for j in range(CH):
                        mm = nc.tensor.matmul(ps[cols, 7, P * j:NP], v_tok[:, j, cols],
                                              zb[:, e, SCORE_AT[j]:SCORE_AT[j] + SCORE_W[j]],
                                              start=j == 0, stop=j == CH - 1)
                    mm.then_inc(pv_done.sem, 1)

                unit(0)
                unit(1)
                head_sums(0, sq)
                unit(2)
                head_sums(1, prod)
                unit(3)
                scores(0)
                unit(4)
                wait_output(pe, O_ATT + 2, 8 * t)
                pe.wait_ge(qk_root.sem, qk_root.now(t, 1))
                for c in range(CH):
                    mm = nc.tensor.transpose(ps[:, 7, P * c:P * c + P], vr[:, P * c:P * c + P], ident[:, :])
                mm.then_inc(v_turned.sem, 1)
                tails(0)
                unit(5)
                scores(1)
                unit(6)
                values(0)
                tails(1)
                unit(7)
                values(1)

            def gate(g, step=0, first=(U_GATE, O_GATE)):
                multiply_unit(first[0] + g, step, first[1] + g, step, DT, xg)
            nc.tensor.transpose(ps[0:SB_T * NS, 4, 0:P], qdec[:, :, :].rearrange("p t b -> p (t b)"), ident[:, :]
                                ).then_inc(q_turned, 1)
            for g in range(G_PRE):
                gate(g)
            with pe.Fori(0, NS // SLOTS) as i:
                for b in range(SLOTS):
                    gate(G_PRE + b, SLOTS * i)
            R = SSD_HEADS
            pe.wait_ge(prep_d, 3)
            for c in range(CH):
                for bank, src in ((4, dt_t), (5, la_t)):
                    mm = nc.tensor.transpose(ps[:, bank, R * c:R * c + R], src[:, P * c:P * c + P], ident[0:R, 0:R])
            mm.then_inc(prep_p, 1)
            gate(G0_PREP)
            pe.wait_ge(prep_d, 4)
            lt = la_tok[:, :, :].rearrange("p c h -> p (c h)")
            nc.tensor.matmul(ps[:, 4, 0:CH * R], upto[:, :], lt, start=True, stop=True)
            nc.tensor.matmul(ps[:, 7, 0:CH * R], ones[:, :], lt, start=True, stop=True).then_inc(prep_p, 1)
            pe.wait_ge(spd_ready, 1)
            W8 = NS * SB_HEADS
            for g in range(PAGES):
                for later in range(g, PAGES):
                    mm = nc.tensor.matmul(ps[:, 6, W8 * g:W8 * g + W8], (after if later == g else ones)[:, :],
                                          spd[:, later, :, :].rearrange("p b h -> p (b h)"), start=later == g,
                                          stop=later == PAGES - 1)
            mm.then_inc(taild_ready, 1)
            gate(G0_PREP + 1)
            pe.wait_ge(prep_d, 5)
            for c in range(CH):
                nc.tensor.transpose(ps[0:R, 4, P * c:P * c + P], cs_tok[:, c, :], ident[:, :])
            pe.wait_ge(expand_set, 1)
            pe.wait_ge(prep_a, 4)
            for t in range(SSD_T):
                mm = nc.tensor.matmul(ps[:, 5, 2 * NS * t:2 * NS * t + 2 * NS], expand[:, t, :],
                                      dtda_t[:, :, :].rearrange("p k b -> p (k b)"), start=True, stop=True)
            mm.then_inc(prep_p, 1)
            pe.wait_ge(prep_d, 7)
            pe.wait_ge(prep_a, 9)
            nc.tensor.transpose(ps[0:2 * GROUPS * NS, 4, 0:P], cdec[:, SSD_T:XBC_T, :].rearrange("p t b -> p (t b)"),
                                ident[:, :]).then_inc(bc_turned, 1)

            pe.wait_ge(wd_ready, 1)
            pe.wait_ge(prep_a, 11)
            with pe.Fori(0, NS // SLOTS) as i:
                for b in range(SLOTS):
                    gate(G0_V + b, SLOTS * i)
                    pe.wait_ge(page_landed[b], 64 * i + 64 * (NS // SLOTS + 1))
                    pe.wait_ge(wd4_ready.sem, wd4_ready.now(i))
                    rows = slice(4 * SB_HEADS * b, 4 * SB_HEADS * (b + 1))
                    for g in range(PAGES):
                        mm = nc.tensor.matmul(ps[rows, 7, :], wd4[:, g, :],
                                              pages[:, b, g, :], start=g == 0, stop=g == PAGES - 1)
                    mm.then_inc(pvd_done.sem, 1)
            for g in range(GROUPS):
                for c in range(CH):
                    mm = nc.tensor.transpose(ps[:, 4 + g, P * c:P * c + P], bt[:, g, P * c:P * c + P], ident[:, :])
                mm.then_inc(b_turned, 1)
            pe.wait_ge(own_v_ready, NS // SLOTS)
            for i in range(NS // SLOTS):
                for t in range(SB_T):
                    mm = nc.tensor.matmul(ps[:, 6, SLOTS * (SB_T * i + t):SLOTS * (SB_T * i + t + 1)],
                                          own_v[:, i, P * t:P * t + P], token_rows[:, :], start=True, stop=True)
            mm.then_inc(v_summed, 1)
            for g in range(GROUPS):
                if g:
                    pe.wait_ge(yc_sampled, 1)
                for c in range(CH):
                    cols = slice(P * c, P * c + P)
                    mm = nc.tensor.matmul(ps[:, 7 - g, cols], bt[:, g, cols], ct[:, g, cols], start=True, stop=True)
                mm.then_inc(cb_made, 1)
            pe.wait_ge(b_tok_ready, GROUPS)
            pe.wait_ge(cb_ready, GROUPS)

            def spread(t, e):
                pe.wait_ge(head_cs_ready.sem, head_cs_ready.now(0, 2 * t + e))
                nc.tensor.matmul(ps[:, (6, 4)[e], :], ones[0:R, :], head_cs[e], start=True, stop=True
                                 ).then_inc(cs_spread.sem, 1)

            pe.wait_ge(xs_ready.sem, xs_ready.now(NS // SLOTS - 1, SLOTS - 1))
            def turn(t):
                if t:
                    pe.wait_ge(g_ready.sem, g_ready.now(0, 2 * t - 1))
                    pe.wait_ge(csc_ready.sem, csc_ready.now(0, 2 * t - 1))
                for c in range(CH):
                    mm = nc.tensor.transpose(ps[:, 4, P * c:P * c + P], x_tile(t)[:, P * c:P * c + P], ident[:, :])
                mm.then_inc(xs_turned.sem, 1)

            turn(0)
            spread(0, 0)
            for t in range(SSD_T):
                u, o = U_SSD + 3 * (t // 2), O_SSD + 3 * (t // 2)
                pe.wait_ge(xd_ready.sem, xd_ready.now(0, t))
                spread(t, 1)
                pe.wait_ge(xde_ready.sem, xde_ready.now(0, t))
                pe.wait_ge(hin_ready.sem, hin_ready.now(0, t - 1))
                for c in range(CH):
                    mm = nc.tensor.matmul(ps[:, 5, P * c:P * c + P], b_tok[:, t // GT, c, :], xde[:, c, :], start=True,
                                          stop=True)
                mm.then_inc(states_ready.sem, 1)
                for j in ((0,), (1, 2))[t % 2]:
                    multiply_unit(u + j, 0, o + j, 0, DT, xg)
                for e in range(2):
                    pe.wait_ge(g_ready.sem, g_ready.now(0, 2 * t + e))
                    pe.wait_ge(csc_ready.sem, csc_ready.now(0, 2 * t + e))
                    if e == 0:
                        pe.wait_ge(hin_ready.sem, hin_ready.now(0, t))
                        pe.wait_ge(y_ready.sem, y_ready.now(0, t - 1))
                    rows = slice(HD * e, HD * e + HD)
                    for c in range(CH):
                        cols = slice(P * c, P * c + P)
                        nc.tensor.matmul(ps[rows, 7, cols], xd[:, t % 2, c, rows], gbuf[:, e, cols], start=True, stop=False)
                        mm = nc.tensor.matmul(ps[rows, 7, cols], hin[:, c, rows], csc[:, e, cols], start=False,
                                              stop=True)
                    if e == 0 and t < SSD_T - 1:
                        turn(t + 1)
                        spread(t + 1, 0)
                mm.then_inc(y_summed.sem, 1)

            for g in range(GATES - G_POST, GATES):
                gate(g, first=(U_POST - (GATES - G_POST), O_POST - (GATES - G_POST)))

            pe.wait_ge(ysum_ready, SSD_T)
            for g in range(GROUPS):
                for h in range(2):
                    mm = nc.tensor.matmul(ps[:, 4 + 2 * g + h, 0:HALF], ones[:, :],
                                          ysum[:, g, h * HALF:(h + 1) * HALF], start=True, stop=True)
                mm.then_inc(ysum_spread, 1)
            with pe.Fori(0, DT // 2) as i:
                for c in range(2):
                    u, o = U_MERGE + c, O_MERGE + 2 * c
                    r = u % SPLITS
                    pe.wait_ge(unit_split, STAGES + u + 1 + 2 * i)
                    for n in range(2):
                        pe.wait_ge(y_split, n + 1)
                        pe.wait_ge(acc_read, o + n + 1 + 4 * i)
                        for k in range(4):
                            for m, (wt, v) in enumerate(((w_hi, y_hi), (w_hi, y_lo), (w_lo, y_hi))):
                                for h in range(2):
                                    mm = nc.tensor.matmul(acc(o + n)[:, h, :], wt[:, r, 4 * n + k, :],
                                                          v[:, 8 + 4 * n + k, h * HALF:(h + 1) * HALF],
                                                          start=k == 0 and m == 0, stop=k == 3 and m == 2)
                        mm.then_inc((b_done, unit_done)[n], 1)
            with pe.Fori(0, DT // 2) as i:
                for c in range(2):
                    multiply_unit(U_MERGE_A + c, 2 * i, O_MERGE_A + c, 2 * i, DT,
                                  lambda k: (y_hi[:, k, :], y_lo[:, k, :]), ready=lambda k: (y_split, 3 + k // GT))
            with pe.Fori(0, 2) as i:
                for j in range(4):
                    multiply_unit(U_OUT + j, 4 * i, O_OUT + j, 4 * i, DT, lambda k: (m_hi[:, k, :], m_lo[:, k, :]),
                                  ready=(lambda k: (m_ready, k + 1)) if j == 0 else None)
            ffn(2, U_FFN2A, O_FFN2A, U_FFN2B, O_FFN2B)


def kernel(**inputs):
    import numpy as np
    import concourse.bacc as bacc
    from concourse.bass_utils import run_bass_kernel_spmd as run

    a = {k: np.asarray(v) for k, v in inputs.items()}

    def cols(v):
        return v.reshape(-1, P).T

    def flat(parts):
        return np.ascontiguousarray(np.stack(parts, 1))
    tok = np.concatenate([a["x_prompt"].reshape(-1, D), a["x_sample"].reshape(-1, D)], 0)
    laid = {
        "x_t": np.ascontiguousarray(tok.T.reshape(DT, P, T).transpose(1, 0, 2)),
        "norms": flat([cols(a["ffn1_norm"]), cols(a["mix_norm"]), cols(a["ffn2_norm"])]),
        "gate_b": np.ascontiguousarray(cols(a["gate_bias"])),
        "conv_w": flat([cols(a["ssd_conv_w"][0, k]) for k in range(4)] + [cols(a["ssd_conv_b"])]),
        "sc_w": flat([cols(a["sc_conv_w"][0, k]) for k in range(3)]),
        "qk_g": np.ascontiguousarray(np.stack([np.tile(a["sb_q_norm"][0], 2), np.tile(a["sb_k_norm"][0], 2)], 1)),
        "ssd_cols": flat([cols(np.repeat(a["ssd_d"][0], HD)), cols(a["ssd_norm"])]),
        "ssd_rows": np.ascontiguousarray(np.stack([a["ssd_dt_bias"][0], a["ssd_a_log"][0]], 1)),
        "table": a["page_table"].reshape(1, -1),
        "sb_bias": a["sb_logit_bias"].reshape(-1),
        "ssd_prev": np.ascontiguousarray(a["state_ssd_conv"][0].reshape(NS, 3, XBC_T, P).transpose(3, 2, 1, 0)),
        "sc_prev": np.ascontiguousarray(a["state_sc_conv"][0].reshape(NS, 2, SC_T, P).transpose(3, 2, 1, 0)),
    }
    laid["w_proj_bc"] = np.concatenate([a["w_proj_b"], a["w_proj_c"]], 1)
    for name in ("cache_sb_k", "cache_sb_v", "state_ssd", "ffn1_w_gate", "ffn1_w_up", "ffn1_w_down", "w_in",
                 "w_proj_a", "w_out", "ffn2_w_gate", "ffn2_w_up", "ffn2_w_down"):
        laid[name] = a[name]
    shapes = {"y_t": (P, DT, T), "k_t": (P, SB_T, T), "v_t": (P, SB_T, T), "ssd_p": (P, SSD_T * P),
              "ssd_s": (1, NS, SSD_HEADS, HD, P), "ssd_conv_p": (P, XBC_T, 3), "ssd_conv_s": (P, XBC_T, 3, NS),
              "sc_conv_p": (P, SC_T, 2), "sc_conv_s": (P, SC_T, 2, NS)}
    nc = bacc.Bacc("TRN2", target_bir_lowering=False, num_devices=1)
    ins = {k: nc.dram_tensor("in_" + k, v.shape, mybir.dt.from_np(v.dtype), kind="ExternalInput").ap()
           for k, v in laid.items()}
    outs = {k: nc.dram_tensor("out_" + k, s, F32, kind="ExternalOutput").ap() for k, s in shapes.items()}
    build(nc, ins, outs)
    r = run(nc, [{"in_" + k: v for k, v in laid.items()}], core_ids=[0]).results[0]

    def tokens(name):
        v = r["out_" + name].transpose(2, 1, 0).reshape(T, -1)
        return v[:NP], v[NP:]
    (yp, ys), (kp, ks), (vp, vs) = tokens("y_t"), tokens("k_t"), tokens("v_t")
    return (yp.reshape(1, NP, D), ys.reshape(NS, 1, D),
            kp.reshape(1, 1, NP, SB_HEADS, HD), vp.reshape(1, 1, NP, SB_HEADS, HD),
            ks.reshape(1, NS, 1, SB_HEADS, HD), vs.reshape(1, NS, 1, SB_HEADS, HD),
            r["out_ssd_p"].T.reshape(1, 1, SSD_HEADS, HD, P), r["out_ssd_s"],
            r["out_ssd_conv_p"].transpose(2, 1, 0).reshape(1, 1, 3, XBC_T * P),
            r["out_ssd_conv_s"].transpose(3, 2, 1, 0).reshape(1, NS, 3, XBC_T * P),
            r["out_sc_conv_p"].transpose(2, 1, 0).reshape(1, 1, 2, SC_T * P),
            r["out_sc_conv_s"].transpose(3, 2, 1, 0).reshape(1, NS, 2, SC_T * P))
```

```python
from contextlib import ExitStack

import concourse.bass as bass
from concourse import mybir

F32 = mybir.dt.float32
F32R = mybir.dt.float32r
I32 = mybir.dt.int32
ALU = mybir.AluOpType
ACT = mybir.ActivationFunctionType
AX_X = mybir.AxisListType.X
ds = bass.ds

P = 128
D = 1024
NP = 512
NS = 8
T = NP + NS
HALF = T // 2
DT = D // P
D_FF = 2816
FT = D_FF // P
EPS = 1e-6
HD = 64
SB_HEADS = 8
SB_T = SB_HEADS * HD // P
PAGES = 4
SSD_HEADS = 16
SSD_T = SSD_HEADS * HD // P
GROUPS = 2
GT = SSD_T // GROUPS
CH = NP // P
XBC_T = SSD_T + 2 * GROUPS
SC_T = 4

COL_GATE = 0
COL_Z = 3 * D
COL_XBC = COL_Z + D
COL_DT = COL_XBC + XBC_T * P
COL_SCB = COL_DT + SSD_HEADS
COL_SCC = COL_SCB + SC_T * P
COL_SCX = COL_SCC + SC_T * P
COL_Q = COL_SCX + SC_T * P
COL_K = COL_Q + SB_T * P
COL_V = COL_K + SB_T * P

KMAX = 8
STAGES = 4
SPLITS = 2
DOWN_K = [(0, 8), (8, 7), (15, 7)]
GATES = 3 * DT
G_PRE, G_K, G_V, G_POST = 4, NS, NS, 2
G_PREP = GATES - G_PRE - G_K - G_V - G_POST
G0_PREP = G_PRE + G_K
G0_V = G0_PREP + G_PREP
GATE_SLOTS = 4
SLOTS = 4

U_FFN1A, O_FFN1A = 0, 0
U_FFN1B, O_FFN1B = 2 * FT, 2 * FT
U_DT, O_DT = U_FFN1B + 3 * DT, O_FFN1B + DT
U_ATT, O_ATT = U_DT + 1, O_DT + 1
U_GATE, O_GATE = U_ATT + 8 * SB_T, O_ATT + 8 * SB_T
U_SSD, O_SSD = U_GATE + GATES - G_POST, O_GATE + GATES - G_POST
U_POST, O_POST = U_SSD + 3 * SC_T, O_SSD + 3 * SC_T
U_MERGE, O_MERGE = U_POST + G_POST, O_POST + G_POST
U_MERGE_A, O_MERGE_A = U_MERGE + DT, O_MERGE + 2 * DT
U_OUT, O_OUT = U_MERGE_A + DT, O_MERGE_A + DT
U_FFN2A, O_FFN2A = U_OUT + DT, O_OUT + DT
U_FFN2B, O_FFN2B = U_FFN2A + 2 * FT, O_FFN2A + 2 * FT
U_END = U_FFN2B + 3 * DT

SCORE_AT = [0, 512, 1024, 896]
SCORE_W = [512, 384, 256, 128]
SCORES = 1280
SCORE_PARTS = (slice(640, SCORES), slice(0, 640))
CONSTS = 6


class Signal:

    def __init__(self, sem, n):
        self.sem, self.n = sem, n

    def now(self, i, k=0):
        return self.n * i + (self.n + k + 1)

    def before(self, i, k=0):
        return self.n * i + (k + 1)


class Chain:

    def __init__(self, eng, sem):
        self.eng, self.sem, self.n, self.step = eng, sem, 0, 0

    def __call__(self, ins):
        ins.then_inc(self.sem, 1)
        self.n += 1
        self.eng.wait_ge(self.sem, self.n + self.step)

    def loop(self, i, per):
        self.step, self.first, self.per = per * i, self.n, per

    def end(self, turns):
        assert self.n == self.first + self.per, (self.n - self.first, self.per)
        self.step, self.n = 0, self.first + self.per * turns


def build(nc, ins, outs):
    ctx = ExitStack()
    with ctx:
        def sb(name, shape, dt=F32):
            return ctx.enter_context(nc.sbuf_tensor(name, shape, dt))

        def sem(name):
            return ctx.enter_context(nc.semaphore(name))

        ARENA = 128 * 1024
        arena_at = (nc.sbuf_base + 31) // 32 * 32
        arena = sb("arena", [P, ARENA // 4])
        xg_hi = sb("xg_hi", [P, DT, T], F32R)
        xg_lo = sb("xg_lo", [P, DT, T], F32R)
        stage = sb("stage", [P, STAGES, KMAX, P])
        w_hi = sb("w_hi", [P, SPLITS, KMAX, P], F32R)
        w_lo = sb("w_lo", [P, SPLITS, KMAX, P], F32R)
        rstd = sb("rstd", [P, T])
        sumsq = sb("sumsq", [P, T])
        sq = sb("sq", [P, T])
        silu = sb("silu", [P, T])
        prod = sb("prod", [P, T])
        ones = sb("ones", [P, P])
        ident = sb("ident", [P, P])
        upto = sb("upto", [P, P])
        after = sb("after", [P, P])
        ones_r = sb("ones_r", [P, P], F32R)
        after_r = sb("after_r", [P, P], F32R)
        blocks = sb("blocks", [P, P])
        norms = sb("norms", [P, 3, DT])
        gate_b = sb("gate_b", [P, 3 * DT])
        conv_w = sb("conv_w", [P, 5, XBC_T])
        sc_w = sb("sc_w", [P, 3, SC_T])
        qk_g = sb("qk_g", [P, 2])
        sb_bias = sb("sb_bias", [P, SB_HEADS])
        ssd_cols = sb("ssd_cols", [P, 2, SSD_T])
        ssd_rows = sb("ssd_rows", [SSD_HEADS, 2])
        eps = sb("eps", [P, 1])
        one = sb("one", [P, 1])
        table = sb("table", [1, NS * PAGES], I32)
        ps = ctx.enter_context(nc.psum_tensor("ps", [P, 8, 512], F32))
        flat = ps[:, :, :].rearrange("p b c -> p (b c)")

        def plan(at, *tenants):
            made = []
            for name, shape, dt in tenants:
                size = 4
                for n in shape[1:]:
                    size *= n
                made.append(nc.alloc_sbuf_tensor_at(name, shape, dt, offset=arena_at + at))
                at += (size + 31) // 32 * 32
            assert at <= ARENA, (tenants[0][0], at, ARENA)
            return made + [at]
        x, after_x = plan(0, ("x", [P, DT, T], F32))
        hid_hi, hid_lo, _ = plan(after_x, ("hid_hi", [P, FT, T], F32R), ("hid_lo", [P, FT, T], F32R))
        m_hi, m_lo, y_hi, y_lo, _ = plan(ARENA - 4 * T * 48, ("m_hi", [P, DT, T], F32R), ("m_lo", [P, DT, T], F32R),
                                         ("y_hi", [P, 16, T], F32R), ("y_lo", [P, 16, T], F32R))
        part, _ = plan(ARENA - 4 * T * 40, ("part", [P, DT, T], F32))
        gates, end_gates = plan(after_x, ("gates", [P, GATE_SLOTS, T], F32))
        assert end_gates <= ARENA - 4 * T * 48
        zs, yb, yc, xb, qdec, dt_t, la_t, end_branch = plan(
            0, ("zs", [P, SSD_T, T], F32), ("yb", [P, SC_T, T], F32), ("yc", [P, SB_T, T], F32),
            ("xb", [P, XBC_T, 3 + T], F32), ("qdec", [P, SB_T, NS], F32), ("dt_t", [SSD_HEADS, T], F32),
            ("la_t", [SSD_HEADS, T], F32))
        ysq, ysum, _ = plan(4 * T * (SSD_T + SB_T + SC_T), ("ysq", [P, 2, T], F32), ("ysum", [P, GROUPS, T], F32))
        qr, kr, vr, qh, kh, v_tok, zb, lg, spl, strict, spl_hi, spl_lo, _ = plan(
            end_branch, ("qr", [P, T], F32), ("kr", [P, T], F32), ("vr", [P, T], F32), ("qh", [P, T], F32),
            ("kh", [P, T], F32), ("v_tok", [P, CH, P], F32), ("zb", [P, 2, SCORES], F32),
            ("lg", [P, 2, SCORES], F32), ("spl", [P, 2, SCORES], F32), ("strict", [P, P], F32),
            ("spl_hi", [P, 2, SCORES], F32R), ("spl_lo", [P, 2, SCORES], F32R))
        pages, q_row, qb, zd, lgd, spd, end_sample = plan(
            end_branch, ("pages", [P, SLOTS, PAGES, 512], F32), ("q_row", [SB_T * NS, P], F32),
            ("qb", [P, SB_T, NS, P], F32), ("zd", [P, PAGES, NS, SB_HEADS], F32),
            ("lgd", [P, PAGES, NS, SB_HEADS], F32), ("spd", [P, PAGES, NS, SB_HEADS], F32))
        expand, own, own_v, token_rows, wd4, at_ = plan(
            end_sample - 4 * 3 * 256 - 4 * NS * 512, ("expand", [SSD_HEADS, SSD_T, P], F32),
            ("own", [P, SB_HEADS, HD], F32), ("own_v", [P, NS // SLOTS, SB_HEADS * HD], F32),
            ("token_rows", [P, SLOTS], F32), ("wd4", [P, PAGES, SLOTS * SB_HEADS], F32))
        assert at_ <= end_sample - 4 * 3 * 256
        (bt, ct, dt_tok, la_tok, cs_tok, to_end, ch_dec, cs_t, sprev, scprev, cdec, ctmp, dtda, dtda_t, xdd, bc_row,
         sel_1, _) = plan(
            end_sample, ("bt", [P, GROUPS, NP], F32), ("ct", [P, GROUPS, NP], F32),
            ("dt_tok", [P, CH, SSD_HEADS], F32), ("la_tok", [P, CH, SSD_HEADS], F32),
            ("cs_tok", [P, CH, SSD_HEADS], F32), ("to_end", [P, CH, SSD_HEADS], F32),
            ("ch_dec", [P, CH, SSD_HEADS], F32), ("cs_t", [SSD_HEADS, T], F32),
            ("sprev", [P, XBC_T, 3, NS], F32), ("scprev", [P, SC_T, 2, NS], F32), ("cdec", [P, XBC_T, NS], F32),
            ("ctmp", [P, XBC_T, NS], F32), ("dtda", [P, SSD_T, 2, NS], F32), ("dtda_t", [SSD_HEADS, 2, NS], F32),
            ("xdd", [P, SSD_T, NS], F32), ("bc_row", [2 * GROUPS * NS, P], F32),
            ("sel_1", [SSD_HEADS, P], F32R))
        (sctail, b_tok, cb, xd, xde, hin, gbuf, csc, state, stmp, outer, bb, cbb, ydec, scx, sel_0, end_ssd) = plan(
            end_branch, ("sctail", [P, SC_T, 2 + NS], F32), ("b_tok", [P, GROUPS, CH, P], F32), ("cb", [P, GROUPS, NP], F32),
            ("xd", [P, 2, CH, P], F32), ("xde", [P, CH, P], F32),
            ("hin", [P, CH + 1, P], F32), ("gbuf", [P, 2, NP], F32), ("csc", [P, 2, NP], F32),
            ("state", [P, 2, NS, P], F32), ("stmp", [P, NS, P], F32), ("outer", [P, NS, P], F32), ("bb", [P, NS, P], F32),
            ("cbb", [P, NS, P], F32), ("ydec", [P, NS], F32), ("scx", [P, 2 + T], F32),
            ("sel_0", [SSD_HEADS, P], F32R))
        assert end_ssd <= end_sample
        cs_hi, cs_lo, _ = plan(end_branch - 2 * 4 * T, ("cs_hi", [SSD_HEADS, T], F32R), ("cs_lo", [SSD_HEADS, T], F32R))
        heads_sel = sel_0, sel_1

        def x_tile(t):
            return xb[:, t, 0:NP]
        x_kept = nc.dram_tensor("x_kept", (P, DT, T), F32, kind="Internal").ap()
        bc_kept = nc.dram_tensor("bc_kept", (2 * GROUPS * NS, P), F32, kind="Internal").ap()
        q_kept = nc.dram_tensor("q_kept", (SB_T * NS, P), F32, kind="Internal").ap()
        gates_kept = nc.dram_tensor("gates_kept", (P, GATES, T), F32, kind="Internal").ap()

        row_e, row_s, row_l = sq[0:SSD_HEADS, :], sumsq[0:SSD_HEADS, :], cs_t[:, :]

        def acc(o):
            return ps[:, 2 * (o % 2):2 * (o % 2) + 2, 0:HALF]

        def halves(ap):
            return ap.rearrange("p (a b) -> p a b", a=2)

        landed = sem("landed")
        norms_landed = sem("norms_landed")
        x_landed = [sem(f"x_landed{k}") for k in range(DT)]
        consts_set = sem("consts_set")
        w_landed = [sem(f"w_landed{s}") for s in range(STAGES)]
        unit_split = sem("unit_split")
        hi_ready = sem("hi_ready")
        unit_done = sem("unit_done")
        acc_read = sem("acc_read")
        silu_ready = sem("silu_ready")
        hid_hi_ready = sem("hid_hi_ready")
        hid_ready = sem("hid_ready")
        xg_hi_ready = sem("xg_hi_ready")
        xg_ready = sem("xg_ready")
        sq_ready = sem("sq_ready")
        sumsq_ready = sem("sumsq_ready")
        stats_ready = sem("stats_ready")
        rms_ready = sem("rms_ready")
        rstd_ready = sem("rstd_ready")
        x_saved = sem("x_saved")
        x_back = sem("x_back")
        out_written = sem("out_written")
        dve_step = sem("dve_step")
        act_step = sem("act_step")
        pool_step = sem("pool_step")
        signals = []

        def signal(name, n):
            signals.append(Signal(sem(name), n))
            return signals[-1]
        qk_squared = signal("qk_squared", 2)
        qk_summed = signal("qk_summed", 2)
        qk_root = signal("qk_root", 2)
        qk_normed = signal("qk_normed", 2)
        kv_written = sem("kv_written")
        v_turned = signal("v_turned", 1)
        v_tok_ready = signal("v_tok_ready", 1)
        scored = signal("scored", 2)
        z_biased = signal("z_biased", 4)
        log_ready = signal("log_ready", 4)
        sums_rounded = sem("sums_rounded")
        sp_made = signal("sp_made", 4)
        sp_hi_ready = signal("sp_hi_ready", 4)
        sp_ready = signal("sp_ready", 4)
        tail_summed = signal("tail_summed", 2)
        tail_taken = signal("tail_taken", 2)
        w_exped = signal("w_exped", 2)
        w_ready = signal("w_ready", 2)
        pv_done = signal("pv_done", 2)
        yc_ready = signal("yc_ready", 1)
        page_landed = [sem(f"page_landed{b}") for b in range(SLOTS)]
        q_turned = sem("q_turned")
        q_row_ready = sem("q_row_ready")
        q_row_kept = sem("q_row_kept")
        qb_landed = sem("qb_landed")
        pages_used = signal("pages_used", SLOTS)
        kq_ready = signal("kq_ready", SLOTS)
        gate_kept = [sem("gate_kept0"), sem("gate_kept1")]
        spd_ready = sem("spd_ready")
        zd_ready = sem("zd_ready")
        lgd_ready = sem("lgd_ready")
        taild_ready = sem("taild_ready")
        wd_raw = sem("wd_raw")
        wd_ready = sem("wd_ready")
        wd4_ready = signal("wd4_ready", 1)
        own_set = sem("own_set")
        own_v_ready = sem("own_v_ready")
        v_summed = sem("v_summed")
        pvd_done = signal("pvd_done", SLOTS)
        expand_set = sem("expand_set")
        bc_conved = sem("bc_conved")
        b_turned = sem("b_turned")
        b_tok_ready = sem("b_tok_ready")
        cb_made = sem("cb_made")
        cb_ready = sem("cb_ready")
        yc_sampled = sem("yc_sampled")
        bc_turned = sem("bc_turned")
        bc_row_ready = sem("bc_row_ready")
        bc_row_kept = sem("bc_row_kept")
        bc_landed = [sem("b_landed"), sem("c_landed")]
        prep_d = sem("prep_d")
        prep_a = sem("prep_a")
        s_used = sem("s_used")
        inverse_ready = sem("inverse_ready")
        prep_p = sem("prep_p")
        conv_in = sem("conv_in")
        zs_ready = sem("zs_ready")
        cdec_conved = sem("cdec_conved")
        cdec_ready = sem("cdec_ready")
        bc_silued = sem("bc_silued")
        xdd_ready = sem("xdd_ready")
        conv_ready = signal("conv_ready", SLOTS)
        xs_ready = signal("xs_ready", SLOTS)
        xs_turned = signal("xs_turned", 2)
        xd_ready = signal("xd_ready", 2)
        xde_ready = signal("xde_ready", 2)
        states_ready = signal("states_ready", 2)
        hin_ready = signal("hin_ready", 2)
        hfin_written = [sem("hfin_written0"), sem("hfin_written1")]
        sel_ready = signal("sel_ready", 4)
        cs_spread = signal("cs_spread", 4)
        seg_ready = signal("seg_ready", 4)
        decay_ready = signal("decay_ready", 4)
        ecs_ready = signal("ecs_ready", 4)
        csc_ready = signal("csc_ready", 4)
        g_ready = signal("g_ready", 4)
        y_summed = signal("y_summed", 2)
        y_ready = signal("y_ready", 2)
        state_landed = [sem("state_landed0"), sem("state_landed1")]
        state_written = [sem("state_written0"), sem("state_written1")]
        state_decayed = signal("state_decayed", 2)
        state_ready = signal("state_ready", 2)
        cs_state_ready = signal("cs_state_ready", 2)
        sample_done = signal("sample_done", 2)
        ysq_ready = sem("ysq_ready")
        ysum_ready = sem("ysum_ready")
        ysum_spread = sem("ysum_spread")
        yroot_ready = sem("yroot_ready")
        yprod_ready = sem("yprod_ready")
        yhi_ready = sem("yhi_ready")
        y_split = sem("y_split")
        gate_landed = [sem(f"gate_landed{b}") for b in range(GATE_SLOTS)]
        gate_open = sem("gate_open")
        b_done = sem("b_done")
        merged = sem("merged")
        m_hi_ready = sem("m_hi_ready")
        m_ready = sem("m_ready")

        def kpm(w):
            return w.rearrange("l (k p) m -> (l p) k m", p=P)
        w = {n: kpm(ins[n]) for n in ("ffn1_w_gate", "ffn1_w_up", "ffn1_w_down", "w_in", "w_proj_a", "w_proj_bc", "w_out",
                                      "ffn2_w_gate", "ffn2_w_up", "ffn2_w_down")}

        def load_unit(u0, step, src, kt):
            s = u0 % STAGES
            nc.sync.wait_ge(unit_split, u0 + 1 + step)
            nc.sync.dma_start(stage[:, s, 0:kt, :], src).then_inc(w_landed[s], 16)

        def round_unit(u0, step, kt):
            s, r = u0 % STAGES, u0 % SPLITS
            nc.scalar.wait_ge(w_landed[s], 16 * (u0 // STAGES + 1) + 16 // STAGES * step)
            nc.scalar.wait_ge(unit_done, u0 + 1 + step)
            nc.scalar.activation(w_hi[:, r, 0:kt, :], stage[:, s, 0:kt, :], ACT.Copy).then_inc(hi_ready, 1)

        def rest_unit(u0, step, kt):
            s, r = u0 % STAGES, u0 % SPLITS
            nc.vector.wait_ge(hi_ready, u0 + 1 + step)
            nc.vector.tensor_tensor(w_lo[:, r, 0:kt, :], stage[:, s, 0:kt, :], w_hi[:, r, 0:kt, :].bitcast(F32),
                                    ALU.subtract).then_inc(unit_split, 1)

        def multiply_unit(u0, step, o0, ostep, kt, rhs, start=True, stop=True, ready=None, span=None):
            r = u0 % SPLITS
            out = acc(o0)
            begin, end = span or (0, kt)
            if begin == 0:
                if start:
                    nc.tensor.wait_ge(acc_read, o0 + 1 + ostep)
                nc.tensor.wait_ge(unit_split, STAGES + u0 + 1 + step)
            for k in range(begin, end):
                hi, lo = rhs(k)
                if ready:
                    nc.tensor.wait_ge(*ready(k))
                for n, (wt, v) in enumerate(((w_hi, hi), (w_hi, lo), (w_lo, hi))):
                    for h in range(2):
                        mm = nc.tensor.matmul(out[:, h, :], wt[:, r, k, :], v[:, h * HALF:(h + 1) * HALF],
                                              start=start and k == 0 and n == 0,
                                              stop=stop and k == kt - 1 and n == 2)
            if end == kt:
                mm.then_inc(unit_done, 1)

        def evac_buffer(g):
            return (silu, prod)[g % 2]

        def take_gate(u0, o0, g, step=0):
            nc.vector.wait_ge(gate_kept[g % 2], 16 * (g // 2 + 1) + 8 * step)
            wait_unit(nc.vector, u0, step)
            nc.vector.tensor_tensor(halves(evac_buffer(g)[:, :]), acc(o0), halves(rstd[:, :]), ALU.mult
                                    ).then_inc(acc_read, 1)

        def keep_gate(o0, g, step=0):
            wait_output(nc.scalar, o0, step)
            nc.scalar.dma_start(gates_kept[:, ds(step + g, 1), :], evac_buffer(g)[:, :].unsqueeze(1)
                                ).then_inc(gate_kept[g % 2], 16)

        def gates_stored(eng, count):
            for b in range(2):
                eng.wait_ge(gate_kept[b], 16 + 8 * count)

        def xg(k):
            return xg_hi[:, k, :], xg_lo[:, k, :]

        def wait_unit(dve, u0, step=0):
            dve.wait_ge(unit_done, SPLITS + u0 + 1 + step)

        def wait_output(eng, o0, step=0):
            eng.wait_ge(acc_read, 2 + o0 + 1 + step)

        def squares_of(t):
            if t < GT:
                return range(0)
            first = 4 * ((t - GT) // 2) + (t - GT) % 2
            return range(first, first + (3 if t % 2 else 1))

        sc_tail_copied = sem("sc_tail_copied")

        def wait_sctail(eng):
            eng.wait_ge(sc_tail_copied, SC_T)

        def branches_stored(eng):
            for written in state_written:
                eng.wait_ge(written, 16 * SC_T)
            eng.wait_ge(hfin_written[0], 16 * SSD_T)
            eng.wait_ge(out_written, 96)

        w_in_att = [COL_Q, COL_K, COL_V, COL_Z, COL_Z + P, COL_XBC, COL_XBC + P, COL_XBC + 2 * P]
        w_in_step = [P, P, P, 2 * P, 2 * P, 3 * P, 3 * P, 3 * P]

        block = ctx.enter_context(nc.Block())

        @block.sync
        def _(sp):
            for s in signals:
                sp.sem_inc(s.sem, s.n)
            sp.sem_inc(kv_written, 32)
            for kept in gate_kept:
                sp.sem_inc(kept, 16)
            sp.dma_start(norms[:, :, :], ins["norms"]).then_inc(norms_landed, 16)
            for k in range(DT):
                sp.dma_start(x[:, k, :], ins["x_t"][:, k, :]).then_inc(x_landed[k], 16)
                if k == 0:
                    load_unit(0, 0, w["ffn1_w_gate"][:, :, 0:P], DT)

            def ffn_loads(n, u_a, u_b):
                wg, wu, wd = w[f"ffn{n}_w_gate"], w[f"ffn{n}_w_up"], w[f"ffn{n}_w_down"]
                for j in range(n == 1, 4):
                    load_unit(u_a + j, 0, (wg, wu)[j % 2][:, :, j // 2 * P:j // 2 * P + P], DT)
                with sp.Fori(0, FT // 2 - 1) as i:
                    for j in range(4):
                        load_unit(u_a + 4 + j, 4 * i, (wg, wu)[j % 2][:, :, ds((i * 2 + j // 2 + 2) * P, P)], DT)
                with sp.Fori(0, 2) as i:
                    for j in range(12):
                        k0, kt = DOWN_K[j % 3]
                        load_unit(u_b + j, 12 * i, wd[:, k0:k0 + kt, ds((i * 4 + j // 3) * P, P)], kt)
            ffn_loads(1, U_FFN1A, U_FFN1B)
            load_unit(U_DT, 0, w["w_in"][:, :, COL_DT:COL_DT + P], DT)
            with sp.Fori(0, SB_T) as t:
                for j in range(8):
                    load_unit(U_ATT + j, 8 * t, w["w_in"][:, :, ds(t * w_in_step[j] + w_in_att[j], P)], DT)
                    if j == 5:
                        sp.wait_ge(qk_normed.sem, qk_normed.now(t, 1))
                        sp.dma_start(outs["k_t"][:, ds(t, 1), :], kh[:, :].unsqueeze(1)).then_inc(kv_written, 16)
                        sp.dma_start(outs["v_t"][:, ds(t, 1), :], vr[:, :].unsqueeze(1)).then_inc(kv_written, 16)

            def load_gate(g, step=0, first=U_GATE):
                load_unit(first + g, step, w["w_in"][:, :, ds(step * P + g * P, P)], DT)

            def load_sc(n):
                col = (COL_SCC, COL_SCX, COL_SCB)[n % 3] + n // 3 * P
                load_unit(U_SSD + n, 0, w["w_in"][:, :, col:col + P], DT)

            def load_pages(cache, i, b):
                for p in range(PAGES):
                    page = sp.value_load(table[0:1, ds(i * (SLOTS * PAGES) + b * PAGES + p, 1)], min_val=0,
                                         max_val=cache.shape[1] - 1)
                    sp.dma_start(pages[:, b, p, :], cache[0, ds(page, 1)].rearrange("o t h d -> (o t) (h d)")
                                 ).then_inc(page_landed[b], 16)

            sp.wait_ge(landed, 8 * 16)
            AHEAD = 4
            for g in range(AHEAD):
                load_gate(g)
            sp.wait_ge(q_row_ready, 1)
            sp.dma_start(q_kept, q_row[:, :]).then_inc(q_row_kept, 16)
            sp.wait_ge(yc_ready.sem, yc_ready.now(SB_T - 1))
            sp.dma_start(sprev[:, :, :, :], ins["ssd_prev"]).then_inc(conv_in, 16)
            sp.dma_start(scprev[:, :, :, :], ins["sc_prev"]).then_inc(conv_in, 16)
            sp.wait_ge(kv_written, 32 * SB_T + 32)
            sp.wait_ge(q_row_kept, 16)
            sp.dma_start(qb[:, :, :, :].rearrange("p t b f -> p (t b f)"),
                         q_kept.rearrange("r f -> (r f)").partition_broadcast(P)).then_inc(qb_landed, 16)
            with sp.Fori(0, NS // SLOTS) as i:
                for b in range(SLOTS):
                    sp.wait_ge(pages_used.sem, pages_used.before(i, b))
                    load_pages(ins["cache_sb_k"], i, b)
                    load_gate(AHEAD + b, SLOTS * i)
            for g in range(AHEAD + G_K, G0_V):
                load_gate(g)
            with sp.Fori(0, NS // SLOTS) as i:
                for b in range(SLOTS):
                    sp.wait_ge(pages_used.sem, pages_used.now(NS // SLOTS - 1, b))
                    sp.wait_ge(pvd_done.sem, pvd_done.before(i, b))
                    load_pages(ins["cache_sb_v"], i, b)
                    load_gate(G0_V + b, SLOTS * i)
            for n in range(3):
                load_sc(n)
            sp.wait_ge(pvd_done.sem, pvd_done.now(NS // SLOTS - 1, SLOTS - 1))

            def state_ap(dram, t):
                return dram[0, :, 2 * t:2 * t + 2].rearrange("b e p n -> (e p) b n")

            def load_state(t):
                k = t % 2
                if t >= 2:
                    sp.wait_ge(state_written[k], 16 * (t // 2))
                    sp.wait_ge(sample_done.sem, sample_done.now(0, t - 2))
                sp.dma_start(state[:, k, :, :], state_ap(ins["state_ssd"], t)).then_inc(state_landed[k], 16)

            def load_bc(g, k):
                rows = bc_kept[(GROUPS * k + g) * NS:(GROUPS * k + g + 1) * NS, :]
                sp.dma_start((bb, cbb)[k][:, :, :].rearrange("p b n -> p (b n)"),
                             rows.rearrange("b n -> (b n)").partition_broadcast(P)).then_inc(bc_landed[k], 16)

            def load_next(n):
                if n < 3 * SC_T:
                    load_sc(n)
                elif n < 3 * SC_T + G_POST:
                    load_gate(GATES - G_POST + n - 3 * SC_T, first=U_POST - (GATES - G_POST))
            sp.wait_ge(bc_row_kept, 16)
            load_state(0)
            sp.wait_ge(v_summed, 1)
            load_bc(0, 0)
            load_bc(0, 1)
            sp.dma_start(outs["ssd_conv_p"], xb[:, :, NP:NP + 3]).then_inc(out_written, 16)
            sp.dma_start(outs["ssd_conv_s"][:, :, 2, :], xb[:, :, 3 + NP:3 + T]).then_inc(out_written, 16)
            sp.wait_ge(conv_in, 32)
            sp.dma_start(outs["ssd_conv_s"][:, :, 0:2, :], sprev[:, :, 1:3, :]).then_inc(out_written, 16)
            sp.dma_start(outs["sc_conv_s"][:, :, 0, :], scprev[:, :, 1, :]).then_inc(out_written, 16)
            for t in range(SSD_T):
                for n in ((3,), (4, 5))[t % 2]:
                    load_next(t // 2 * 3 + n)
                if t == GT:
                    load_bc(1, 0)
                    sp.wait_ge(sample_done.sem, sample_done.now(0, t - 1))
                    load_bc(1, 1)
                if t < SSD_T - 1:
                    load_state(t + 1)
                sp.wait_ge(hin_ready.sem, hin_ready.now(0, t))
                sp.dma_start(outs["ssd_p"][:, P * t:P * t + P], hin[:, CH, :]).then_inc(hfin_written[0], 16)
                sp.wait_ge(state_ready.sem, state_ready.now(0, t))
                sp.dma_start(state_ap(outs["ssd_s"], t), state[:, t % 2, :, :]).then_inc(state_written[t % 2], 16)
            wait_sctail(sp)
            sp.dma_start(outs["sc_conv_p"], sctail[:, :, 0:2]).then_inc(out_written, 16)
            sp.dma_start(outs["sc_conv_s"][:, :, 1, :], sctail[:, :, 2:2 + NS]).then_inc(out_written, 16)
            for w_proj, u0 in (("w_proj_bc", U_MERGE), ("w_proj_a", U_MERGE_A)):
                with sp.Fori(0, DT // 4) as i:
                    for c in range(4):
                        load_unit(u0 + c, 4 * i, w[w_proj][:, :, ds(i * (4 * P) + c * P, P)], DT)
            sp.wait_ge(y_split, 4)
            sp.wait_ge(out_written, 96)
            sp.wait_ge(x_saved, 16 * DT)
            for k in range(DT):
                sp.dma_start(x[:, k, :], x_kept[:, k, :]).then_inc(x_back, 16)
            with sp.Fori(0, 2) as i:
                for j in range(4):
                    load_unit(U_OUT + j, 4 * i, w["w_out"][:, :, ds(i * (4 * P) + j * P, P)], DT)
            ffn_loads(2, U_FFN2A, U_FFN2B)
            for c in range(DT):
                wait_output(sp, O_FFN2B + c)
                sp.dma_start(outs["y_t"][:, c, :], x[:, c, :]).then_inc(out_written, 16)
            sp.wait_ge(out_written, 96 + 16 * DT)

        @block.scalar
        def _(act):
            link = Chain(act, act_step)
            act.sem_inc(unit_done, SPLITS)

            def square(n, k):
                if n:
                    act.wait_ge(xg_ready, n * DT + k + 1)
                else:
                    act.wait_ge(x_landed[k], 16)
                if n or k >= 2:
                    act.wait_ge(sumsq_ready, n * DT + k - 1)
                nc.scalar.activation((sq, prod)[k % 2][:, :], x[:, k, :], ACT.Square).then_inc(sq_ready, 1)

            def inverse_rms(n):
                act.preload_act_table_set("natural_log_exp_and_others")
                act.wait_ge(stats_ready, n + 1)
                nc.scalar.activation(halves(rstd[:, :]), ps[:, 4:6, 0:HALF], ACT.Ln, bias=eps[:, 0:1], scale=1.0 / D
                                     ).then_inc(rms_ready, 1)
                act.wait_ge(rms_ready, n + 1)
                nc.scalar.activation(rstd[:, :], rstd[:, :], ACT.Exp, scale=-0.5).then_inc(rstd_ready, 1)

            def ffn_a(n, u_a, o_a):
                def turn(a, i):
                    for j in range(4):
                        m = j // 2
                        h = 2 * i + (2 * a + m)
                        u, o = u_a + 4 * a + j, o_a + 4 * a + j
                        round_unit(u + 1, 4 * i, DT)
                        if a == 0 and j == 0:
                            inverse_rms(2 * (n - 1))
                            act.preload_act_table(ACT.Silu)
                        wait_output(act, o, 4 * i)
                        if j % 2 == 0:
                            nc.scalar.activation(silu[:, :], silu[:, :], ACT.Silu).then_inc(silu_ready, 1)
                        else:
                            nc.scalar.activation(hid_hi[:, ds(h, 1), :], prod[:, :].unsqueeze(1), ACT.Copy
                                                 ).then_inc(hid_hi_ready, 1)
                turn(0, 0)
                with act.Fori(0, FT // 2 - 1) as i:
                    turn(1, i)

            def ffn_b(n, u_b):
                for k in range(3 * DT):
                    if u_b + k + 1 < U_END:
                        round_unit(u_b + k + 1, 0, DOWN_K[(k + 1) % 3][1])
                    if k % 3 == 2 and n == 1:
                        square(1, k // 3)

            round_unit(0, 0, DT)
            act.wait_ge(consts_set, CONSTS)
            nc.scalar.activation(ones_r[:, :], ones[:, :], ACT.Copy).then_inc(sums_rounded, 1)
            nc.scalar.activation(after_r[:, :], after[:, :], ACT.Copy).then_inc(sums_rounded, 1)
            for k in range(DT):
                square(0, k)
            ffn_a(1, U_FFN1A, O_FFN1A)
            ffn_b(1, U_FFN1B)
            round_unit(U_ATT, 0, DT)
            inverse_rms(1)
            act.wait_ge(landed, 8 * 16)

            with act.Fori(0, SB_T) as t:
                link.loop(t, 2 + 2 * 2 * 2)
                up = 8 * t

                def rms_inverse(k, dst):
                    act.wait_ge(qk_summed.sem, qk_summed.now(t, k))
                    link(nc.scalar.activation(halves(dst), ps[:, 4 + 2 * k:6 + 2 * k, 0:HALF], ACT.Ln,
                                              bias=eps[:, 0:1], scale=1.0 / HD))
                    nc.scalar.activation(dst, dst, ACT.Exp, scale=-0.5).then_inc(qk_root.sem, 1)

                def softplus_log(e):
                    for n, part in enumerate(SCORE_PARTS):
                        act.wait_ge(z_biased.sem, z_biased.now(t, 2 * e + n))
                        link(nc.scalar.activation(lg[:, e, part], zb[:, e, part], ACT.Abs))
                        link(nc.scalar.activation(lg[:, e, part], lg[:, e, part], ACT.Exp, scale=-1.0))
                        nc.scalar.activation(lg[:, e, part], lg[:, e, part], ACT.Ln, bias=one[:, 0:1]
                                             ).then_inc(log_ready.sem, 1)

                def softplus_high(e):
                    for n, part in enumerate(SCORE_PARTS):
                        act.wait_ge(sp_made.sem, sp_made.now(t, 2 * e + n))
                        nc.scalar.activation(spl_hi[:, e, part], spl[:, e, part], ACT.Copy
                                             ).then_inc(sp_hi_ready.sem, 1)

                def weights(e):
                    act.wait_ge(tail_taken.sem, tail_taken.now(t, e))
                    nc.scalar.activation(zb[:, e, :], zb[:, e, :], ACT.Exp).then_inc(w_exped.sem, 1)

                round_unit(U_ATT + 1, up, DT)
                round_unit(U_ATT + 2, up, DT)
                wait_output(act, O_ATT, up)
                act.wait_ge(qk_normed.sem, qk_normed.before(t, 1))
                nc.scalar.activation(sq[:, :], qr[:, :], ACT.Square).then_inc(qk_squared.sem, 1)
                round_unit(U_ATT + 3, up, DT)
                wait_output(act, O_ATT + 1, up)
                nc.scalar.activation(prod[:, :], kr[:, :], ACT.Square).then_inc(qk_squared.sem, 1)
                rms_inverse(0, sq[:, :])
                rms_inverse(1, prod[:, :])
                round_unit(U_ATT + 4, up, DT)
                round_unit(U_ATT + 5, up, DT)
                softplus_log(0)
                softplus_high(0)
                round_unit(U_ATT + 6, up, DT)
                weights(0)
                round_unit(U_ATT + 7, up, DT)
                softplus_log(1)
                softplus_high(1)
                round_unit(U_ATT + 8, up, DT)
                weights(1)
            link.end(SB_T)

            def pass_gate(g, step=0, first=(U_GATE, O_GATE)):
                round_unit(first[0] + g + 1, step, DT)
                keep_gate(first[1] + g, g, step)
            def round_gate(g):
                round_unit(U_GATE + g, 0, DT)
            round_gate(1)
            act.wait_ge(prep_d, 1)
            link(nc.scalar.activation(row_e, dt_t[:, :], ACT.Abs))
            nc.scalar.activation(row_e, row_e, ACT.Exp, scale=-1.0).then_inc(prep_a, 1)
            nc.scalar.activation(ssd_rows[:, 1:2], ssd_rows[:, 1:2], ACT.Exp).then_inc(prep_a, 1)
            act.wait_ge(prep_d, 2)
            nc.scalar.activation(row_l, row_s, ACT.Ln).then_inc(prep_a, 1)
            act.wait_ge(prep_a, 3)
            act.wait_ge(s_used, 1)
            nc.scalar.activation(row_s, row_l, ACT.Exp, scale=-1.0).then_inc(inverse_ready, 1)
            round_gate(2)
            keep_gate(O_GATE, 0)
            act.wait_ge(prep_d, 3)
            nc.scalar.activation(dtda_t[:, 1, :], la_t[:, NP:T], ACT.Exp).then_inc(prep_a, 1)
            round_gate(3)
            keep_gate(O_GATE + 1, 1)
            act.preload_act_table(ACT.Silu)

            def silu_bc(g, part):
                for k in range(GROUPS):
                    act.wait_ge(bc_conved, GROUPS * g + k + 1)
                    nc.scalar.activation(part[:, k, :], part[:, k, :], ACT.Silu).then_inc(bc_silued, 1)
            silu_bc(0, bt)
            act.wait_ge(cdec_conved, 1)
            nc.scalar.activation(cdec[:, :, :], cdec[:, :, :], ACT.Silu).then_inc(cdec_ready, 1)
            round_gate(4)
            keep_gate(O_GATE + 2, 2)
            keep_gate(O_GATE + 3, 3)
            assert G_PRE == 4 and G_PREP == 2
            act.preload_act_table_set("natural_log_exp_and_others")
            with act.Fori(0, NS // SLOTS) as i:
                for b in range(SLOTS):
                    pass_gate(G_PRE + b, SLOTS * i)
            act.wait_ge(zd_ready, 1)
            link(nc.scalar.activation(lgd[:, :, :, :], zd[:, :, :, :], ACT.Abs))
            link(nc.scalar.activation(lgd[:, :, :, :], lgd[:, :, :, :], ACT.Exp, scale=-1.0))
            nc.scalar.activation(lgd[:, :, :, :], lgd[:, :, :, :], ACT.Ln, bias=one[:, 0:1]).then_inc(lgd_ready, 1)
            round_unit(U_GATE + G0_PREP + 1, 0, DT)
            act.wait_ge(prep_d, 5)
            nc.scalar.activation(to_end[:, :, :], to_end[:, :, :], ACT.Exp).then_inc(prep_a, 1)
            nc.scalar.activation(ch_dec[:, :, :], flat[:, 7 * 512:7 * 512 + CH * SSD_HEADS].rearrange(
                "p (c h) -> p c h", c=CH), ACT.Exp).then_inc(prep_a, 1)
            keep_gate(O_GATE + G0_PREP, G0_PREP)
            act.wait_ge(wd_raw, 1)
            nc.scalar.activation(zd[:, :, :, :], zd[:, :, :, :], ACT.Exp).then_inc(wd_ready, 1)
            pass_gate(G0_PREP + 1)
            act.preload_act_table(ACT.Silu)
            silu_bc(1, ct)

            def pick(t, e):
                h = 2 * t + e
                act.wait_ge(cs_spread.sem, cs_spread.now(0, h - 2))
                nc.scalar.activation(heads_sel[e][:, :], ones[0:SSD_HEADS, :], ACT.Copy, scale=ident[0:SSD_HEADS, h:h + 1]
                                     ).then_inc(sel_ready.sem, 1)

            def decays(t, e):
                h = 2 * t + e
                act.wait_ge(cs_spread.sem, cs_spread.now(0, h))
                for c in range(CH):
                    last = nc.scalar.activation(gbuf[:, e, P * c:P * c + P], ps[:, (6, 4)[e], P * c:P * c + P],
                                                ACT.Relu, bias=cs_tok[:, c, h:h + 1], scale=-1.0)
                last.then_inc(seg_ready.sem, 1)
                nc.scalar.activation(csc[:, e, :], ps[:, (6, 4)[e], :], ACT.Exp).then_inc(ecs_ready.sem, 1)
                act.wait_ge(seg_ready.sem, seg_ready.now(0, h))
                nc.scalar.activation(gbuf[:, e, :], gbuf[:, e, :], ACT.Exp, scale=-1.0).then_inc(decay_ready.sem, 1)

            with act.Fori(0, NS // SLOTS) as i:
                def silu_x(b):
                    act.wait_ge(conv_ready.sem, conv_ready.now(i, b))
                    nc.scalar.activation(xb[:, ds(SLOTS * i + b, 1), 0:NP], (sq, sumsq)[b % 2][:, 0:NP].unsqueeze(1),
                                         ACT.Silu).then_inc(xs_ready.sem, 1)
                for b in range(SLOTS):
                    g, t = G0_V + b, ds(SLOTS * i + b, 1)
                    round_unit(U_GATE + g + 1, SLOTS * i, DT)
                    if b:
                        silu_x(b - 1)
                        keep_gate(O_GATE + g - 1, g - 1, SLOTS * i)
                    nc.scalar.activation(zs[:, t, :], zs[:, t, :], ACT.Silu).then_inc(zs_ready, 1)
                silu_x(SLOTS - 1)
                keep_gate(O_GATE + G0_V + SLOTS - 1, G0_V + SLOTS - 1, SLOTS * i)

            def square_y(t):
                act.wait_ge(y_ready.sem, y_ready.now(0, t))
                act.wait_ge(sample_done.sem, sample_done.now(0, t))
                if t >= 2:
                    act.wait_ge(ysum_ready, t - 1)
                nc.scalar.activation(ysq[:, t % 2, :], zs[:, t, :], ACT.Square).then_inc(ysq_ready, 1)

            act.wait_ge(pvd_done.sem, pvd_done.now(NS // SLOTS - 1, SLOTS - 1))
            act.wait_ge(prep_d, 7)
            for e in range(2):
                pick(0, e)
            for t in range(SSD_T):
                u = U_SSD + 3 * (t // 2)
                decays(t, 0)
                decays(t, 1)
                if t < SSD_T - 1:
                    pick(t + 1, 0)
                    pick(t + 1, 1)
                if t % 2 == 0:
                    round_unit(u + 1, 0, DT)
                    if t == GT:
                        act.wait_ge(out_written, 64)
                    for n in squares_of(t):
                        square_y(n)
                act.wait_ge(state_landed[t % 2], 16 * (t // 2 + 1))
                for b in range(NS):
                    last = nc.scalar.activation(state[:, t % 2, b, :], state[:, t % 2, b, :], ACT.Copy,
                                                scale=dtda[:, t, 1, b:b + 1])
                last.then_inc(state_decayed.sem, 1)
                round_unit(u + 2 + t % 2, 0, DT)
                if t % 2:
                    for n in squares_of(t):
                        if n < SSD_T - 1:
                            square_y(n)

            def split_y(first, src, n, tiles):
                act.wait_ge(yprod_ready, n + 1)
                nc.scalar.activation(y_hi[:, first:first + tiles, :], src, ACT.Copy).then_inc(yhi_ready, 1)
            round_unit(U_POST + 1, 0, DT)
            act.preload_act_table(ACT.Sigmoid)
            split_y(8, yb[:, :, :], 0, 4)
            square_y(SSD_T - 1)
            round_unit(U_MERGE, 0, DT)
            keep_gate(O_POST, GATES - 2)
            split_y(12, yc[:, :, :], 1, 4)
            keep_gate(O_POST + 1, GATES - 1)
            assert G_POST == 2

            def open_gate(n):
                c = n // 2 if n < 2 * DT else n - 2 * DT
                column = (1 + n % 2) * DT + c if n < 2 * DT else c
                slot = n % GATE_SLOTS
                act.wait_ge(gate_landed[slot], 16 * (n // GATE_SLOTS + 1))
                nc.scalar.activation(gates[:, slot, :], gates[:, slot, :], ACT.Sigmoid, bias=gate_b[:, column:column + 1]
                                     ).then_inc(gate_open, 1)
            for c in range(DT):
                round_unit(U_MERGE + c + 1, 0, DT)
                open_gate(2 * c)
                open_gate(2 * c + 1)
                if c == 0:
                    act.preload_act_table_set("natural_log_exp_and_others")
                    for g in range(GROUPS):
                        act.wait_ge(ysum_spread, g + 1)
                        link(nc.scalar.activation(halves(ysum[:, g, :]), ps[:, 4 + 2 * g:6 + 2 * g, 0:HALF], ACT.Ln,
                                                  bias=eps[:, 0:1], scale=1.0 / (GT * P)))
                        nc.scalar.activation(ysum[:, g, :], ysum[:, g, :], ACT.Exp, scale=-0.5).then_inc(yroot_ready, 1)
                if c in (3, 6):
                    g = c // 3 - 1
                    split_y(GT * g, zs[:, GT * g:GT * g + GT, :], 2 + g, GT)
            for c in range(DT):
                round_unit(U_MERGE_A + c + 1, 0, DT)
                open_gate(2 * DT + c)
                act.wait_ge(merged, c + 1)
                nc.scalar.activation(m_hi[:, c, :], (prod, silu)[c % 2][:, :], ACT.Copy).then_inc(m_hi_ready, 1)
            for c in range(DT):
                round_unit(U_OUT + c + 1, 0, DT)
                square(2, c)
            ffn_a(2, U_FFN2A, O_FFN2A)
            ffn_b(2, U_FFN2B)

        @block.vector
        def _(dve):
            link = Chain(dve, dve_step)
            dve.sem_inc(unit_split, STAGES)
            dve.sem_inc(acc_read, 2)
            nc.vector.memset(eps[:, :], EPS).then_inc(consts_set, 1)
            nc.vector.memset(one[:, :], 1.0).then_inc(consts_set, 1)
            link(nc.vector.memset(blocks[:, :], 0.0))
            nc.vector.memset(blocks[0:HD, 0:HD], 1.0)
            nc.vector.memset(blocks[HD:P, HD:P], 1.0).then_inc(consts_set, 1)
            dve.wait_ge(norms_landed, 16)

            def make_xg(c, n, count):
                nc.vector.tensor_scalar(xg_hi[:, c, :], x[:, c, :], norms[:, n, c:c + 1], None, ALU.mult
                                        ).then_inc(xg_hi_ready, 1)
                dve.wait_ge(xg_hi_ready, count + 1)
                nc.vector.scalar_tensor_tensor(xg_lo[:, c, :], x[:, c, :], norms[:, n, c:c + 1],
                                               xg_hi[:, c, :].bitcast(F32), ALU.mult, ALU.subtract
                                               ).then_inc(xg_ready, 1)

            def scaled(dst, o):
                return nc.vector.tensor_tensor(dst, acc(o), halves(rstd[:, :]), ALU.mult)

            def ffn_a(n, u_a, o_a):
                def turn(a, i):
                    for j in range(4):
                        m = j // 2
                        h = 2 * i + (2 * a + m)
                        u, o = u_a + 4 * a + j, o_a + 4 * a + j
                        rest_unit(u + 1, 4 * i, DT)
                        if a == 0 and j == 0:
                            dve.wait_ge(rstd_ready, 2 * n - 1)
                        if j % 2 == 0:
                            wait_unit(dve, u, 4 * i)
                            scaled(halves(silu[:, :]), o).then_inc(acc_read, 1)
                        else:
                            dve.wait_ge(silu_ready, h + (1 + (n - 1) * FT))
                            link(nc.vector.tensor_tensor(silu[:, :], silu[:, :], rstd[:, :], ALU.mult))
                            wait_unit(dve, u, 4 * i)
                            nc.vector.tensor_tensor(halves(prod[:, :]), acc(o), halves(silu[:, :]), ALU.mult
                                                    ).then_inc(acc_read, 1)
                            dve.wait_ge(hid_hi_ready, h + (1 + (n - 1) * FT))
                            nc.vector.tensor_tensor(hid_lo[:, ds(h, 1), :], prod[:, :].unsqueeze(1),
                                                    hid_hi[:, ds(h, 1), :].bitcast(F32), ALU.subtract
                                                    ).then_inc(hid_ready, 1)
                turn(0, 0)
                with dve.Fori(0, FT // 2 - 1) as i:
                    link.loop(i, 2)
                    turn(1, i)
                link.end(FT // 2 - 1)

            def add_to_x(c, o, factor, n):
                nc.vector.scalar_tensor_tensor(halves(x[:, c, :]), acc(o), factor, halves(x[:, c, :]),
                                               ALU.mult, ALU.add).then_inc(acc_read, 1)
                if n < 3:
                    wait_output(dve, o)
                    make_xg(c, n, n * DT + c)

            def ffn_b(n, u_b, o_b):
                for k in range(3 * DT):
                    if u_b + k + 1 < U_END:
                        rest_unit(u_b + k + 1, 0, DOWN_K[(k + 1) % 3][1])
                    if k % 3 == 2:
                        wait_unit(dve, u_b + k)
                        add_to_x(k // 3, o_b + k // 3, 0.5, 1 if n == 1 else 3)

            for c in range(DT):
                dve.wait_ge(x_landed[c], 16)
                make_xg(c, 0, c)
                if c == 0:
                    rest_unit(0, 0, DT)
            ffn_a(1, U_FFN1A, O_FFN1A)
            ffn_b(1, U_FFN1B, O_FFN1B)
            rest_unit(U_ATT, 0, DT)
            dve.wait_ge(rstd_ready, 2)
            dve.wait_ge(landed, 8 * 16)
            dve.wait_ge(consts_set, CONSTS)
            link(nc.vector.tensor_scalar(qk_g[:, 0:1], qk_g[:, 0:1], HD ** -0.5, None, ALU.mult))
            wait_unit(dve, U_DT)
            dve.wait_ge(x_saved, 16 * DT)
            nc.vector.tensor_tensor(halves(dt_t[:, :]), acc(O_DT)[0:SSD_HEADS], halves(rstd[0:SSD_HEADS, :]), ALU.mult
                                    ).then_inc(acc_read, 1)
            nc.vector.memset(xb[:, :, 0:3], 0.0)
            link(nc.vector.tensor_tensor(strict[:, :], upto[:, :], ident[:, :], ALU.subtract))

            with dve.Fori(0, SB_T) as t:
                link.loop(t, 2 * 3 + 1)
                up = 8 * t

                def take(j, dst):
                    rest_unit(U_ATT + j + 1, up, DT)
                    wait_unit(dve, U_ATT + j, up)
                    scaled(dst, O_ATT + j).then_inc(acc_read, 1)

                def take_z(j):
                    take(3 + j, zs[:, ds(2 * t + j, 1), :].rearrange("p o (a b) -> p (o a) b", a=2))

                def take_x(j):
                    take(5 + j, xb[:, ds(3 * t + j, 1), 3:3 + T].rearrange("p o (a b) -> p (o a) b", a=2))

                def bias_z(e):
                    dve.wait_ge(scored.sem, scored.now(t, e))
                    for part in SCORE_PARTS:
                        nc.vector.tensor_scalar(zb[:, e, part], flat[:, 2048 + part.start:2048 + part.stop],
                                                sb_bias[:, ds(2 * t + e, 1)], None, ALU.add).then_inc(z_biased.sem, 1)

                def mask_diagonal(buf, part):
                    if part == 0:
                        tiles = buf[:, 896:1152].rearrange("p (j i) -> p j i", j=2)
                    else:
                        tiles = buf[:, 0:1024].rearrange("p (j i) -> p j i", j=2)[:, :, 0:P]
                    return nc.vector.tensor_tensor(tiles, tiles, strict[:, :].unsqueeze(1).broadcast_to([P, 2, P]),
                                                   ALU.mult)

                def softplus(e):
                    for n, part in enumerate(SCORE_PARTS):
                        dve.wait_ge(log_ready.sem, log_ready.now(t, 2 * e + n))
                        link(nc.vector.scalar_tensor_tensor(spl[:, e, part], zb[:, e, part], 0.0, lg[:, e, part],
                                                            ALU.max, ALU.add))
                        mask_diagonal(spl[:, e, :], n).then_inc(sp_made.sem, 1)
                    for n, part in enumerate(SCORE_PARTS):
                        dve.wait_ge(sp_hi_ready.sem, sp_hi_ready.now(t, 2 * e + n))
                        nc.vector.tensor_tensor(spl_lo[:, e, part], spl[:, e, part], spl_hi[:, e, part].bitcast(F32),
                                                ALU.subtract).then_inc(sp_ready.sem, 1)
                    link(nc.vector.scalar_tensor_tensor(zb[:, e, :], zb[:, e, :], 0.0, lg[:, e, :], ALU.min,
                                                        ALU.subtract))

                def take_tail(e):
                    dve.wait_ge(tail_summed.sem, tail_summed.now(t, e))
                    nc.vector.tensor_tensor(zb[:, e, :], zb[:, e, :], flat[:, 2048:2048 + SCORES], ALU.subtract
                                            ).then_inc(tail_taken.sem, 1)

                def mask_weights(e):
                    dve.wait_ge(w_exped.sem, w_exped.now(t, e))
                    mask_diagonal(zb[:, e, :], 0)
                    mask_diagonal(zb[:, e, :], 1).then_inc(w_ready.sem, 1)

                take(0, halves(qr[:, :]))
                dve.wait_ge(kv_written, 32 * t + 32)
                take(1, halves(kr[:, :]))
                take(2, halves(vr[:, :]))
                for k, (raw, hat, inv) in enumerate(((qr, qh, sq), (kr, kh, prod))):
                    dve.wait_ge(qk_root.sem, qk_root.now(t, k))
                    nc.vector.scalar_tensor_tensor(hat[:, :], raw[:, :], qk_g[:, k:k + 1], inv[:, :], ALU.mult,
                                                   ALU.mult).then_inc(qk_normed.sem, 1)
                dve.wait_ge(qk_normed.sem, qk_normed.now(t, 0))
                link(nc.vector.tensor_copy(qdec[:, ds(t, 1), :], qh[:, NP:T].unsqueeze(1)))
                take_z(0)
                bias_z(0)
                rest_unit(U_ATT + 5, up, DT)
                softplus(0)
                wait_unit(dve, U_ATT + 4, up)
                scaled(zs[:, ds(2 * t + 1, 1), :].rearrange("p o (a b) -> p (o a) b", a=2), O_ATT + 4
                       ).then_inc(acc_read, 1)
                dve.wait_ge(v_turned.sem, v_turned.now(t))
                nc.vector.tensor_copy(v_tok[:, :, :], ps[:, 7, :].rearrange("p (c d) -> p c d", c=CH)
                                      ).then_inc(v_tok_ready.sem, 1)
                take_tail(0)
                rest_unit(U_ATT + 6, up, DT)
                wait_unit(dve, U_ATT + 5, up)
                scaled(xb[:, ds(3 * t, 1), 3:3 + T].rearrange("p o (a b) -> p (o a) b", a=2), O_ATT + 5
                       ).then_inc(acc_read, 1)
                bias_z(1)
                mask_weights(0)
                rest_unit(U_ATT + 7, up, DT)
                softplus(1)
                wait_unit(dve, U_ATT + 6, up)
                scaled(xb[:, ds(3 * t + 1, 1), 3:3 + T].rearrange("p o (a b) -> p (o a) b", a=2), O_ATT + 6
                       ).then_inc(acc_read, 1)
                take_tail(1)
                rest_unit(U_ATT + 8, up, DT)
                mask_weights(1)
                wait_unit(dve, U_ATT + 7, up)
                scaled(xb[:, ds(3 * t + 2, 1), 3:3 + T].rearrange("p o (a b) -> p (o a) b", a=2), O_ATT + 7
                       ).then_inc(acc_read, 1)
                dve.wait_ge(pv_done.sem, pv_done.now(t, 1))
                nc.vector.tensor_copy(yc[:, ds(t, 1), 0:NP], ps[:, 7:8, :]).then_inc(yc_ready.sem, 1)
            link.end(SB_T)

            dve.wait_ge(q_turned, 1)
            nc.vector.tensor_copy(q_row[:, :], ps[0:SB_T * NS, 4, 0:P]).then_inc(q_row_ready, 1)
            dve.wait_ge(qk_normed.sem, qk_normed.now(SB_T - 1, 1))

            def pass_gate(g, step=0, first=(U_GATE, O_GATE)):
                rest_unit(first[0] + g + 1, step, DT)
                take_gate(first[0] + g, first[1] + g, g, step)
            def conv(dst, t):
                link(nc.vector.tensor_scalar(dst, xb[:, t, 0:NP], conv_w[:, 0, t:t + 1], conv_w[:, 4, t:t + 1],
                                             ALU.mult, ALU.add))
                for k in range(1, 4):
                    last = nc.vector.scalar_tensor_tensor(dst, xb[:, t, k:k + NP], conv_w[:, k, t:t + 1], dst,
                                                          ALU.mult, ALU.add)
                    if k < 3:
                        link(last)
                return last
            R = SSD_HEADS
            nc.vector.tensor_scalar(dt_t[:, :], dt_t[:, :], ssd_rows[:, 0:1], None, ALU.add).then_inc(prep_d, 1)
            rest_unit(U_GATE + 1, 0, DT)
            dve.wait_ge(prep_a, 1)
            nc.vector.tensor_scalar(row_s, row_e, 1.0, None, ALU.add).then_inc(prep_d, 1)
            dve.wait_ge(prep_d, 2)
            nc.vector.scalar_tensor_tensor(la_t[:, :], row_s, -1.0, row_e, ALU.add, ALU.subtract).then_inc(s_used, 1)
            take_gate(U_GATE, O_GATE, 0)
            rest_unit(U_GATE + 2, 0, DT)
            dve.wait_ge(inverse_ready, 1)
            dve.wait_ge(s_used, 1)
            link(nc.vector.tensor_tensor(la_t[:, :], la_t[:, :], row_s, ALU.mult))
            link(nc.vector.tensor_tensor(row_l, row_l, la_t[:, :], ALU.subtract))
            link(nc.vector.scalar_tensor_tensor(dt_t[:, :], dt_t[:, :], 0.0, row_l, ALU.max, ALU.add))
            nc.vector.tensor_copy(dtda_t[:, 0, :], dt_t[:, NP:T])
            nc.vector.tensor_scalar(la_t[:, :], dt_t[:, :], ssd_rows[:, 1:2], -1.0, ALU.mult, ALU.mult
                                    ).then_inc(prep_d, 1)
            take_gate(U_GATE + 1, O_GATE + 1, 1)
            rest_unit(U_GATE + 3, 0, DT)
            for k in range(GROUPS):
                conv(bt[:, k, :], SSD_T + k).then_inc(bc_conved, 1)
            take_gate(U_GATE + 2, O_GATE + 2, 2)
            rest_unit(U_GATE + 4, 0, DT)
            take_gate(U_GATE + 3, O_GATE + 3, 3)
            with dve.Fori(0, NS // SLOTS) as i:
                for b in range(SLOTS):
                    pass_gate(G_PRE + b, SLOTS * i)
                    dve.wait_ge(kq_ready.sem, kq_ready.now(i, b))
                    nc.vector.tensor_reduce(zd[:, :, ds(SLOTS * i + b, 1), :].rearrange("p g o h -> p (g o) h"),
                                            pages[:, b, :, :].rearrange("p g (h d) -> p g h d", d=HD), AX_X, ALU.add
                                            ).then_inc(pages_used.sem, 1)
            dve.wait_ge(pages_used.sem, pages_used.now(NS // SLOTS - 1, SLOTS - 1))
            nc.vector.tensor_tensor(zd[:, :, :, :].rearrange("p g b h -> p (g b) h"),
                                    zd[:, :, :, :].rearrange("p g b h -> p (g b) h"),
                                    sb_bias[:, :].unsqueeze(1).broadcast_to([P, PAGES * NS, SB_HEADS]), ALU.add
                                    ).then_inc(zd_ready, 1)
            dve.wait_ge(prep_p, 1)
            tok = "p (c h) -> p c h"
            nc.vector.tensor_copy(dt_tok[:, :, :], ps[:, 4, 0:CH * R].rearrange(tok, c=CH))
            nc.vector.tensor_copy(la_tok[:, :, :], ps[:, 5, 0:CH * R].rearrange(tok, c=CH)).then_inc(prep_d, 1)
            rest_unit(U_GATE + G0_PREP + 1, 0, DT)
            dve.wait_ge(lgd_ready, 1)
            nc.vector.scalar_tensor_tensor(spd[:, :, :, :], zd[:, :, :, :], 0.0, lgd[:, :, :, :], ALU.max, ALU.add
                                           ).then_inc(spd_ready, 1)
            link(nc.vector.scalar_tensor_tensor(zd[:, :, :, :], zd[:, :, :, :], 0.0, lgd[:, :, :, :], ALU.min,
                                                ALU.subtract))
            dve.wait_ge(prep_p, 2)
            link(nc.vector.tensor_copy(cs_tok[:, :, :], ps[:, 4, 0:CH * R].rearrange(tok, c=CH)))
            nc.vector.tensor_tensor(to_end[:, :, :], ps[:, 7, 0:CH * R].rearrange(tok, c=CH), cs_tok[:, :, :],
                                    ALU.subtract).then_inc(prep_d, 1)
            conv(ct[:, 0, :], SSD_T + GROUPS).then_inc(bc_conved, 1)
            take_gate(U_GATE + G0_PREP, O_GATE + G0_PREP, G0_PREP)
            dve.wait_ge(taild_ready, 1)
            nc.vector.tensor_tensor(zd[:, :, :, :], zd[:, :, :, :],
                                    ps[:, 6, 0:PAGES * NS * SB_HEADS].rearrange("p (g b h) -> p g b h", g=PAGES, b=NS),
                                    ALU.subtract).then_inc(wd_raw, 1)
            rest_unit(U_GATE + G0_PREP + 2, 0, DT)
            conv(ct[:, 1, :], SSD_T + GROUPS + 1).then_inc(bc_conved, 1)
            take_gate(U_GATE + G0_PREP + 1, O_GATE + G0_PREP + 1, G0_PREP + 1)
            dve.wait_ge(prep_p, 3)
            link(nc.vector.tensor_copy(cs_t[:, 0:NP], ps[0:R, 4, :]))
            link(nc.vector.tensor_copy(cs_hi[:, 0:NP], cs_t[:, 0:NP]))
            nc.vector.tensor_tensor(cs_lo[:, 0:NP], cs_t[:, 0:NP], cs_hi[:, 0:NP].bitcast(F32), ALU.subtract
                                    ).then_inc(prep_d, 1)
            nc.vector.tensor_copy(dtda[:, :, :, :], ps[:, 5, 0:SSD_T * 2 * NS].rearrange(
                "p (t k b) -> p t k b", t=SSD_T, k=2)).then_inc(prep_d, 1)

            dve.wait_ge(cdec_ready, 1)
            dve.wait_ge(prep_d, 7)
            nc.vector.tensor_tensor(xdd[:, :, :], cdec[:, 0:SSD_T, :], dtda[:, :, 0, :], ALU.mult).then_inc(xdd_ready, 1)
            dve.wait_ge(bc_turned, 1)
            nc.vector.tensor_copy(bc_row[:, :], ps[0:2 * GROUPS * NS, 6, 0:P]).then_inc(bc_row_ready, 1)
            with dve.Fori(0, NS // SLOTS) as i:
                link.loop(i, 3 * SLOTS)
                dve.wait_ge(wd_ready, 1)
                nc.vector.tensor_copy(wd4[:, :, :].rearrange("p g (b h) -> p g b h", b=SLOTS),
                                      zd[:, :, ds(SLOTS * i, SLOTS), :]).then_inc(wd4_ready.sem, 1)
                for b in range(SLOTS):
                    g = G0_V + b
                    rest_unit(U_GATE + g + 1, SLOTS * i, DT)
                    t = ds(SLOTS * i + b, 1)
                    conved = (sq, sumsq)[b % 2][:, 0:NP].unsqueeze(1)
                    if b < 2:
                        dve.wait_ge(xs_ready.sem, xs_ready.before(i, b + 2))
                    else:
                        dve.wait_ge(xs_ready.sem, xs_ready.now(i, b - 2))
                    link(nc.vector.tensor_scalar(conved, xb[:, t, 0:NP], conv_w[:, 0, t], conv_w[:, 4, t], ALU.mult,
                                                 ALU.add))
                    for k in range(1, 4):
                        tap_ = nc.vector.scalar_tensor_tensor(conved, xb[:, t, k:k + NP], conv_w[:, k, t], conved,
                                                              ALU.mult, ALU.add)
                        if k < 3:
                            link(tap_)
                    tap_.then_inc(conv_ready.sem, 1)
                    take_gate(U_GATE + g, O_GATE + g, g, SLOTS * i)
                dve.wait_ge(own_set, 1)
                dve.wait_ge(pvd_done.sem, pvd_done.now(i, SLOTS - 1))
                nc.vector.tensor_tensor(own_v[:, ds(i, 1), :], ps[:, 7:8, :],
                                        own[:, :, :].rearrange("p h d -> p (h d)").unsqueeze(1), ALU.mult
                                        ).then_inc(own_v_ready, 1)
                dve.wait_ge(own_v_ready, i + 1)
            link.end(NS // SLOTS)

            dve.wait_ge(pvd_done.sem, pvd_done.now(NS // SLOTS - 1, SLOTS - 1))
            nc.vector.memset(hin[:, 0, :], 0.0)
            nc.vector.memset(scx[:, 0:2], 0.0)
            for g in range(GROUPS):
                dve.wait_ge(b_turned, g + 1)
                nc.vector.tensor_copy(b_tok[:, g, :, :], ps[:, 4 + g, :].rearrange("p (c n) -> p c n", c=CH)
                                      ).then_inc(b_tok_ready, 1)
            for g in range(GROUPS):
                dve.wait_ge(cb_made, g + 1)
                chunks = "p (c l) -> p c l"
                nc.vector.tensor_tensor(cb[:, g, :].rearrange(chunks, c=CH), ps[:, 6 + g, :].rearrange(chunks, c=CH),
                                        upto[:, :].unsqueeze(1).broadcast_to([P, CH, P]), ALU.mult
                                        ).then_inc(cb_ready, 1)
            dve.wait_ge(v_summed, 1)
            nc.vector.tensor_copy(yc[:, :, NP:T].rearrange("p t (i b) -> p t i b", i=NS // SLOTS),
                                  ps[:, 5, 0:SB_T * NS].rearrange("p (i t b) -> p t i b", i=NS // SLOTS, t=SB_T)
                                  ).then_inc(yc_sampled, 1)
            dve.wait_ge(cb_ready, GROUPS)
            gates_stored(dve, GATES - G_POST)
            dve.wait_ge(zs_ready, SSD_T)

            rstd_2 = sumsq[:, :]
            dve.wait_ge(xs_ready.sem, xs_ready.now(NS // SLOTS - 1, SLOTS - 1))
            link(nc.vector.tensor_tensor(rstd_2, rstd[:, :], rstd[:, :], ALU.mult))

            def tile_xd(t):
                dve.wait_ge(xs_turned.sem, xs_turned.now(0, t))
                nc.vector.tensor_tensor(xd[:, t % 2, :, :].rearrange("p c (h d) -> p c h d", h=2),
                                        ps[:, 4, :].rearrange("p (c h d) -> p c h d", c=CH, h=2),
                                        dt_tok[:, :, 2 * t:2 * t + 2].unsqueeze(3).broadcast_to([P, CH, 2, HD]),
                                        ALU.mult).then_inc(xd_ready.sem, 1)

            def tile_states(t):
                dve.wait_ge(states_ready.sem, states_ready.now(0, t))
                if t:
                    dve.wait_ge(hfin_written[0], 16 * t)
                last = nc.vector.tensor_copy(hin[:, 1, :], ps[:, 5, 0:P])
                for c in range(1, CH):
                    link(last)
                    for e in range(2):
                        cols = slice(HD * e, HD * e + HD)
                        last = nc.vector.scalar_tensor_tensor(
                            hin[:, c + 1, cols], hin[:, c, cols], ch_dec[:, c, 2 * t + e:2 * t + e + 1],
                            ps[:, 5, P * c + HD * e:P * c + HD * e + HD], ALU.mult, ALU.add)
                last.then_inc(hin_ready.sem, 1)

            def head_g(t, e):
                dve.wait_ge(decay_ready.sem, decay_ready.now(0, 2 * t + e))
                nc.vector.tensor_tensor(gbuf[:, e, :], gbuf[:, e, :], cb[:, t // GT, :], ALU.mult
                                        ).then_inc(g_ready.sem, 1)

            def tile_y(t):
                x_t = x_tile(t)
                dve.wait_ge(y_summed.sem, y_summed.now(0, t))
                link(nc.vector.scalar_tensor_tensor(x_t, x_t, ssd_cols[:, 0, t:t + 1], ps[:, 7, :], ALU.mult, ALU.add))
                nc.vector.tensor_tensor(zs[:, t, 0:NP], zs[:, t, 0:NP], x_t, ALU.mult).then_inc(y_ready.sem, 1)

            def sample_y(t):
                dve.wait_ge(cs_state_ready.sem, cs_state_ready.now(0, t))
                link(nc.vector.tensor_reduce(ydec[:, :], stmp[:, :, :], AX_X, ALU.add))
                link(nc.vector.scalar_tensor_tensor(ydec[:, :], cdec[:, t, :], ssd_cols[:, 0, t:t + 1], ydec[:, :],
                                                    ALU.mult, ALU.add))
                nc.vector.tensor_tensor(zs[:, t, NP:T], zs[:, t, NP:T], ydec[:, :], ALU.mult
                                        ).then_inc(sample_done.sem, 1)

            def sc_unit(it, j):
                u, o = U_SSD + 3 * it + j, O_SSD + 3 * it + j
                wait_unit(dve, u)
                if j == 0:
                    nc.vector.tensor_tensor(halves(silu[:, :]), acc(o), halves(rstd_2), ALU.mult).then_inc(acc_read, 1)
                    wait_output(dve, o)
                elif j == 1:
                    nc.vector.tensor_tensor(halves(scx[:, 2:2 + T]), acc(o), halves(silu[:, :]), ALU.mult
                                            ).then_inc(acc_read, 1)
                    wait_output(dve, o)
                else:
                    nc.vector.tensor_tensor(halves(yb[:, it, :]), acc(o), halves(prod[:, :]), ALU.mult
                                            ).then_inc(acc_read, 1)

            def sc_conv(it):
                nc.vector.tensor_copy(sctail[:, it, :], scx[:, NP:2 + T]).then_inc(sc_tail_copied, 1)
                link(nc.vector.tensor_scalar(prod[:, 0:NP], scx[:, 0:NP], sc_w[:, 0, it:it + 1], None, ALU.mult))
                for n in range(1, 3):
                    link(nc.vector.scalar_tensor_tensor(prod[:, 0:NP], scx[:, n:n + NP], sc_w[:, n, it:it + 1],
                                                        prod[:, 0:NP], ALU.mult, ALU.add))
                link(nc.vector.tensor_scalar(prod[:, NP:T], scx[:, 2 + NP:2 + T], sc_w[:, 2, it:it + 1], None,
                                             ALU.mult))
                for n in range(2):
                    link(nc.vector.scalar_tensor_tensor(prod[:, NP:T], scprev[:, it, n, :],
                                                        sc_w[:, n, it:it + 1], prod[:, NP:T], ALU.mult, ALU.add))
                link(nc.vector.tensor_tensor(prod[:, :], prod[:, :], rstd[:, :], ALU.mult))

            for t in range(SSD_T):
                it = t // 2
                u = U_SSD + 3 * it
                tile_xd(t)
                if t:
                    tile_y(t - 1)
                if t and t % 2 == 0:
                    sc_unit(it - 1, 2)
                if t % 2:
                    rest_unit(u + 2, 0, DT)
                tile_states(t)
                head_g(t, 0)
                head_g(t, 1)
                if t % 2 == 0:
                    rest_unit(u + 1, 0, DT)
                if t and t % 2 == 0:
                    sample_y(t - 1)
                sc_unit(it, t % 2)
                if t % 2:
                    rest_unit(u + 3, 0, DT)
                    sample_y(t - 1)
                    sc_conv(it)
            sc_unit(SC_T - 1, 2)
            tile_y(SSD_T - 1)

            def low_y(first, src, n, tiles):
                dve.wait_ge(yhi_ready, n + 1)
                nc.vector.tensor_tensor(y_lo[:, first:first + tiles, :], src,
                                        y_hi[:, first:first + tiles, :].bitcast(F32), ALU.subtract).then_inc(y_split, 1)
            dve.wait_ge(state_written[0], 16 * SC_T)
            nc.vector.drain().then_inc(yprod_ready, 1)
            rest_unit(U_POST + 1, 0, DT)
            low_y(8, yb[:, :, :], 0, 4)
            sample_y(SSD_T - 1)
            take_gate(U_POST, O_POST, GATES - 2)
            branches_stored(dve)
            nc.vector.drain().then_inc(yprod_ready, 1)
            rest_unit(U_MERGE, 0, DT)
            low_y(12, yc[:, :, :], 1, 4)
            take_gate(U_POST + 1, O_POST + 1, GATES - 1)
            for c in range(DT):
                rest_unit(U_MERGE + c + 1, 0, DT)
                if c == 0:
                    gates_stored(dve, GATES)
                for n, (done, dst) in enumerate(((b_done, part[:, c, :]), (unit_done, silu[:, :]))):
                    dve.wait_ge(gate_open, 2 * c + n + 1)
                    dve.wait_ge(done, c + 1 if n == 0 else SPLITS + U_MERGE + c + 1)
                    nc.vector.tensor_tensor(halves(dst), acc(O_MERGE + n), halves(gates[:, (2 * c + n) % GATE_SLOTS, :]),
                                            ALU.mult).then_inc(acc_read, 1)
                wait_output(dve, O_MERGE + 2 * c + 1)
                link(nc.vector.tensor_tensor(part[:, c, :], part[:, c, :], silu[:, :], ALU.add))
                if c in (1, 2, 4, 5):
                    g = c // 3
                    dve.wait_ge(yroot_ready, g + 1)
                    first = GT * g + (0 if c % 3 == 1 else GT // 2)
                    for t in range(first, first + GT // 2):
                        last = nc.vector.scalar_tensor_tensor(zs[:, t, :], zs[:, t, :], ssd_cols[:, 1, t:t + 1],
                                                              ysum[:, g, :], ALU.mult, ALU.mult)
                    if c % 3 == 2:
                        last.then_inc(yprod_ready, 1)
                if c in (3, 6):
                    g = c // 3 - 1
                    low_y(GT * g, zs[:, GT * g:GT * g + GT, :], 2 + g, GT)
            for c in range(DT):
                total = (prod, silu)[c % 2]
                rest_unit(U_MERGE_A + c + 1, 0, DT)
                dve.wait_ge(gate_open, 2 * DT + c + 1)
                wait_unit(dve, U_MERGE_A + c)
                if c >= 2:
                    dve.wait_ge(m_ready, c - 1)
                nc.vector.tensor_tensor(halves(total[:, :]), acc(O_MERGE_A + c),
                                        halves(gates[:, (2 * DT + c) % GATE_SLOTS, :]), ALU.mult).then_inc(acc_read, 1)
                wait_output(dve, O_MERGE_A + c)
                nc.vector.tensor_tensor(total[:, :], total[:, :], part[:, c, :], ALU.add
                                        ).then_inc(merged, 1)
                dve.wait_ge(m_hi_ready, c + 1)
                nc.vector.tensor_tensor(m_lo[:, c, :], total[:, :], m_hi[:, c, :].bitcast(F32), ALU.subtract
                                        ).then_inc(m_ready, 1)
            dve.wait_ge(x_back, 16 * DT)
            for c in range(DT):
                rest_unit(U_OUT + c + 1, 0, DT)
                wait_unit(dve, U_OUT + c)
                add_to_x(c, O_OUT + c, 1.0, 2)
            ffn_a(2, U_FFN2A, O_FFN2A)
            ffn_b(2, U_FFN2B, O_FFN2B)

        @block.gpsimd
        def _(pool):
            link = Chain(pool, pool_step)
            link(nc.gpsimd.memset(ones[:, :], 1.0))
            link(nc.gpsimd.memset(ident[:, :], 0.0))
            nc.gpsimd.affine_select(out=ident[:, :], in_=ident[:, :], compare_op=ALU.not_equal, fill=1.0, base=0,
                                    pattern=[[-1, P]], channel_multiplier=1).then_inc(consts_set, 1)
            nc.gpsimd.affine_select(out=upto[:, :], in_=ones[:, :], compare_op=ALU.is_ge, fill=0.0, base=0,
                                    pattern=[[1, P]], channel_multiplier=-1).then_inc(consts_set, 1)
            nc.gpsimd.affine_select(out=after[:, :], in_=ones[:, :], compare_op=ALU.is_ge, fill=0.0, base=-1,
                                    pattern=[[-1, P]], channel_multiplier=1).then_inc(consts_set, 1)

            def add_squares(n):
                for k in range(DT):
                    pool.wait_ge(sq_ready, n * DT + k + 1)
                    if k == 0:
                        nc.gpsimd.tensor_copy(sumsq[:, :], sq[:, :]).then_inc(sumsq_ready, 1)
                    else:
                        pool.wait_ge(sumsq_ready, n * DT + k)
                        nc.gpsimd.tensor_tensor(sumsq[:, :], sumsq[:, :], (sq, prod)[k % 2][:, :], ALU.add
                                                ).then_inc(sumsq_ready, 1)
                    if n == 1:
                        pool.dma_start(x_kept[:, k, :], x[:, k, :]).then_inc(x_saved, 16)
            add_squares(0)
            for name, tile in (("gate_b", gate_b[:, :]), ("conv_w", conv_w[:, :, :]), ("sc_w", sc_w[:, :, :]),
                               ("qk_g", qk_g[:, :]), ("ssd_cols", ssd_cols[:, :, :]), ("ssd_rows", ssd_rows[:, :]),
                               ("table", table[:, :])):
                pool.dma_start(tile, ins[name]).then_inc(landed, 16)
            pool.dma_start(sb_bias[:, :], ins["sb_bias"].partition_broadcast(P)).then_inc(landed, 16)
            pool.wait_ge(stats_ready, 1)
            add_squares(1)

            pool.wait_ge(landed, 8 * 16)
            pool.wait_ge(yc_ready.sem, yc_ready.now(SB_T - 1))
            pool.wait_ge(conv_in, 32)

            def tap(k):
                return conv_w[:, k, :].unsqueeze(2).broadcast_to([P, XBC_T, NS])
            link(nc.gpsimd.tensor_tensor(cdec[:, :, :], sprev[:, :, 0, :], tap(0), ALU.mult))
            for src, k in ((sprev[:, :, 1, :], 1), (sprev[:, :, 2, :], 2), (xb[:, :, 3 + NP:3 + T], 3)):
                link(nc.gpsimd.tensor_tensor(ctmp[:, :, :], src, tap(k), ALU.mult))
                link(nc.gpsimd.tensor_tensor(cdec[:, :, :], cdec[:, :, :], ctmp[:, :, :], ALU.add))
            nc.gpsimd.tensor_tensor(cdec[:, :, :], cdec[:, :, :], tap(4), ALU.add).then_inc(cdec_conved, 1)
            pool.wait_ge(qb_landed, 16)
            with pool.Fori(0, NS // SLOTS) as i:
                for b in range(SLOTS):
                    pool.wait_ge(page_landed[b], 64 * i + 64)
                    tiles = pages[:, b, :, :].rearrange("p g (t f) -> p g t f", f=P)
                    query = qb[:, :, ds(SLOTS * i + b, 1), :].rearrange("p t o f -> p (o t) f")
                    nc.gpsimd.tensor_tensor(tiles, tiles, query.unsqueeze(1).broadcast_to([P, PAGES, SB_T, P]),
                                            ALU.mult).then_inc(kq_ready.sem, 1)

            pool.wait_ge(kq_ready.sem, kq_ready.now(NS // SLOTS - 1, SLOTS - 1))
            e2 = expand[:, :, :].rearrange("h t m -> h (t m)")
            link(nc.gpsimd.memset(e2, 1.0))
            link(nc.gpsimd.affine_select(out=e2, in_=e2, compare_op=ALU.is_ge, fill=0.0, base=0,
                                         pattern=[[1, SSD_T * P]], channel_multiplier=-HD))
            nc.gpsimd.affine_select(out=e2, in_=e2, compare_op=ALU.is_ge, fill=0.0, base=HD - 1,
                                    pattern=[[-1, SSD_T * P]], channel_multiplier=HD).then_inc(expand_set, 1)
            link(nc.gpsimd.memset(own[:, :, :], 0.0))
            link(nc.gpsimd.memset(token_rows[:, :], 0.0))
            for b in range(SLOTS):
                rows = slice(32 * b, 32 * b + 32)
                nc.gpsimd.affine_select(out=own[rows, :, :], in_=own[rows, :, :], compare_op=ALU.not_equal, fill=1.0,
                                        base=-SB_HEADS * b, pattern=[[-1, SB_HEADS], [0, HD]], channel_multiplier=1)
                last = nc.gpsimd.memset(token_rows[rows, b:b + 1], 1.0)
            last.then_inc(own_set, 1)

            pool.wait_ge(bc_row_ready, 1)
            pool.dma_start(bc_kept, bc_row[:, :]).then_inc(bc_row_kept, 16)
            def add_y(t):
                total = ysum[:, t // GT, :]
                pool.wait_ge(ysq_ready, t + 1)
                if t % GT == 0:
                    nc.gpsimd.tensor_copy(total, ysq[:, t % 2, :]).then_inc(ysum_ready, 1)
                else:
                    pool.wait_ge(ysum_ready, t)
                    nc.gpsimd.tensor_tensor(total, total, ysq[:, t % 2, :], ALU.add).then_inc(ysum_ready, 1)
            pool.wait_ge(pvd_done.sem, pvd_done.now(NS // SLOTS - 1, SLOTS - 1))
            pool.wait_ge(prep_a, 6)
            pool.wait_ge(bc_silued, 4)
            pool.wait_ge(prep_d, 7)
            pool.wait_ge(xdd_ready, 1)

            def add_outer(t):
                pool.wait_ge(state_decayed.sem, state_decayed.now(0, t))
                nc.gpsimd.tensor_tensor(state[:, t % 2, :, :], state[:, t % 2, :, :], outer[:, :, :], ALU.add
                                        ).then_inc(state_ready.sem, 1)

            def cs_state(t):
                pool.wait_ge(state_ready.sem, state_ready.now(0, t))
                pool.wait_ge(sample_done.sem, sample_done.now(0, t - 1))
                if t % GT == 0:
                    pool.wait_ge(bc_landed[1], 16 * (t // GT + 1))
                nc.gpsimd.tensor_tensor(stmp[:, :, :], state[:, t % 2, :, :], cbb[:, :, :], ALU.mult
                                        ).then_inc(cs_state_ready.sem, 1)
            for t in range(SSD_T):
                pool.wait_ge(xd_ready.sem, xd_ready.now(0, t))
                pool.wait_ge(states_ready.sem, states_ready.now(0, t - 1))
                nc.gpsimd.tensor_tensor(xde[:, :, :].rearrange("p c (h d) -> p c h d", h=2),
                                        xd[:, t % 2, :, :].rearrange("p c (h d) -> p c h d", h=2),
                                        to_end[:, :, 2 * t:2 * t + 2].unsqueeze(3).broadcast_to([P, CH, 2, HD]),
                                        ALU.mult).then_inc(xde_ready.sem, 1)
                for e in range(2):
                    pool.wait_ge(ecs_ready.sem, ecs_ready.now(0, 2 * t + e))
                    nc.gpsimd.tensor_tensor(csc[:, e, :], csc[:, e, :], ct[:, t // GT, :], ALU.mult
                                            ).then_inc(csc_ready.sem, 1)
                if t % 2:
                    add_outer(t - 1)
                if t:
                    cs_state(t - 1)
                if t % 2 == 0:
                    for n in squares_of(t):
                        add_y(n)
                if t % GT == 0:
                    pool.wait_ge(bc_landed[0], 16 * (t // GT + 1))
                link(nc.gpsimd.tensor_tensor(outer[:, :, :], bb[:, :, :],
                                             xdd[:, t, :].unsqueeze(2).broadcast_to([P, NS, P]), ALU.mult))
                if t % 2:
                    add_outer(t)
                if t == SSD_T - 1:
                    cs_state(t)
                if t % 2:
                    for n in squares_of(t):
                        add_y(n)

            def load_back(n):
                c = n // 2 if n < 2 * DT else n - 2 * DT
                g = (1 + n % 2) * DT + c if n < 2 * DT else c
                slot = n % GATE_SLOTS
                if n >= GATE_SLOTS:
                    wait_output(pool, O_MERGE + n - GATE_SLOTS)
                pool.dma_start(gates[:, slot, :], gates_kept[:, g, :]).then_inc(gate_landed[slot], 16)
            assert GATE_SLOTS <= SC_T
            pool.wait_ge(y_split, 1)
            gates_stored(pool, GATES - G_POST)
            for n in range(GATE_SLOTS):
                load_back(n)
            gates_stored(pool, GATES)
            for n in range(GATE_SLOTS, GATES):
                load_back(n)
            pool.wait_ge(y_split, 4)
            add_squares(2)

        @block.tensor
        def _(pe):
            def stats(n):
                pe.wait_ge(sumsq_ready, DT * (n + 1))
                for h in range(2):
                    mm = nc.tensor.matmul(ps[:, 4 + h, 0:HALF], ones[:, :], sumsq[:, h * HALF:(h + 1) * HALF],
                                          start=True, stop=True)
                mm.then_inc(stats_ready, 1)

            def ffn(n, u_a, o_a, u_b, o_b):
                for j in range(4):
                    multiply_unit(u_a + j, 0, o_a + j, 0, DT, xg,
                                  ready=(lambda k: (xg_ready, 2 * (n - 1) * DT + k + 1)) if j == 0 else None)
                    if j == 0:
                        stats(2 * (n - 1))
                with pe.Fori(0, FT // 2 - 1) as i:
                    for j in range(4):
                        multiply_unit(u_a + 4 + j, 4 * i, o_a + 4 + j, 4 * i, DT, xg)
                with pe.Fori(0, 2) as i:
                    for j in range(12):
                        k0, kt = DOWN_K[j % 3]
                        multiply_unit(u_b + j, 12 * i, o_b + j // 3, 4 * i, kt,
                                      lambda k: (hid_hi[:, k0 + k, :], hid_lo[:, k0 + k, :]), j % 3 == 0, j % 3 == 2,
                                      ready=(lambda k: (hid_ready, (n - 1) * FT + k0 + k + 1)) if j < 3 else None)

            pe.wait_ge(consts_set, CONSTS)
            pe.wait_ge(sums_rounded, 2)
            ffn(1, U_FFN1A, O_FFN1A, U_FFN1B, O_FFN1B)
            multiply_unit(U_DT, 0, O_DT, 0, DT, xg, ready=lambda k: (xg_ready, DT + k + 1))
            stats(1)

            with pe.Fori(0, SB_T) as t:
                def unit(j, begin=0, end=DT):
                    multiply_unit(U_ATT + j, 8 * t, O_ATT + j, 8 * t, DT, xg, span=(begin, end))

                def head_sums(k, src):
                    pe.wait_ge(qk_squared.sem, qk_squared.now(t, k))
                    if k == 0:
                        pe.wait_ge(tail_taken.sem, tail_taken.before(t, 1))
                    else:
                        pe.wait_ge(yc_ready.sem, yc_ready.before(t))
                    for h in range(2):
                        mm = nc.tensor.matmul(ps[:, 4 + 2 * k + h, 0:HALF], blocks[:, :],
                                              src[:, h * HALF:(h + 1) * HALF], start=True, stop=True)
                    mm.then_inc(qk_summed.sem, 1)

                def scores(e):
                    pe.wait_ge(qk_normed.sem, qk_normed.now(t, 1))
                    if e:
                        pe.wait_ge(tail_taken.sem, tail_taken.now(t, 0))
                    rows = slice(HD * e, HD * e + HD)
                    for j in range(CH):
                        mm = nc.tensor.matmul(flat[:, 2048 + SCORE_AT[j]:2048 + SCORE_AT[j] + SCORE_W[j]],
                                              kh[rows, P * j:P * j + P], qh[rows, P * j:NP], start=True, stop=True)
                    mm.then_inc(scored.sem, 1)

                def tails(e):
                    for j in reversed(range(CH)):
                        if j in (3, 1):
                            pe.wait_ge(sp_ready.sem, sp_ready.now(t, 2 * e + (j == 1)))
                        at = SCORE_AT[j]
                        for n, part in enumerate((spl_hi, spl_lo)):
                            mm = nc.tensor.matmul(flat[:, 2048 + at:2048 + at + SCORE_W[j]], after_r[:, :],
                                                  part[:, e, at:at + SCORE_W[j]], start=n == 0,
                                                  stop=j == CH - 1 and n == 1)
                        for later in range(j + 1, CH):
                            skip = P * (later - j)
                            for n, part in enumerate((spl_hi, spl_lo)):
                                mm = nc.tensor.matmul(flat[:, 2048 + at + skip:2048 + at + SCORE_W[j]], ones_r[:, :],
                                                      part[:, e, SCORE_AT[later]:SCORE_AT[later] + SCORE_W[later]],
                                                      start=False, stop=later == CH - 1 and n == 1)
                    mm.then_inc(tail_summed.sem, 1)

                def values(e):
                    pe.wait_ge(w_ready.sem, w_ready.now(t, e))
                    pe.wait_ge(v_tok_ready.sem, v_tok_ready.now(t))
                    cols = slice(HD * e, HD * e + HD)
                    for j in range(CH):
                        mm = nc.tensor.matmul(ps[cols, 7, P * j:NP], v_tok[:, j, cols],
                                              zb[:, e, SCORE_AT[j]:SCORE_AT[j] + SCORE_W[j]],
                                              start=j == 0, stop=j == CH - 1)
                    mm.then_inc(pv_done.sem, 1)

                unit(0)
                unit(1)
                head_sums(0, sq)
                unit(2)
                head_sums(1, prod)
                unit(3)
                scores(0)
                unit(4)
                wait_output(pe, O_ATT + 2, 8 * t)
                pe.wait_ge(qk_root.sem, qk_root.now(t, 1))
                for c in range(CH):
                    mm = nc.tensor.transpose(ps[:, 7, P * c:P * c + P], vr[:, P * c:P * c + P], ident[:, :])
                mm.then_inc(v_turned.sem, 1)
                unit(5, end=4)
                tails(0)
                unit(5, begin=4)
                scores(1)
                unit(6)
                values(0)
                unit(7, end=2)
                tails(1)
                unit(7, begin=2)
                values(1)

            def gate(g, step=0, first=(U_GATE, O_GATE)):
                multiply_unit(first[0] + g, step, first[1] + g, step, DT, xg)
            nc.tensor.transpose(ps[0:SB_T * NS, 4, 0:P], qdec[:, :, :].rearrange("p t b -> p (t b)"), ident[:, :]
                                ).then_inc(q_turned, 1)
            for g in range(G_PRE):
                gate(g)
            with pe.Fori(0, NS // SLOTS) as i:
                for b in range(SLOTS):
                    gate(G_PRE + b, SLOTS * i)
            R = SSD_HEADS
            pe.wait_ge(prep_d, 3)
            for c in range(CH):
                for bank, src in ((4, dt_t), (5, la_t)):
                    mm = nc.tensor.transpose(ps[:, bank, R * c:R * c + R], src[:, P * c:P * c + P], ident[0:R, 0:R])
            mm.then_inc(prep_p, 1)
            gate(G0_PREP)
            pe.wait_ge(prep_d, 4)
            lt = la_tok[:, :, :].rearrange("p c h -> p (c h)")
            nc.tensor.matmul(ps[:, 4, 0:CH * R], upto[:, :], lt, start=True, stop=True)
            nc.tensor.matmul(ps[:, 7, 0:CH * R], ones[:, :], lt, start=True, stop=True).then_inc(prep_p, 1)
            pe.wait_ge(spd_ready, 1)
            W8 = NS * SB_HEADS
            for g in range(PAGES):
                for later in range(g, PAGES):
                    mm = nc.tensor.matmul(ps[:, 6, W8 * g:W8 * g + W8], (after if later == g else ones)[:, :],
                                          spd[:, later, :, :].rearrange("p b h -> p (b h)"), start=later == g,
                                          stop=later == PAGES - 1)
            mm.then_inc(taild_ready, 1)
            gate(G0_PREP + 1)
            pe.wait_ge(cdec_ready, 1)
            pe.wait_ge(wd_raw, 1)
            nc.tensor.transpose(ps[0:2 * GROUPS * NS, 6, 0:P], cdec[:, SSD_T:XBC_T, :].rearrange("p t b -> p (t b)"),
                                ident[:, :]).then_inc(bc_turned, 1)
            pe.wait_ge(prep_d, 5)
            for c in range(CH):
                nc.tensor.transpose(ps[0:R, 4, P * c:P * c + P], cs_tok[:, c, :], ident[:, :])
            pe.wait_ge(expand_set, 1)
            pe.wait_ge(prep_a, 4)
            for t in range(SSD_T):
                mm = nc.tensor.matmul(ps[:, 5, 2 * NS * t:2 * NS * t + 2 * NS], expand[:, t, :],
                                      dtda_t[:, :, :].rearrange("p k b -> p (k b)"), start=True, stop=True)
            mm.then_inc(prep_p, 1)

            pe.wait_ge(wd_ready, 1)
            pe.wait_ge(prep_a, 6)
            with pe.Fori(0, NS // SLOTS) as i:
                for b in range(SLOTS):
                    gate(G0_V + b, SLOTS * i)
                    pe.wait_ge(page_landed[b], 64 * i + 64 * (NS // SLOTS + 1))
                    pe.wait_ge(wd4_ready.sem, wd4_ready.now(i))
                    rows = slice(4 * SB_HEADS * b, 4 * SB_HEADS * (b + 1))
                    for g in range(PAGES):
                        mm = nc.tensor.matmul(ps[rows, 7, :], wd4[:, g, :],
                                              pages[:, b, g, :], start=g == 0, stop=g == PAGES - 1)
                    mm.then_inc(pvd_done.sem, 1)
            pe.wait_ge(bc_silued, 4)
            pe.wait_ge(prep_d, 7)
            pe.wait_ge(bc_row_ready, 1)
            for g in range(GROUPS):
                for c in range(CH):
                    mm = nc.tensor.transpose(ps[:, 4 + g, P * c:P * c + P], bt[:, g, P * c:P * c + P], ident[:, :])
                mm.then_inc(b_turned, 1)
            def score_bc(g):
                for c in range(CH):
                    cols = slice(P * c, P * c + P)
                    mm = nc.tensor.matmul(ps[:, 6 + g, cols], bt[:, g, cols], ct[:, g, cols], start=True, stop=True)
                mm.then_inc(cb_made, 1)
            score_bc(0)
            pe.wait_ge(own_v_ready, NS // SLOTS)
            score_bc(1)
            pe.wait_ge(b_tok_ready, GROUPS)
            for i in range(NS // SLOTS):
                for t in range(SB_T):
                    mm = nc.tensor.matmul(ps[:, 5, SLOTS * (SB_T * i + t):SLOTS * (SB_T * i + t + 1)],
                                          own_v[:, i, P * t:P * t + P], token_rows[:, :], start=True, stop=True)
            mm.then_inc(v_summed, 1)
            pe.wait_ge(cb_ready, GROUPS)

            def spread(t, e):
                pe.wait_ge(sel_ready.sem, sel_ready.now(0, 2 * t + e))
                for n, part in enumerate((cs_hi, cs_lo)):
                    mm = nc.tensor.matmul(ps[:, (6, 4)[e], :], heads_sel[e][:, :], part[:, 0:NP], start=n == 0,
                                          stop=n == 1)
                mm.then_inc(cs_spread.sem, 1)

            def turn(t):
                pe.wait_ge(xs_ready.sem, xs_ready.now(t // SLOTS, t % SLOTS))
                if t:
                    pe.wait_ge(g_ready.sem, g_ready.now(0, 2 * t - 1))
                    pe.wait_ge(csc_ready.sem, csc_ready.now(0, 2 * t - 1))
                for c in range(CH):
                    mm = nc.tensor.transpose(ps[:, 4, P * c:P * c + P], x_tile(t)[:, P * c:P * c + P], ident[:, :])
                mm.then_inc(xs_turned.sem, 1)

            turn(0)
            spread(0, 0)
            for t in range(SSD_T):
                u, o = U_SSD + 3 * (t // 2), O_SSD + 3 * (t // 2)
                j = t % 2
                multiply_unit(u + j, 0, o + j, 0, DT, xg, span=(0, 2))
                pe.wait_ge(xd_ready.sem, xd_ready.now(0, t))
                spread(t, 1)
                pe.wait_ge(xde_ready.sem, xde_ready.now(0, t))
                pe.wait_ge(hin_ready.sem, hin_ready.now(0, t - 1))
                if t == 0:
                    pe.wait_ge(yc_sampled, 1)
                for c in range(CH):
                    mm = nc.tensor.matmul(ps[:, 5, P * c:P * c + P], b_tok[:, t // GT, c, :], xde[:, c, :], start=True,
                                          stop=True)
                mm.then_inc(states_ready.sem, 1)
                multiply_unit(u + j, 0, o + j, 0, DT, xg, span=(2, DT))
                if t % 2:
                    multiply_unit(u + 2, 0, o + 2, 0, DT, xg)
                for e in range(2):
                    pe.wait_ge(g_ready.sem, g_ready.now(0, 2 * t + e))
                    pe.wait_ge(csc_ready.sem, csc_ready.now(0, 2 * t + e))
                    if e == 0:
                        pe.wait_ge(hin_ready.sem, hin_ready.now(0, t))
                        pe.wait_ge(y_ready.sem, y_ready.now(0, t - 1))
                    rows = slice(HD * e, HD * e + HD)
                    for c in range(CH):
                        cols = slice(P * c, P * c + P)
                        nc.tensor.matmul(ps[rows, 7, cols], xd[:, t % 2, c, rows], gbuf[:, e, cols], start=True, stop=False)
                        mm = nc.tensor.matmul(ps[rows, 7, cols], hin[:, c, rows], csc[:, e, cols], start=False,
                                              stop=True)
                    if e == 0 and t < SSD_T - 1:
                        turn(t + 1)
                        spread(t + 1, 0)
                mm.then_inc(y_summed.sem, 1)

            for g in range(GATES - G_POST, GATES):
                gate(g, first=(U_POST - (GATES - G_POST), O_POST - (GATES - G_POST)))

            pe.wait_ge(ysum_ready, SSD_T)
            for g in range(GROUPS):
                for h in range(2):
                    mm = nc.tensor.matmul(ps[:, 4 + 2 * g + h, 0:HALF], ones[:, :],
                                          ysum[:, g, h * HALF:(h + 1) * HALF], start=True, stop=True)
                mm.then_inc(ysum_spread, 1)
            with pe.Fori(0, DT // 2) as i:
                for c in range(2):
                    u, o = U_MERGE + c, O_MERGE + 2 * c
                    r = u % SPLITS
                    pe.wait_ge(unit_split, STAGES + u + 1 + 2 * i)
                    for n in range(2):
                        pe.wait_ge(y_split, n + 1)
                        pe.wait_ge(acc_read, o + n + 1 + 4 * i)
                        for k in range(4):
                            for m, (wt, v) in enumerate(((w_hi, y_hi), (w_hi, y_lo), (w_lo, y_hi))):
                                for h in range(2):
                                    mm = nc.tensor.matmul(acc(o + n)[:, h, :], wt[:, r, 4 * n + k, :],
                                                          v[:, 8 + 4 * n + k, h * HALF:(h + 1) * HALF],
                                                          start=k == 0 and m == 0, stop=k == 3 and m == 2)
                        mm.then_inc((b_done, unit_done)[n], 1)
            with pe.Fori(0, DT // 2) as i:
                for c in range(2):
                    multiply_unit(U_MERGE_A + c, 2 * i, O_MERGE_A + c, 2 * i, DT,
                                  lambda k: (y_hi[:, k, :], y_lo[:, k, :]), ready=lambda k: (y_split, 3 + k // GT))
            with pe.Fori(0, 2) as i:
                for j in range(4):
                    multiply_unit(U_OUT + j, 4 * i, O_OUT + j, 4 * i, DT, lambda k: (m_hi[:, k, :], m_lo[:, k, :]),
                                  ready=(lambda k: (m_ready, k + 1)) if j == 0 else None)
            ffn(2, U_FFN2A, O_FFN2A, U_FFN2B, O_FFN2B)


def kernel(**inputs):
    import numpy as np
    import concourse.bacc as bacc
    from concourse.bass_utils import run_bass_kernel_spmd as run

    a = {k: np.asarray(v) for k, v in inputs.items()}

    def cols(v):
        return v.reshape(-1, P).T

    def flat(parts):
        return np.ascontiguousarray(np.stack(parts, 1))
    tok = np.concatenate([a["x_prompt"].reshape(-1, D), a["x_sample"].reshape(-1, D)], 0)
    laid = {
        "x_t": np.ascontiguousarray(tok.T.reshape(DT, P, T).transpose(1, 0, 2)),
        "norms": flat([cols(a["ffn1_norm"]), cols(a["mix_norm"]), cols(a["ffn2_norm"])]),
        "gate_b": np.ascontiguousarray(cols(a["gate_bias"])),
        "conv_w": flat([cols(a["ssd_conv_w"][0, k]) for k in range(4)] + [cols(a["ssd_conv_b"])]),
        "sc_w": flat([cols(a["sc_conv_w"][0, k]) for k in range(3)]),
        "qk_g": np.ascontiguousarray(np.stack([np.tile(a["sb_q_norm"][0], 2), np.tile(a["sb_k_norm"][0], 2)], 1)),
        "ssd_cols": flat([cols(np.repeat(a["ssd_d"][0], HD)), cols(a["ssd_norm"])]),
        "ssd_rows": np.ascontiguousarray(np.stack([a["ssd_dt_bias"][0], a["ssd_a_log"][0]], 1)),
        "table": a["page_table"].reshape(1, -1),
        "sb_bias": a["sb_logit_bias"].reshape(-1),
        "ssd_prev": np.ascontiguousarray(a["state_ssd_conv"][0].reshape(NS, 3, XBC_T, P).transpose(3, 2, 1, 0)),
        "sc_prev": np.ascontiguousarray(a["state_sc_conv"][0].reshape(NS, 2, SC_T, P).transpose(3, 2, 1, 0)),
    }
    laid["w_proj_bc"] = np.concatenate([a["w_proj_b"], a["w_proj_c"]], 1)
    for name in ("cache_sb_k", "cache_sb_v", "state_ssd", "ffn1_w_gate", "ffn1_w_up", "ffn1_w_down", "w_in",
                 "w_proj_a", "w_out", "ffn2_w_gate", "ffn2_w_up", "ffn2_w_down"):
        laid[name] = a[name]
    shapes = {"y_t": (P, DT, T), "k_t": (P, SB_T, T), "v_t": (P, SB_T, T), "ssd_p": (P, SSD_T * P),
              "ssd_s": (1, NS, SSD_HEADS, HD, P), "ssd_conv_p": (P, XBC_T, 3), "ssd_conv_s": (P, XBC_T, 3, NS),
              "sc_conv_p": (P, SC_T, 2), "sc_conv_s": (P, SC_T, 2, NS)}
    nc = bacc.Bacc("TRN2", target_bir_lowering=False, num_devices=1)
    ins = {k: nc.dram_tensor("in_" + k, v.shape, mybir.dt.from_np(v.dtype), kind="ExternalInput").ap()
           for k, v in laid.items()}
    outs = {k: nc.dram_tensor("out_" + k, s, F32, kind="ExternalOutput").ap() for k, s in shapes.items()}
    build(nc, ins, outs)
    r = run(nc, [{"in_" + k: v for k, v in laid.items()}], core_ids=[0]).results[0]

    def tokens(name):
        v = r["out_" + name].transpose(2, 1, 0).reshape(T, -1)
        return v[:NP], v[NP:]
    (yp, ys), (kp, ks), (vp, vs) = tokens("y_t"), tokens("k_t"), tokens("v_t")
    return (yp.reshape(1, NP, D), ys.reshape(NS, 1, D),
            kp.reshape(1, 1, NP, SB_HEADS, HD), vp.reshape(1, 1, NP, SB_HEADS, HD),
            ks.reshape(1, NS, 1, SB_HEADS, HD), vs.reshape(1, NS, 1, SB_HEADS, HD),
            r["out_ssd_p"].T.reshape(1, 1, SSD_HEADS, HD, P), r["out_ssd_s"],
            r["out_ssd_conv_p"].transpose(2, 1, 0).reshape(1, 1, 3, XBC_T * P),
            r["out_ssd_conv_s"].transpose(3, 2, 1, 0).reshape(1, NS, 3, XBC_T * P),
            r["out_sc_conv_p"].transpose(2, 1, 0).reshape(1, 1, 2, SC_T * P),
            r["out_sc_conv_s"].transpose(3, 2, 1, 0).reshape(1, NS, 2, SC_T * P))
```
